# Optimizing a Trainium2 kernel written in Bass

```python
import jax, jax.numpy as jnp
from jax import lax
import numpy as np
import functools
import math
import jax
import jax.numpy as jnp

D_MODEL = 1024
BATCH = 1
SEQ = 512
DEPTH = 2

POOL_GROUPS = 4
POOL_WINDOWS = (2, 4, 8, 16)
POOL_WIDTH = 3 * D_MODEL // 8
POOL_GROUP_DIM = POOL_WIDTH // POOL_GROUPS
CONV_WIDTH = 3 * D_MODEL // 8
HEAD_DIM = 64
DIL_CONFIGS = ((128, 1), (512, 4), (2048, 16))
HEADS_PER_GROUP = 4
ATTN_HEADS = HEADS_PER_GROUP * len(DIL_CONFIGS)
ATTN_WIDTH = ATTN_HEADS * HEAD_DIM
ATTN_OUT_WIDTH = HEADS_PER_GROUP * HEAD_DIM
ROT_DIM = HEAD_DIM // 4
ROPE_THETA = 500000.0
QUERY_BLOCK = 128
N_BRANCHES = 3
IN_SPLITS = (POOL_WIDTH, CONV_WIDTH, CONV_WIDTH, CONV_WIDTH, ATTN_WIDTH, ATTN_WIDTH, ATTN_WIDTH, N_BRANCHES * D_MODEL)
IN_WIDTH = POOL_WIDTH + 3 * CONV_WIDTH + 3 * ATTN_WIDTH + N_BRANCHES * D_MODEL
MEM_LEN = 256
MEM_HEADS = 4
MEM_HEAD_DIM = D_MODEL // 8
MEM_WIDTH = MEM_HEADS * MEM_HEAD_DIM
D_FF = ((8 * D_MODEL // 3 + 127) // 128) * 128
CONV_K = 3
RMS_EPS = 1e-6


def rmsnorm(x, g):
    xf = x.astype(jnp.float32)
    y = xf * lax.rsqrt(jnp.mean(xf * xf, axis=-1, keepdims=True) + RMS_EPS)
    return (y * g.astype(jnp.float32)).astype(x.dtype)

def split_cols(u, sizes):
    outs, start = [], 0
    for s in sizes:
        outs.append(u[..., start:start + s])
        start += s
    return outs

def causal_dwconv(u, w):
    k, c = w.shape
    return lax.conv_general_dilated(
        u, w[:, None, :].astype(u.dtype), window_strides=(1,), padding=((k - 1, 0),),
        dimension_numbers=("NWC", "WIO", "NWC"), feature_group_count=c)

def rope_tables(positions):
    inv = ROPE_THETA ** (-jnp.arange(0, ROT_DIM, 2, dtype=jnp.float32) / ROT_DIM)
    ang = positions.astype(jnp.float32)[..., None] * inv
    return jnp.cos(ang)[:, :, None, :], jnp.sin(ang)[:, :, None, :]

def apply_partial_rope(u, cos, sin):
    half = ROT_DIM // 2
    uf = u[..., :ROT_DIM].astype(jnp.float32)
    u1, u2 = uf[..., :half], uf[..., half:]
    rot = jnp.concatenate([u1 * cos - u2 * sin, u2 * cos + u1 * sin], axis=-1).astype(u.dtype)
    return jnp.concatenate([rot, u[..., ROT_DIM:]], axis=-1)

def multiscale_pool(u, pool_w, pool_scale):
    b, s, _ = u.shape
    ug = u.reshape(b, s, POOL_GROUPS, POOL_GROUP_DIM).astype(jnp.float32)
    cs = jnp.cumsum(ug, axis=1)
    t = jnp.arange(s)
    outs = []
    for g, w in enumerate(POOL_WINDOWS):
        c = cs[:, :, g]
        prev = jnp.pad(c, ((0, 0), (w, 0), (0, 0)))[:, :s]
        cnt = jnp.minimum(t + 1, w).astype(jnp.float32)[None, :, None]
        outs.append((c - prev) / cnt - ug[:, :, g])
    pooled = jnp.stack(outs, axis=2)
    mixed = jnp.einsum("bsgc,gcd->bsgd", pooled, pool_w.astype(jnp.float32))
    return (mixed.reshape(b, s, POOL_WIDTH) * pool_scale.astype(jnp.float32)).astype(u.dtype)

def dilated_attention(q, k, v):
    b, s, _, hd = q.shape
    ng = len(DIL_CONFIGS)
    def grp(u):
        return u.reshape(b, s, ng, HEADS_PER_GROUP, hd).transpose(2, 0, 3, 1, 4)
    qg, kg, vg = grp(q), grp(k), grp(v)
    scale = hd ** -0.5

    def block(bi):
        start = bi * QUERY_BLOCK
        t = start + jnp.arange(QUERY_BLOCK)
        qb = lax.dynamic_slice_in_dim(qg, start, QUERY_BLOCK, axis=3)
        outs, lses = [], []
        for g, (window, dil) in enumerate(DIL_CONFIGS):
            offs = jnp.arange(window // dil + 1) * dil
            idx = t[:, None] - offs[None, :]
            valid = idx >= 0
            idx = jnp.maximum(idx, 0)
            kk = jnp.take(kg[g], idx, axis=2)
            vv = jnp.take(vg[g], idx, axis=2)
            sc = jnp.einsum("bhqd,bhqkd->bhqk", qb[g], kk).astype(jnp.float32) * scale
            sc = jnp.where(valid, sc, -jnp.inf)
            m = jnp.max(sc, axis=-1, keepdims=True)
            p = jnp.exp(sc - m)
            den = jnp.sum(p, axis=-1, keepdims=True)
            o = jnp.einsum("bhqk,bhqkd->bhqd", p, vv.astype(jnp.float32)) / den
            outs.append(o)
            lses.append(m + jnp.log(den))
        wts = jax.nn.softmax(jnp.stack(lses, axis=0), axis=0)
        return jnp.sum(wts * jnp.stack(outs, axis=0), axis=0).astype(q.dtype)

    out = lax.map(block, jnp.arange(s // QUERY_BLOCK))
    return out.transpose(1, 0, 3, 2, 4).reshape(b, s, ATTN_OUT_WIDTH)

def memory_cross_attention(h, mem_n, w_q, w_kv, w_o):
    b, s, _ = h.shape
    q = (h @ w_q).reshape(b, s, MEM_HEADS, MEM_HEAD_DIM)
    kv = mem_n @ w_kv
    k = kv[..., :MEM_WIDTH].reshape(b, -1, MEM_HEADS, MEM_HEAD_DIM)
    v = kv[..., MEM_WIDTH:].reshape(b, -1, MEM_HEADS, MEM_HEAD_DIM)
    sc = jnp.einsum("bshd,bmhd->bhsm", q, k).astype(jnp.float32) * (MEM_HEAD_DIM ** -0.5)
    p = jax.nn.softmax(sc, axis=-1)
    o = jnp.einsum("bhsm,bmhd->bshd", p, v.astype(jnp.float32)).astype(h.dtype)
    return o.reshape(b, s, MEM_WIDTH) @ w_o

def first_inputs(seed: int = 0) -> dict:
    key = jax.random.key(seed)
    ks = jax.random.split(key, 32)
    f32 = jnp.float32

    def nrm(k, shape, fan_in):
        return jax.random.normal(k, shape, f32) * (fan_in ** -0.5)

    def gain(k, n):
        return 1.0 + 0.05 * jax.random.normal(k, (DEPTH, n), f32)

    return {
        "x": jax.random.normal(ks[0], (BATCH, SEQ, D_MODEL), f32),
        "mem": jax.random.normal(ks[1], (BATCH, MEM_LEN, D_MODEL), f32),
        "positions": jnp.broadcast_to(jnp.arange(SEQ, dtype=jnp.int32), (BATCH, SEQ)),
        "norm_mix_pre": gain(ks[2], D_MODEL),
        "norm_mix_post": gain(ks[3], D_MODEL),
        "w_in": nrm(ks[4], (DEPTH, D_MODEL, IN_WIDTH), D_MODEL),
        "pool_w": nrm(ks[5], (DEPTH, POOL_GROUPS, POOL_GROUP_DIM, POOL_GROUP_DIM), POOL_GROUP_DIM),
        "pool_scale": 1.0 + 0.1 * jax.random.normal(ks[6], (DEPTH, POOL_WIDTH), f32),
        "conv_b_w": nrm(ks[7], (DEPTH, CONV_K, CONV_WIDTH), CONV_K),
        "w_branch_a": nrm(ks[8], (DEPTH, POOL_WIDTH, D_MODEL), POOL_WIDTH),
        "w_branch_b": nrm(ks[9], (DEPTH, CONV_WIDTH, D_MODEL), CONV_WIDTH),
        "w_branch_c": nrm(ks[10], (DEPTH, ATTN_OUT_WIDTH, D_MODEL), ATTN_OUT_WIDTH),
        "w_out": nrm(ks[11], (DEPTH, D_MODEL, D_MODEL), D_MODEL),
        "norm_mem_pre": gain(ks[12], D_MODEL),
        "norm_mem_post": gain(ks[13], D_MODEL),
        "norm_memkv": gain(ks[14], D_MODEL),
        "w_mq": nrm(ks[15], (DEPTH, D_MODEL, MEM_WIDTH), D_MODEL),
        "w_mkv": nrm(ks[16], (DEPTH, D_MODEL, 2 * MEM_WIDTH), D_MODEL),
        "w_mo": nrm(ks[17], (DEPTH, MEM_WIDTH, D_MODEL), MEM_WIDTH),
        "norm_ffn_pre": gain(ks[18], D_MODEL),
        "norm_ffn_post": gain(ks[19], D_MODEL),
        "w_up": nrm(ks[20], (DEPTH, D_MODEL, 2 * D_FF), D_MODEL),
        "conv_ffn_w": nrm(ks[21], (DEPTH, CONV_K, D_FF), CONV_K),
        "w_down": nrm(ks[22], (DEPTH, D_FF, D_MODEL), D_FF),
    }

def first_block(x, mem, positions, norm_mix_pre, norm_mix_post, w_in, pool_w, pool_scale, conv_b_w,
              w_branch_a, w_branch_b, w_branch_c, w_out, norm_mem_pre, norm_mem_post, norm_memkv,
              w_mq, w_mkv, w_mo, norm_ffn_pre, norm_ffn_post, w_up, conv_ffn_w, w_down):
    b, s, d = x.shape
    cos, sin = rope_tables(positions)
    cos, sin = cos.astype(x.dtype), sin.astype(x.dtype)
    for l in range(DEPTH):
        h = rmsnorm(x, norm_mix_pre[l])
        a_in, b_x, b_b, b_c, q, k, v, gate_in = split_cols(h @ w_in[l], IN_SPLITS)
        br_a = multiscale_pool(a_in, pool_w[l], pool_scale[l]) @ w_branch_a[l]
        br_b = (b_b * causal_dwconv(b_c * b_x, conv_b_w[l])) @ w_branch_b[l]
        q = apply_partial_rope(q.reshape(b, s, ATTN_HEADS, HEAD_DIM), cos, sin)
        k = apply_partial_rope(k.reshape(b, s, ATTN_HEADS, HEAD_DIM), cos, sin)
        v = v.reshape(b, s, ATTN_HEADS, HEAD_DIM)
        br_c = dilated_attention(q, k, v) @ w_branch_c[l]
        gates = jax.nn.sigmoid(gate_in.astype(jnp.float32)).astype(x.dtype).reshape(b, s, N_BRANCHES, d)
        merged = gates[:, :, 0] * br_a + gates[:, :, 1] * br_b + gates[:, :, 2] * br_c
        x = x + rmsnorm(merged @ w_out[l], norm_mix_post[l])
        h = rmsnorm(x, norm_mem_pre[l])
        mem_n = rmsnorm(mem, norm_memkv[l])
        x = x + rmsnorm(memory_cross_attention(h, mem_n, w_mq[l], w_mkv[l], w_mo[l]), norm_mem_post[l])
        h = rmsnorm(x, norm_ffn_pre[l])
        u = h @ w_up[l]
        ua, ub = u[..., :D_FF], u[..., D_FF:]
        y = (jax.nn.silu(causal_dwconv(ua, conv_ffn_w[l])) * ub) @ w_down[l]
        x = x + rmsnorm(y, norm_ffn_post[l])
    return x


GRID_W = 64
CTX_LEN = 256
ROPE_THETA_2 = 10000.0
NORM_EPS = 1e-6
NEG_INF = -1e30
BLOCK = 128
WINDOW = 128

A_HEADS = 8
A_KV_HEADS = 2
A_HEAD_DIM = 64
B_HEADS = 4
B_QK_DIM = 64
B_V_DIM = 2 * B_QK_DIM
A_Q_W = A_HEADS * A_HEAD_DIM
A_KV_W = A_KV_HEADS * A_HEAD_DIM
B_QK_W = B_HEADS * 2 * B_QK_DIM
B_V_W = B_HEADS * B_V_DIM
AB_Q_W = A_Q_W + B_QK_W
AB_IN_W = AB_Q_W + 2 * A_KV_W + B_QK_W + B_V_W
AB_OUT_W = A_Q_W + B_V_W

C_HEADS = 16
C_Q_LORA = 384
C_KV_LORA = 256
C_NOPE = 64
C_ROPE = 32
C_V = 64
C_IN_W = C_Q_LORA + C_KV_LORA + C_ROPE
C_OUT_W = C_HEADS * C_V

FFN_HIDDEN = ((8 * D_MODEL + 3 * 256 - 1) // (3 * 256)) * 256

N_EVEN = (DEPTH + 1) // 2
N_ODD = DEPTH // 2

F32 = jnp.float32


def rmsnorm_2(x, g):
    xf = x.astype(F32)
    y = xf * lax.rsqrt(jnp.mean(xf * xf, axis=-1, keepdims=True) + NORM_EPS)
    return (y * g.astype(F32)).astype(x.dtype)

def modulate(xn, shift, scale):
    return xn * (1.0 + scale) + shift

def joint_softmax(*logits):
    m = functools.reduce(jnp.maximum, [s.max(axis=-1, keepdims=True) for s in logits])
    e = [jnp.exp(s - m) for s in logits]
    inv = 1.0 / functools.reduce(jnp.add, [t.sum(axis=-1, keepdims=True) for t in e])
    return [t * inv for t in e]

def axial_rope_tables(rows, rot_dim):
    row = jnp.repeat(jnp.arange(rows, dtype=F32), GRID_W)
    col = jnp.tile(jnp.arange(GRID_W, dtype=F32), rows)
    axis_dim = rot_dim // 2
    inv_freq = ROPE_THETA_2 ** (-jnp.arange(0, axis_dim, 2, dtype=F32) / axis_dim)
    ang = jnp.concatenate([row[:, None] * inv_freq, col[:, None] * inv_freq], axis=-1)
    return jnp.cos(ang), jnp.sin(ang)

def apply_axial_rope(x, tab):
    cos, sin = tab
    quarter = x.shape[-1] // 4
    xr, xc = jnp.split(x.astype(F32), 2, axis=-1)

    def rot(u, cs, sn):
        u1, u2 = jnp.split(u, 2, axis=-1)
        return jnp.concatenate([u1 * cs - u2 * sn, u2 * cs + u1 * sn], axis=-1)

    out = jnp.concatenate([
        rot(xr, cos[:, None, :quarter], sin[:, None, :quarter]),
        rot(xc, cos[:, None, quarter:], sin[:, None, quarter:])], axis=-1)
    return out.astype(x.dtype)

def to_blocks(t):
    b, n = t.shape[:2]
    return jnp.moveaxis(t.reshape(b, n // BLOCK, BLOCK, *t.shape[2:]), 1, 0)

def from_blocks(t):
    t = jnp.moveaxis(t, 0, 1)
    return t.reshape(t.shape[0], -1, *t.shape[3:])

def swiglu(h, w13, w2):
    gate, up = jnp.split(h @ w13, 2, axis=-1)
    return (jax.nn.silu(gate) * up) @ w2

def lambda_init(layer_idx):
    return 0.8 - 0.6 * math.exp(-0.3 * layer_idx)

def window_gqa_latent(q, k, v, k_ctx, v_ctx, sink):
    bsz, n, _, dh = q.shape
    nb = n // BLOCK
    g = A_HEADS // A_KV_HEADS
    scale = dh ** -0.5
    qb = q.reshape(bsz, nb, BLOCK, A_KV_HEADS, g, dh)

    def band(t):
        tp = jnp.pad(t, ((0, 0), (BLOCK, BLOCK), (0, 0), (0, 0)))
        tp = tp.reshape(bsz, nb + 2, BLOCK, A_KV_HEADS, dh)
        return jnp.concatenate([tp[:, :-2], tp[:, 1:-1], tp[:, 2:]], axis=2)

    kb, vb = band(k), band(v)
    s_loc = jnp.einsum('bnqhgd,bnkhd->bhgnqk', qb, kb).astype(F32) * scale
    s_ctx = jnp.einsum('bnqhgd,bchd->bhgnqc', qb, k_ctx).astype(F32) * scale
    qi = jnp.arange(BLOCK)[:, None]
    kj = jnp.arange(3 * BLOCK)[None, :]
    key_pos = (jnp.arange(nb)[:, None, None] - 1) * BLOCK + kj[None]
    valid = (jnp.abs(kj - BLOCK - qi) <= WINDOW)[None] & (key_pos >= 0) & (key_pos < n)
    s_loc = jnp.where(valid, s_loc, NEG_INF)
    s_sink = sink.astype(F32).reshape(1, A_KV_HEADS, g, 1, 1, 1)
    p_loc, p_ctx, _ = joint_softmax(s_loc, s_ctx, s_sink)
    o = (jnp.einsum('bhgnqk,bnkhd->bnqhgd', p_loc.astype(v.dtype), vb)
         + jnp.einsum('bhgnqc,bchd->bnqhgd', p_ctx.astype(v.dtype), v_ctx))
    return o.reshape(bsz, n, A_HEADS * dh)

def gqa_ctx(q, k, v, sink):
    bsz, t, _, dh = q.shape
    g = A_HEADS // A_KV_HEADS
    qg = q.reshape(bsz, t, A_KV_HEADS, g, dh)
    s = jnp.einsum('bqhgd,bkhd->bhgqk', qg, k).astype(F32) * dh ** -0.5
    p, _ = joint_softmax(s, sink.astype(F32).reshape(1, A_KV_HEADS, g, 1, 1))
    o = jnp.einsum('bhgqk,bkhd->bqhgd', p.astype(v.dtype), v)
    return o.reshape(bsz, t, A_HEADS * dh)

def diff_attend(q, kv_parts, lam):
    scale = q.shape[-1] ** -0.5
    logits = [jnp.einsum('bqhmd,bkhmd->bmhqk', q, k).astype(F32) * scale for k, _ in kv_parts]
    probs = joint_softmax(*logits)
    outs = [jnp.einsum('bhqk,bkhd->bqhd', (p[:, 0] - lam * p[:, 1]).astype(v.dtype), v)
            for p, (_, v) in zip(probs, kv_parts)]
    return functools.reduce(jnp.add, outs)

def diff_out(o, subln_g, lam_init):
    b, t = o.shape[:2]
    return (rmsnorm_2(o, subln_g) * (1.0 - lam_init)).reshape(b, t, -1)

def ab_queries(p_q):
    b, t = p_q.shape[:2]
    qa = p_q[..., :A_Q_W].reshape(b, t, A_HEADS, A_HEAD_DIM)
    qb = p_q[..., A_Q_W:].reshape(b, t, B_HEADS, 2, B_QK_DIM)
    return qa, qb

def ab_keys_values(p_kv):
    b, t = p_kv.shape[:2]
    o1 = A_KV_W
    o2 = 2 * A_KV_W
    o3 = o2 + B_QK_W
    ka = p_kv[..., :o1].reshape(b, t, A_KV_HEADS, A_HEAD_DIM)
    va = p_kv[..., o1:o2].reshape(b, t, A_KV_HEADS, A_HEAD_DIM)
    kb = p_kv[..., o2:o3].reshape(b, t, B_HEADS, 2, B_QK_DIM)
    vb = p_kv[..., o3:].reshape(b, t, B_HEADS, B_V_DIM)
    return ka, va, kb, vb

def rope_diff(t, tab):
    b, n = t.shape[:2]
    return apply_axial_rope(t.reshape(b, n, B_HEADS * 2, B_QK_DIM), tab).reshape(t.shape)

def mixer_ab(hx, hc, w_in, w_out, sink, lam_vec, subln_g, lam_init, tab, ctx_queries):
    p = hx @ w_in
    qa, qb = ab_queries(p[..., :AB_Q_W])
    ka, va, kb, vb = ab_keys_values(p[..., AB_Q_W:])
    qa, ka = apply_axial_rope(qa, tab), apply_axial_rope(ka, tab)
    qb, kb = rope_diff(qb, tab), rope_diff(kb, tab)
    if ctx_queries:
        pc = hc @ w_in
        cqa, cqb = ab_queries(pc[..., :AB_Q_W])
        cka, cva, ckb, cvb = ab_keys_values(pc[..., AB_Q_W:])
    else:
        cka, cva, ckb, cvb = ab_keys_values(hc @ w_in[:, AB_Q_W:])
    lv = lam_vec.astype(F32)
    lam = jnp.exp(jnp.sum(lv[0] * lv[1])) - jnp.exp(jnp.sum(lv[2] * lv[3])) + lam_init

    oa = window_gqa_latent(qa, ka, va, cka, cva, sink)
    ob = from_blocks(lax.map(lambda qblk: diff_attend(qblk, [(kb, vb), (ckb, cvb)], lam),
                             to_blocks(qb)))
    yx = jnp.concatenate([oa, diff_out(ob, subln_g, lam_init)], axis=-1) @ w_out
    if not ctx_queries:
        return yx, None
    oca = gqa_ctx(cqa, cka, cva, sink)
    ocb = diff_out(diff_attend(cqb, [(ckb, cvb)], lam), subln_g, lam_init)
    yc = jnp.concatenate([oca, ocb], axis=-1) @ w_out
    return yx, yc

def mla_queries(p_q, q_norm_g, wq_b):
    b, t = p_q.shape[:2]
    q = (rmsnorm_2(p_q, q_norm_g) @ wq_b).reshape(b, t, C_HEADS, C_NOPE + C_ROPE)
    return q[..., :C_NOPE], q[..., C_NOPE:]

def mla_keys_values(p_kv, kv_norm_g, wkv_b):
    b, t = p_kv.shape[:2]
    kv_lat, k_rope = p_kv[..., :C_KV_LORA], p_kv[..., C_KV_LORA:]
    kv = (rmsnorm_2(kv_lat, kv_norm_g) @ wkv_b).reshape(b, t, C_HEADS, C_NOPE + C_V)
    return kv[..., :C_NOPE], k_rope, kv[..., C_NOPE:]

def mla_attend(q_nope, q_rope, kv_parts):
    scale = (C_NOPE + C_ROPE) ** -0.5
    logits = [(jnp.einsum('bqhd,bkhd->bhqk', q_nope, kn)
               + jnp.einsum('bqhr,bkr->bhqk', q_rope, kr)).astype(F32) * scale
              for kn, kr, _ in kv_parts]
    probs = joint_softmax(*logits)
    outs = [jnp.einsum('bhqk,bkhd->bqhd', p.astype(v.dtype), v) for p, (_, _, v) in zip(probs, kv_parts)]
    return functools.reduce(jnp.add, outs)

def mixer_mla(hx, hc, w_in, q_norm_g, kv_norm_g, wq_b, wkv_b, w_out, tab, ctx_queries):
    bsz, n, _ = hx.shape
    p = hx @ w_in
    qn, qr = mla_queries(p[..., :C_Q_LORA], q_norm_g, wq_b)
    kn, kr, v = mla_keys_values(p[..., C_Q_LORA:], kv_norm_g, wkv_b)
    qr = apply_axial_rope(qr, tab)
    kr = apply_axial_rope(kr[:, :, None, :], tab)[:, :, 0, :]
    if ctx_queries:
        pc = hc @ w_in
        cqn, cqr = mla_queries(pc[..., :C_Q_LORA], q_norm_g, wq_b)
        ckn, ckr, cv = mla_keys_values(pc[..., C_Q_LORA:], kv_norm_g, wkv_b)
    else:
        ckn, ckr, cv = mla_keys_values(hc @ w_in[:, C_Q_LORA:], kv_norm_g, wkv_b)
    o = from_blocks(lax.map(lambda qs: mla_attend(qs[0], qs[1], [(kn, kr, v), (ckn, ckr, cv)]),
                            (to_blocks(qn), to_blocks(qr))))
    yx = o.reshape(bsz, n, C_OUT_W) @ w_out
    if not ctx_queries:
        return yx, None
    oc = mla_attend(cqn, cqr, [(ckn, ckr, cv)])
    yc = oc.reshape(bsz, hc.shape[1], C_OUT_W) @ w_out
    return yx, yc

def second_inputs(seed: int = 0) -> dict:
    key = jax.random.key(seed)
    ks = jax.random.split(key, 20)

    def nrm(k, shape, scale):
        return jax.random.normal(k, shape, F32) * scale

    d = D_MODEL
    return {
        'x': nrm(ks[0], (BATCH, SEQ, d), 1.0),
        'c': nrm(ks[1], (BATCH, d), 1.0),
        'ctx': nrm(ks[2], (BATCH, CTX_LEN, d), 1.0),
        'c_ctx': nrm(ks[3], (d,), 1.0),
        'ada_w': nrm(ks[4], (DEPTH, d, 6 * d), 0.5 * d ** -0.5),
        'ada_b': nrm(ks[5], (DEPTH, 6 * d), 0.01),
        'norm_g': 1.0 + nrm(ks[6], (DEPTH, 4, d), 0.05),
        'ffn_w13': nrm(ks[7], (DEPTH, d, 2 * FFN_HIDDEN), d ** -0.5),
        'ffn_w2': nrm(ks[8], (DEPTH, FFN_HIDDEN, d), FFN_HIDDEN ** -0.5),
        'ab_w_in': nrm(ks[9], (N_EVEN, d, AB_IN_W), d ** -0.5),
        'ab_w_out': nrm(ks[10], (N_EVEN, AB_OUT_W, d), AB_OUT_W ** -0.5),
        'ab_sink': nrm(ks[11], (N_EVEN, A_HEADS), 0.5),
        'diff_lambda': nrm(ks[12], (N_EVEN, 4, B_QK_DIM), 0.1),
        'diff_subln_g': 1.0 + nrm(ks[13], (N_EVEN, B_V_DIM), 0.05),
        'mla_w_in': nrm(ks[14], (N_ODD, d, C_IN_W), d ** -0.5),
        'mla_q_norm_g': 1.0 + nrm(ks[15], (N_ODD, C_Q_LORA), 0.05),
        'mla_kv_norm_g': 1.0 + nrm(ks[16], (N_ODD, C_KV_LORA), 0.05),
        'mla_wq_b': nrm(ks[17], (N_ODD, C_Q_LORA, C_HEADS * (C_NOPE + C_ROPE)), C_Q_LORA ** -0.5),
        'mla_wkv_b': nrm(ks[18], (N_ODD, C_KV_LORA, C_HEADS * (C_NOPE + C_V)), C_KV_LORA ** -0.5),
        'mla_w_out': nrm(ks[19], (N_ODD, C_OUT_W, d), C_OUT_W ** -0.5),
    }

def second_block(x, c, ctx, c_ctx, ada_w, ada_b, norm_g, ffn_w13, ffn_w2,
              ab_w_in, ab_w_out, ab_sink, diff_lambda, diff_subln_g,
              mla_w_in, mla_q_norm_g, mla_kv_norm_g, mla_wq_b, mla_wkv_b, mla_w_out):
    bsz, n, d = x.shape
    ROWS = n // GRID_W
    tab_ab = axial_rope_tables(ROWS, A_HEAD_DIM)
    tab_c = axial_rope_tables(ROWS, C_ROPE)
    sc_x = jax.nn.silu(c)
    sc_c = jax.nn.silu(c_ctx)
    for l in range(DEPTH):
        ctx_out = l < DEPTH - 1
        mx = (sc_x @ ada_w[l] + ada_b[l]).reshape(bsz, 6, 1, d)
        mc = (sc_c @ ada_w[l] + ada_b[l]).reshape(6, d)
        hx = modulate(rmsnorm_2(x, norm_g[l, 0]), mx[:, 0], mx[:, 1])
        hc = modulate(rmsnorm_2(ctx, norm_g[l, 0]), mc[0], mc[1])
        if l % 2 == 0:
            e = l // 2
            yx, yc = mixer_ab(hx, hc, ab_w_in[e], ab_w_out[e], ab_sink[e], diff_lambda[e],
                              diff_subln_g[e], lambda_init(l), tab_ab, ctx_out)
        else:
            o = l // 2
            yx, yc = mixer_mla(hx, hc, mla_w_in[o], mla_q_norm_g[o], mla_kv_norm_g[o],
                               mla_wq_b[o], mla_wkv_b[o], mla_w_out[o], tab_c, ctx_out)
        x = x + mx[:, 2] * rmsnorm_2(yx, norm_g[l, 1])
        hx = modulate(rmsnorm_2(x, norm_g[l, 2]), mx[:, 3], mx[:, 4])
        x = x + mx[:, 5] * rmsnorm_2(swiglu(hx, ffn_w13[l], ffn_w2[l]), norm_g[l, 3])
        if ctx_out:
            ctx = ctx + mc[2] * rmsnorm_2(yc, norm_g[l, 1])
            hc = modulate(rmsnorm_2(ctx, norm_g[l, 2]), mc[3], mc[4])
            ctx = ctx + mc[5] * rmsnorm_2(swiglu(hc, ffn_w13[l], ffn_w2[l]), norm_g[l, 3])
    return x


def setup_inputs(seed=0):
    out = dict(first_inputs(seed))
    for name, value in second_inputs(seed + 1).items():
        if name != "x":
            out[name + "_2"] = value
    return out


def reference(
    x, mem, positions, norm_mix_pre, norm_mix_post, w_in, pool_w, pool_scale, conv_b_w,
    w_branch_a, w_branch_b, w_branch_c, w_out, norm_mem_pre, norm_mem_post, norm_memkv, w_mq,
    w_mkv, w_mo, norm_ffn_pre, norm_ffn_post, w_up, conv_ffn_w, w_down, c_2, ctx_2, c_ctx_2,
    ada_w_2, ada_b_2, norm_g_2, ffn_w13_2, ffn_w2_2, ab_w_in_2, ab_w_out_2, ab_sink_2,
    diff_lambda_2, diff_subln_g_2, mla_w_in_2, mla_q_norm_g_2, mla_kv_norm_g_2, mla_wq_b_2,
    mla_wkv_b_2, mla_w_out_2,
):
    x = first_block(
        x, mem, positions, norm_mix_pre, norm_mix_post, w_in, pool_w, pool_scale, conv_b_w,
        w_branch_a, w_branch_b, w_branch_c, w_out, norm_mem_pre, norm_mem_post, norm_memkv,
        w_mq, w_mkv, w_mo, norm_ffn_pre, norm_ffn_post, w_up, conv_ffn_w, w_down,
    )
    return second_block(
        x, c_2, ctx_2, c_ctx_2, ada_w_2, ada_b_2, norm_g_2, ffn_w13_2, ffn_w2_2, ab_w_in_2,
        ab_w_out_2, ab_sink_2, diff_lambda_2, diff_subln_g_2, mla_w_in_2, mla_q_norm_g_2,
        mla_kv_norm_g_2, mla_wq_b_2, mla_wkv_b_2, mla_w_out_2,
    )


_drawn_inputs = setup_inputs


def setup_inputs(seed=0):
    import zlib

    import numpy as np

    out = dict(_drawn_inputs(seed))
    spreads = {}
    factors = {'ada_b_2': 5.683,
     'norm_g_2': 3.206,
     'ab_sink_2': 64.0,
     'diff_lambda_2': 8.0,
     'diff_subln_g_2': 8.0,
     'mla_q_norm_g_2': 8.0,
     'mla_kv_norm_g_2': 7.593}
    for name, (base, spread) in spreads.items():
        noise = np.random.default_rng([zlib.crc32(name.encode()), seed]).standard_normal(out[name].shape)
        drawn = base * np.exp(spread * noise) if base else spread * noise
        out[name] = jnp.asarray(drawn.astype(out[name].dtype))
    for name, factor in factors.items():
        out[name] = (out[name] * factor).astype(out[name].dtype)
    return out
```

```python
from contextlib import ExitStack

import numpy as np

import concourse.bass as bass
from concourse import mybir

ALU = mybir.AluOpType
ACT = mybir.ActivationFunctionType
F32 = mybir.dt.float32
F32R = mybir.dt.float32r
BF16 = mybir.dt.bfloat16
I32 = mybir.dt.int32
AX_X = mybir.AxisListType.X

P = 128
D = 1024
KT = D // P
SEQ = 512
CTX = 256
TC = SEQ + CTX
DEPTH = 2
FF = 2816
FT = FF // P
FF_PARTS = ((0, 8), (8, 8), (16, 6))
POOL_W = (2, 4, 8, 16)
PG = 96
CW = 384
CT = CW // P
HD = 64
AW = 768
Q1 = 4 * CW
K1 = Q1 + AW
V1 = K1 + AW
G1 = V1 + AW
RES = 4
MW = 512
EPS = 1e-6
PAD = 16
C_HEADS, C_QL, C_KVL, C_ROPE = 16, 384, 256, 32
LAM_INIT = 0.8 - 0.6
MASKED = -1e30
TWO_PI = 6.283185307179586
NORMS = ("norm_mix_pre", "norm_mix_post", "norm_mem_pre", "norm_mem_post", "norm_memkv", "norm_ffn_pre",
         "norm_ffn_post")
PAR_ROWS = (112, 103, 96, 66, 66, 8)
N_LOADS = 25
CW1 = 6.28125
CW2 = 0.0019350051879882812
CW3 = TWO_PI - CW1 - CW2
ROUND = 12582912.0


class Counts:

    def __init__(self):
        self.here, self.outer = {}, {}

    def start(self, sem, value, view=""):
        self.here[(sem.name, view)] = value

    def next(self, sem, k=1, view=""):
        key = (sem.name, view)
        self.here[key] = self.here.get(key, 0) + k
        return self.outer.get(key, 0) + self.here[key]

    def turn(self, what):
        n = self.here.get(what, 0)
        self.here[what] = n + 1
        return n % 2


class Silent:

    def __getattr__(self, _):
        return lambda *a, **k: self


def turns(e, c, n, body):
    start = dict(c.here)
    body(Silent(), 0)
    per = {k: v - start.get(k, 0) for k, v in c.here.items()}
    if not isinstance(e, Silent):
        outer = dict(c.outer)
        c.here = dict(start)
        with e.Fori(0, n) as i:
            for k, v in per.items():
                if v and isinstance(k, tuple):
                    c.outer[k] = c.outer.get(k, 0) + i * v
            body(e, i)
        c.outer = outer
    assert all(v % 2 == 0 for k, v in per.items() if isinstance(k, str))
    c.here = {k: start.get(k, 0) + n * v for k, v in per.items()}


def two_blocks(nc, A, out):
    with ExitStack() as ctx:
        low = 16512
        high = 229368

        class Region:
            def __init__(self, at, end):
                self.at, self.end = at, end

            def __call__(self, name, shape, dt=F32):
                n = int(np.prod(shape[1:])) * (2 if dt == BF16 else 4)
                t = nc.alloc_sbuf_tensor_at(name, shape, dt, offset=self.at)
                self.at += -(-n // 32) * 32
                assert self.at <= self.end, (name, self.at, self.end)
                return t

        keep = Region(low, high)
        xres = keep("xres", [P, KT, TC])
        wraw = keep("wraw", [P, 2, 9, P])
        whi = keep("whi", [P, 2, 9, P], F32R)
        wlo = keep("wlo", [P, 2, 9, P], F32R)
        par = keep("par", [P, 6, P])
        cur = keep("cur", [P, 136])
        cur2 = keep("cur2", [P, 2, 6, KT])
        rope_c = keep("rope_c", [P, SEQ])
        rope_s = keep("rope_s", [P, SEQ])
        perm = keep("perm", [P, P])
        ones = keep("ones", [P, P])
        ident = keep("ident", [P, P])
        edge = keep("edge", [P, 4, PAD])
        small = keep("small", [P, 64])
        scT = keep("scT", [P, KT, 2])
        mods = keep("mods", [P, DEPTH, 6 * KT, 2])
        rstd = keep("rstd", [P, TC])
        t2 = keep("t2", [P, 2, TC])
        sq = keep("sq", [P, 2, TC])
        ysum = keep("ysum", [P, TC])
        hh = keep("hh", [P, KT, TC], F32R)
        hl = keep("hl", [P, KT, TC], F32R)
        zone = keep.at

        z = Region(zone, high)
        xin = z("xin", [P, 4, D])
        min_ = z("min", [P, 2, D])
        prow = z("prow", [P, 6, P])
        angi = z("angi", [P, SEQ], I32)
        ang = z("ang", [P, SEQ])
        turn_n = z("turn_n", [P, SEQ])
        red = z("red", [P, SEQ])
        inv1 = z("inv1", [P, 1])
        z = Region(zone, high)
        bih = z("bih", [P, 9, SEQ], F32R)
        bil = z("bil", [P, 9, SEQ], F32R)
        mask1 = z("mask1", [P, RES, TC], BF16)
        qkv_at = z.at
        qh = z("qh", [P, 3, SEQ], F32R)
        ql = z("ql", [P, 3, SEQ], F32R)
        kh = z("kh", [P, 3, SEQ], F32R)
        kl = z("kl", [P, 3, SEQ], F32R)
        vt = z("vt", [P, 3, RES, P])
        ot1 = z("ot1", [P, RES, 256])
        z = Region(qkv_at, high)
        mgh = z("mgh", [P, KT, SEQ], F32R)
        mgl = z("mgl", [P, KT, SEQ], F32R)
        z = Region(qkv_at, high)
        ub = z("ub", [P, 2, PAD + SEQ])
        sa = z("sa", [P, 2, PAD + SEQ])
        poh = z("poh", [P, 4, SEQ], F32R)
        pol = z("pol", [P, 4, SEQ], F32R)
        zc = z("zc", [P, 2, PAD + SEQ])
        bxs = z("bxs", [P, 2, SEQ])
        z = Region(zone, high)
        y1 = z("y1", [P, KT, SEQ])
        qmh = z("qmh", [P, 4, SEQ], F32R)
        qml = z("qml", [P, 4, SEQ], F32R)
        kmh = z("kmh", [P, 4, CTX], F32R)
        kml = z("kml", [P, 4, CTX], F32R)
        vm = z("vm", [P, 4, 2, P])
        otm = z("otm", [P, 4, MW])
        ofh = z("ofh", [P, 4, SEQ], F32R)
        ofl = z("ofl", [P, 4, SEQ], F32R)
        z = Region(zone, high)
        y2 = z("y2", [P, KT, TC])
        acth = z("acth", [P, 8, TC], F32R)
        actl = z("actl", [P, 8, TC], F32R)
        z = Region(zone + 4 * KT * SEQ, high)
        act1h = z("act1h", [P, 8, SEQ], F32R)
        act1l = z("act1l", [P, 8, SEQ], F32R)
        zf = z("zf", [P, 2, PAD + SEQ])
        z = Region(zone, high)
        adaw = z("adaw", [P, 2, 4, 512])
        adar = z("adar", [2, 6 * D])
        cin = z("cin", [P, CTX // P, D])
        z = Region(zone, high)
        kgh = z("kgh", [P, TC], F32R)
        kgl = z("kgl", [P, TC], F32R)
        vg = z("vg", [P, 6, P])
        qgh = z("qgh", [P, TC], F32R)
        qgl = z("qgl", [P, TC], F32R)
        qdh = z("qdh", [P, TC], F32R)
        qdl = z("qdl", [P, TC], F32R)
        kdh = z("kdh", [P, TC], F32R)
        kdl = z("kdl", [P, TC], F32R)
        vd = z("vd", [P, 6, P])
        mask2 = z("mask2", [P, 4, TC], BF16)
        ot2 = z("ot2", [P, 6, D])
        sink = z("sink", [P, 8])
        subg = z("subg", [P, P])
        lamv = z("lamv", [P, 4, HD])
        o1 = z("o1", [P, 2, P])
        z = Region(zone, high)
        lat = z("lat", [P, 5, TC])
        lath = z("lath", [P, 5, TC], F32R)
        latl = z("latl", [P, 5, TC], F32R)
        qch = z("qch", [P, 2, SEQ], F32R)
        qcl = z("qcl", [P, 2, SEQ], F32R)
        kch = z("kch", [P, 2, TC], F32R)
        kcl = z("kcl", [P, 2, TC], F32R)
        vc = z("vc", [P, 2, 6, HD])
        z = Region(zone - 2 * 4 * KT * TC, zone)
        ot3 = z("ot3", [P, 4, D])
        z = Region(zone, high)
        o3h = z("o3h", [P, KT, SEQ], F32R)
        o3l = z("o3l", [P, KT, SEQ], F32R)
        z = Region(zone - 2 * 4 * KT * TC, zone)
        y3 = z("y3", [P, KT, SEQ])
        z = Region(zone, high)
        outb = z("outb", [P, 4, D])

        acc = [ctx.enter_context(nc.psum_tensor(f"acc{i}", [P, 2, 512], F32)) for i in range(2)]
        pt = ctx.enter_context(nc.psum_tensor("pt", [P, 2, 512], F32))
        ob = [ctx.enter_context(nc.psum_tensor(f"ob{i}", [P, 512], F32)) for i in range(2)]

        GATE = [sq[:, 0, 0:SEQ], sq[:, 1, 0:SEQ], ysum[:, 0:SEQ]]
        PROD = [t2[:, 0, 0:SEQ], t2[:, 1, 0:SEQ], rstd[:, 0:SEQ]]

        def gain(n):
            return lambda k: cur[:, n + k:n + k + 1]

        def G2(s, i):
            return lambda k: cur2[:, s, i, k:k + 1]

        def segs_a():
            return [(0, SEQ, gain(0), None), (SEQ, TC, gain(32), None)]

        def segs_m():
            return [(0, SEQ, gain(16), None)]

        def segs_f():
            return [(0, SEQ, gain(40), None)]

        def segs_2(base):
            return [(0, SEQ, G2(0, base), G2(0, base + 1)), (SEQ, TC, G2(1, base), G2(1, base + 1))]

        def segs_lat(T):
            return [(0, T, lambda k: par[:, 1, 98 + k:99 + k], None)]

        def sem(name):
            return ctx.enter_context(nc.semaphore(name))

        loaded = sem("loaded")
        mask_in = sem("mask_in")
        ctx_in = sem("ctx_in")
        zone_free = sem("zone_free")
        stored = sem("stored")
        landed = [sem(f"slab_landed{i}") for i in range(2)]
        hi_ready = sem("slab_hi_ready")
        lo_ready = sem("slab_lo_ready")
        slab_done = sem("slab_done")
        acc_free = [sem(f"acc_free{i}") for i in range(2)]
        pt_free = sem("pt_free")
        act_step, dve_step = sem("act_step"), sem("dve_step")
        set_done = sem("setup_done")
        lt_done = sem("load_transposed")
        lt_out = sem("load_copied")
        x_ready = sem("x_ready")
        sq_ready = sem("sq_ready")
        sq_used = sem("sq_used")
        rstd_ready = sem("rstd_ready")
        t_ready = sem("t_ready")
        h_hi = sem("h_hi")
        h_ready = sem("h_ready")
        ysum_ready = sem("ysum_ready")
        ystat_done = sem("ystat_done")
        raw_ready = sem("raw_ready")
        post_done = sem("post_done")
        sum_ready = sem("sum_ready")
        tile_hi = sem("tile_hi")
        tile_ready = sem("tile_ready")
        pool_hi = sem("pool_hi")
        pool_ready = sem("pool_ready")
        bi_hi = sem("bi_hi")
        bi_ready = sem("bi_ready")
        gate_ready = sem("gate_ready")
        merged_ready = sem("merged_ready")
        conv_ready = sem("conv_ready")
        silu_ready = sem("silu_ready")
        act_ready = sem("act_ready")
        scores_done = sem("scores_done")
        nb_ready = sem("nb_ready")
        sink_ready = sem("sink_ready")
        probs_ready = sem("probs_ready")
        tr_done = sem("tr_done")
        pta_ready, ptb_ready = sem("pta_ready"), sem("ptb_ready")
        pv_done = sem("pv_done")
        ob_free = [sem(f"ob_free{i}") for i in range(2)]
        feat_done, feat_hi, feat_ready = sem("feat_done"), sem("feat_hi"), sem("feat_ready")
        ada_in = [sem(f"ada_in{i}") for i in range(2)]
        ada_used = sem("ada_used")
        ada_done, ada_out = sem("ada_done"), sem("ada_out")
        ss_ready, subn_ready = sem("ss_ready"), sem("subn_ready")
        tables_ready, cond_ready = sem("tables_ready"), sem("cond_ready")
        lam_in, lam_out, kr_ready = sem("lam_in"), sem("lam_out"), sem("kr_ready")
        in_ready, up_ready = sem("in_ready"), sem("up_ready")
        gates_used = sem("gates_used")

        pe_past, dve_past = sem("pe_past"), sem("dve_past")

        def past(e, s):
            e.sem_inc(s, 1)

        def nb(T):
            return (1, T) if T <= 512 else (2, T // 2)

        def v3(ap, T):
            return ap.rearrange("p (b n) -> p b n", b=nb(T)[0])

        def p3(ps, T, M=P):
            b, n = nb(T)
            return ps[0:M, 0:b, 0:n]

        def load(e, c, parts, width=P):
            s = c.turn("slab")
            e.wait_ge(lo_ready, c.next(lo_ready))
            for k0, rows, src in parts:
                n = src.shape[1]
                e.dma_start(wraw[0:rows, s, k0:k0 + n, 0:width], src).then_inc(landed[s], 16)

        def rows_of(W, l, k0, n, col, width=P, rows=P):
            w = W[bass.ds(l, 1), k0:k0 + n * rows, bass.ds(col, width)]
            return w.rearrange("o (k p) m -> p (o k) m", p=rows)

        def head(e, c, kt, dmas=1):
            s = c.turn("slab")
            e.wait_ge(landed[s], c.next(landed[s], 16 * dmas))
            e.wait_ge(slab_done, c.next(slab_done, view="slot"))
            e.activation(whi[:, s, 0:kt, :], wraw[:, s, 0:kt, :], ACT.Copy).then_inc(hi_ready, 1)

        def tail(e, c, kt):
            s = c.turn("slab")
            e.wait_ge(hi_ready, c.next(hi_ready))
            e.tensor_tensor(wlo[:, s, 0:kt, :], wraw[:, s, 0:kt, :],
                            whi[:, s, 0:kt, :].bitcast(F32), ALU.subtract).then_inc(lo_ready, 1)

        def passed(c):
            c.turn("acc")
            c.next(slab_done)

        def mm3(e, o, wh, wl, xh, xl, first, last):
            e.matmul(o, wh, xh, start=first, stop=False)
            e.matmul(o, wh, xl, start=False, stop=False)
            return e.matmul(o, wl, xh, start=False, stop=last)

        def slab(e, c, T, xh, xl, kts, M=P, fresh=0, free=True, c0=0, w0=0):
            s = c.turn("slab")
            e.wait_ge(lo_ready, c.next(lo_ready))
            if free:
                e.wait_ge(acc_free[s], c.next(acc_free[s]))
            b, n = nb(T)
            for j, (k, xk, rows) in enumerate(kts):
                if fresh:
                    e.wait_ge(h_ready, c.next(h_ready, fresh))
                for i in range(b):
                    cols = slice(c0 + i * n, c0 + i * n + n)
                    mm = mm3(e, acc[s][0:M, i, 0:n], whi[0:rows, s, k, w0:w0 + M], wlo[0:rows, s, k, w0:w0 + M],
                             xh[0:rows, xk, cols], xl[0:rows, xk, cols], j == 0, j == len(kts) - 1)
            mm.then_inc(slab_done, 1)
            return s

        K8 = [(k, k, P) for k in range(KT)]

        def take(e, c, sems):
            for s in sems:
                e.wait_ge(s, c.next(s))

        def give(e, sems):
            for s in sems:
                e.sem_inc(s, 1)

        def pe_stats(e, c, T):
            b, n = nb(T)
            e.wait_ge(pt_free, c.next(pt_free))
            for k in range(KT):
                e.wait_ge(sq_ready, c.next(sq_ready))
                for i in range(b):
                    mm = e.matmul(pt[:, i, 0:n], ones[:, :], sq[:, k % 2, i * n:i * n + n],
                                  start=k == 0, stop=k == KT - 1)
                mm.then_inc(sq_used, 1)

        def act_rstd(e, c, T, scale=1.0):
            e.activation(v3(rstd[:, 0:T], T), p3(pt, T), ACT.Ln, bias=small[:, 63:64], scale=scale)\
             .then_inc(act_step, 1)
            e.wait_ge(act_step, c.next(act_step))
            e.sem_inc(pt_free, 1)
            e.activation(rstd[:, 0:T], rstd[:, 0:T], ACT.Exp, scale=-0.5).then_inc(rstd_ready, 1)

        def act_prenorm(e, c, T, segs):
            for k in range(KT):
                e.wait_ge(x_ready, c.next(x_ready))
                e.wait_ge(sq_used, c.next(sq_used))
                e.activation(sq[:, k % 2, 0:T], xres[:, k, 0:T], ACT.Square).then_inc(sq_ready, 1)
            e.wait_ge(sq_used, c.next(sq_used, KT, view="all"))
            act_rstd(e, c, T)
            act_apply(e, c, hh, range(KT), segs)

        def act_apply(e, c, hi, tiles, segs):
            for k in tiles:
                for a, b, _, B in segs:
                    e.wait_ge(t_ready, c.next(t_ready))
                    if B is None:
                        e.activation(hi[:, k, a:b], t2[:, k % 2, a:b], ACT.Copy).then_inc(h_hi, 1)
                    else:
                        e.activation(hi[:, k, a:b], t2[:, k % 2, a:b], ACT.Identity, bias=B(k)).then_inc(h_hi, 1)

        def dve_apply(e, c, src, hi, lo, tiles, segs):
            e.wait_ge(rstd_ready, c.next(rstd_ready))
            tiles = list(tiles)

            def scaled(k):
                for a, b, Acol, _ in segs:
                    e.scalar_tensor_tensor(out=t2[:, k % 2, a:b], in0=src[:, k, a:b], scalar=Acol(k),
                                           in1=rstd[:, a:b], op0=ALU.mult, op1=ALU.mult).then_inc(t_ready, 1)

            scaled(tiles[0])
            for k in tiles:
                if k + 1 in tiles:
                    if k > tiles[0]:
                        e.wait_ge(h_ready, c.next(h_ready, len(segs)))
                    scaled(k + 1)
                for a, b, _, B in segs:
                    e.wait_ge(h_hi, c.next(h_hi))
                    if B is None:
                        e.tensor_tensor(lo[:, k, a:b], t2[:, k % 2, a:b], hi[:, k, a:b].bitcast(F32),
                                        ALU.subtract).then_inc(h_ready, 1)
                    else:
                        e.scalar_tensor_tensor(out=lo[:, k, a:b], in0=t2[:, k % 2, a:b], scalar=B(k),
                                               in1=hi[:, k, a:b].bitcast(F32), op0=ALU.add,
                                               op1=ALU.subtract).then_inc(h_ready, 1)
            e.wait_ge(h_ready, c.next(h_ready, 2 * len(segs)))

        def dve_prenorm(e, c, segs):
            dve_apply(e, c, xres, hh, hl, range(KT), segs)

        def pe_linear_y(e, c, T, xh, xl, kt):
            kts = [(k, k, P) for k in range(kt)]

            def body(e, i):
                for _ in range(2):
                    slab(e, c, T, xh, xl, kts)
            turns(e, c, KT // 2, body)

        def act_linear_y(e, c, kt):
            def body(e, i):
                for _ in range(2):
                    head(e, c, kt)
                    passed(c)
            turns(e, c, KT // 2, body)

        def dve_linear_y(e, c, T, y, first=True, last=True):
            if last:
                e.memset(ysum[:, 0:T], 0.0).then_inc(dve_step, 1)
                e.wait_ge(dve_step, c.next(dve_step))
                past(e, dve_past)

            def body(e, i):
                for j in range(2):
                    s = c.turn("slab")
                    ym = y[:, bass.ds(2 * i + j, 1), :].rearrange("p o (b n) -> p (o b) n", b=nb(T)[0])
                    e.wait_ge(slab_done, c.next(slab_done))
                    if first:
                        e.tensor_scalar(ym, p3(acc[s], T), 1.0, None, ALU.mult).then_inc(dve_step, 1)
                    else:
                        e.tensor_tensor(ym, p3(acc[s], T), ym, ALU.add).then_inc(dve_step, 1)
                    e.wait_ge(dve_step, c.next(dve_step))
                    e.sem_inc(acc_free[s], 1)
                    if last:
                        e.tensor_tensor(v3(sq[:, j, 0:T], T), ym, ym, ALU.mult).then_inc(dve_step, 1)
                        e.wait_ge(dve_step, c.next(dve_step))
                        e.tensor_tensor(ysum[:, 0:T], ysum[:, 0:T], sq[:, j, 0:T], ALU.add).then_inc(dve_step, 1)
                        e.wait_ge(dve_step, c.next(dve_step))
            turns(e, c, KT // 2, body)
            if last:
                e.sem_inc(ysum_ready, 1)

        def pe_postnorm(e, c, T):
            b, n = nb(T)
            e.wait_ge(pt_free, c.next(pt_free))
            e.wait_ge(ysum_ready, c.next(ysum_ready))
            for i in range(b):
                mm = e.matmul(pt[:, i, 0:n], ones[:, :], ysum[:, i * n:i * n + n], start=True, stop=True)
            mm.then_inc(ystat_done, 1)

        def act_postnorm(e, c, T):
            e.wait_ge(ystat_done, c.next(ystat_done))
            act_rstd(e, c, T)

        def dve_postnorm(e, c, T, y, segs):
            e.wait_ge(rstd_ready, c.next(rstd_ready))

            def scaled(k):
                for a, b, G in segs:
                    e.scalar_tensor_tensor(out=t2[:, k % 2, a:b], in0=y[:, k, a:b], scalar=G(k),
                                           in1=rstd[:, a:b], op0=ALU.mult, op1=ALU.mult).then_inc(dve_step, 1)

            scaled(0)
            for k in range(KT):
                e.wait_ge(dve_step, c.next(dve_step, len(segs)))
                if k + 1 < KT:
                    if k:
                        e.wait_ge(x_ready, c.next(x_ready))
                    scaled(k + 1)
                e.tensor_tensor(xres[:, k, 0:T], xres[:, k, 0:T], t2[:, k % 2, 0:T], ALU.add).then_inc(x_ready, 1)
            e.wait_ge(x_ready, c.next(x_ready, 2))

        def pe_tiles(e, c, tiles, kts, xh, xl, fresh=0, tail_w=None):
            take(e, c, acc_free + [pt_free] + ob_free)

            def post(j):
                t = tiles[j]
                e.wait_ge(raw_ready, c.next(raw_ready))
                if t["kind"] == "plain":
                    return
                if t["kind"] == "rope":
                    M = t["M"]
                    e.matmul(ob[j % 2][0:M, 0:SEQ], perm[0:M, 0:M], t2raw(j)[0:M, 0:SEQ], start=True,
                             stop=True).then_inc(post_done, 1)
                else:
                    n, r0 = t["n"], t["r0"]
                    past(e, pe_past)
                    for i, cols in enumerate(t["tok"]):
                        tr = e.transpose(pt[:, i * n // 512, i * n % 512:i * n % 512 + n],
                                         t2raw(j)[r0:r0 + n, cols], ident[r0:r0 + n, r0:r0 + n])
                    tr.then_inc(post_done, 1)

            out = 0
            for j in range(len(tiles) + 1):
                if j < len(tiles):
                    t = tiles[j]
                    slab(e, c, t["T"], t.get("xh", xh), t.get("xl", xl), t.get("kts", kts), M=t["M"],
                         fresh=fresh if j == 0 else 0, free=False, c0=t.get("c0", 0))
                if j:
                    need = j - 1 if tiles[j - 1]["kind"] in ("v", "kv") else max(j - 3, 0)
                    if need > out and tiles[j - 1]["kind"] != "plain":
                        e.wait_ge(tile_ready, c.next(tile_ready, need - out))
                        out = need
                    post(j - 1)
            e.wait_ge(tile_ready, c.next(tile_ready, len(tiles) - out))
            give(e, acc_free + [pt_free] + ob_free)

        def t2raw(j):
            return sq[:, j % 2, :]

        def act_tiles(e, c, tiles, heads):
            for j, t in enumerate(tiles):
                head(e, c, *heads[j])
                T, M = t["T"], t["M"]
                e.wait_ge(slab_done, c.next(slab_done))
                if j >= 2:
                    e.wait_ge(tile_ready, c.next(tile_ready))
                e.activation(v3(t2raw(j)[0:M, 0:T], T), p3(acc[c.turn("acc")], T, M), ACT.Copy).then_inc(raw_ready, 1)
                if t["kind"] != "v":
                    e.wait_ge(sum_ready, c.next(sum_ready))
                    e.activation(t["hi"], t.get("arrange", same)(t2[0:t["R"], j % 2, 0:T]), ACT.Copy).then_inc(tile_hi, 1)
            c.next(tile_ready, min(2, len(tiles)))

        def dve_tiles(e, c, tiles):
            for j, t in enumerate(tiles):
                T, M = t["T"], t["M"]
                c.turn("slab")
                c.next(slab_done)
                raw, w = t2raw(j), t2[0:t.get("R", M), j % 2, :]
                e.wait_ge(raw_ready, c.next(raw_ready))
                if t["kind"] == "rope":
                    e.tensor_tensor(w[:, 0:SEQ], raw[0:M, 0:SEQ], rope_c[0:M, :], ALU.mult).then_inc(dve_step, 1)
                    if T > SEQ:
                        e.tensor_copy(w[:, SEQ:T], raw[0:M, SEQ:T]).then_inc(dve_step, 1)
                    e.wait_ge(post_done, c.next(post_done))
                    e.tensor_tensor(ysum[0:M, 0:SEQ], ob[j % 2][0:M, 0:SEQ], rope_s[0:M, :], ALU.mult)\
                     .then_inc(dve_step, 1)
                    e.wait_ge(dve_step, c.next(dve_step, 3 if T > SEQ else 2))
                    e.tensor_tensor(w[:, 0:SEQ], w[:, 0:SEQ], ysum[0:M, 0:SEQ], ALU.add).then_inc(sum_ready, 1)
                elif t["kind"] == "plain":
                    e.tensor_copy(w[:, 0:T], raw[0:M, 0:T]).then_inc(sum_ready, 1)
                else:
                    if t["kind"] == "kv":
                        e.tensor_copy(w[:, 0:T], raw[0:t["R"], 0:T]).then_inc(sum_ready, 1)
                    e.wait_ge(post_done, c.next(post_done))
                    n, cnt = t["n"], len(t["tok"])
                    fit = min(cnt, 512 // n)
                    e.tensor_copy(t["v"][:, 0:fit, :], pt[:, 0, 0:fit * n].rearrange("p (t d) -> p t d", d=n))\
                     .then_inc(dve_step, 1)
                    if cnt > fit:
                        e.tensor_copy(t["v"][:, fit:cnt, :], pt[:, 1, 0:(cnt - fit) * n]
                                      .rearrange("p (t d) -> p t d", d=n)).then_inc(dve_step, 1)
                    e.wait_ge(dve_step, c.next(dve_step, 1 + (cnt > fit)))
                if t["kind"] == "v":
                    e.sem_inc(tile_ready, 1)
                else:
                    e.wait_ge(tile_hi, c.next(tile_hi))
                    e.tensor_tensor(t["lo"], t.get("arrange", same)(w[:, 0:T]), t["hi"].bitcast(F32), ALU.subtract)\
                     .then_inc(tile_ready, 1)

        def same(ap):
            return ap

        def pe_attention(e, c, its):
            N = len(its)
            take(e, c, acc_free + [pt_free])
            for n in range(N + 2):
                if n < N:
                    t = its[n]
                    S = acc[n % 2][:, :, :].rearrange("p b n -> p (b n)")
                    for q_hi, q_lo, k_hi, k_lo, c0 in t["keys"]:
                        mm = mm3(e, S[:, c0:c0 + k_hi.shape[-1]], q_hi, q_lo, k_hi, k_lo, True, True)
                    mm.then_inc(scores_done, 1)
                if n >= 2:
                    e.wait_ge(pta_ready, c.next(pta_ready))
                    if len(its[n - 2]["v"]) > 4:
                        e.wait_ge(ptb_ready, c.next(ptb_ready))
                if 1 <= n <= N:
                    t, s = its[n - 1], (n - 1) % 2
                    e.wait_ge(probs_ready, c.next(probs_ready))
                    for j in range(len(t["v"])):
                        tr = e.transpose(pt[:, j // 4, j % 4 * P:j % 4 * P + P], t2[:, s, j * P:j * P + P], ident[:, :])
                    tr.then_inc(tr_done, 1)
                if n >= 2:
                    t, s = its[n - 2], n % 2
                    e.wait_ge(ob_free[s], c.next(ob_free[s]))
                    for j, vj in enumerate(t["v"]):
                        mm = e.matmul(ob[s][:, 0:t["dv"]], sq[:, s, j * P:j * P + P], vj,
                                      start=j == 0, stop=j == len(t["v"]) - 1)
                    mm.then_inc(pv_done, 1)
            take(e, c, ob_free)
            give(e, acc_free + [pt_free] + ob_free)

        MX, NB, DEN, RD, ES, SK = 0, 4, 8, 12, 16, 20

        def act_attention(e, c, its):
            N = len(its)
            for n in range(N + 2):
                if n < N:
                    t, s = its[n], n % 2
                    w, c0 = len(t["v"]) * P, t["c0"]
                    e.wait_ge(nb_ready, c.next(nb_ready))
                    e.wait_ge(tr_done, c.next(tr_done, view="slot"))
                    S = acc[s][:, :, :].rearrange("p b n -> p (b n)")[:, c0:c0 + w]
                    src = t2[:, s, 0:w] if t["mask"] is not None else S
                    if t["sink"] is not None:
                        e.activation(small[:, ES + n % 4:ES + n % 4 + 1], small[:, SK + t["sink"]:SK + t["sink"] + 1],
                                     ACT.Exp, bias=small[:, NB + n % 4:NB + n % 4 + 1]).then_inc(sink_ready, 1)
                    e.activation(t2[:, s, 0:w], src, ACT.Exp, bias=small[:, NB + n % 4:NB + n % 4 + 1],
                                 scale=t["scale"], accum_out=small[:, DEN + n % 4:DEN + n % 4 + 1])\
                     .then_inc(probs_ready, 1)
                if 1 <= n <= N:
                    t, s = its[n - 1], (n - 1) % 2
                    w = min(len(t["v"]) * P, 512)
                    e.wait_ge(tr_done, c.next(tr_done))
                    e.wait_ge(pv_done, c.next(pv_done, view="slot"))
                    e.activation(sq[:, s, 0:w], pt[:, 0, 0:w], ACT.Copy).then_inc(pta_ready, 1)
                if n >= 2 and its[n - 2]["out"] == "map1":
                    act_subnorm(e, c)

        def dve_attention(e, c, its):
            N = len(its)

            def col(k, n):
                return small[:, k + n % 4:k + n % 4 + 1]

            for n in range(N + 2):
                if n < N:
                    t, s = its[n], n % 2
                    w, c0 = len(t["v"]) * P, t["c0"]
                    S = acc[s][:, :, :].rearrange("p b n -> p (b n)")[:, c0:c0 + w]
                    e.wait_ge(scores_done, c.next(scores_done))
                    e.wait_ge(tr_done, c.next(tr_done, view="slot"))
                    if t["mask"] is not None:
                        past(e, dve_past)
                        e.tensor_tensor_reduce(t2[:, s, 0:w], S, t["mask"], 1.0, -3e38, ALU.add, ALU.max,
                                               col(MX, n)).then_inc(dve_step, 1)
                    else:
                        e.tensor_reduce(col(MX, n), S, AX_X, ALU.max).then_inc(dve_step, 1)
                    e.wait_ge(dve_step, c.next(dve_step))
                    if t["sink"] is not None:
                        k = SK + t["sink"]
                        e.scalar_tensor_tensor(out=col(MX, n), in0=small[:, k:k + 1], scalar=1.0 / t["scale"],
                                               in1=col(MX, n), op0=ALU.mult, op1=ALU.max).then_inc(dve_step, 1)
                        e.wait_ge(dve_step, c.next(dve_step))
                    e.tensor_scalar(col(NB, n), col(MX, n), -t["scale"], None, ALU.mult).then_inc(nb_ready, 1)
                if 1 <= n <= N:
                    t, s = its[n - 1], (n - 1) % 2
                    e.wait_ge(tr_done, c.next(tr_done))
                    free = c.next(pv_done, view="slot")
                    if len(t["v"]) > 4:
                        e.wait_ge(pv_done, free)
                        w = (len(t["v"]) - 4) * P
                        e.tensor_copy(sq[:, s, 512:512 + w], pt[:, 1, 0:w]).then_inc(ptb_ready, 1)
                if n >= 2:
                    t, s, m = its[n - 2], n % 2, n - 2
                    if t["sink"] is not None:
                        e.wait_ge(sink_ready, c.next(sink_ready))
                    e.wait_ge(pv_done, c.next(pv_done))
                    if t["sink"] is not None:
                        e.tensor_tensor(col(DEN, m), col(DEN, m), col(ES, m), ALU.add).then_inc(dve_step, 1)
                        e.wait_ge(dve_step, c.next(dve_step))
                    e.reciprocal(col(RD, m), col(DEN, m)).then_inc(dve_step, 1)
                    e.wait_ge(dve_step, c.next(dve_step))
                    O = ob[s][:, 0:t["dv"]]
                    if t["out"] == "plain":
                        e.tensor_scalar(t["dst"], O, col(RD, m), None, ALU.mult).then_inc(ob_free[s], 1)
                    elif t["out"] == "map0":
                        e.tensor_scalar(o1[:, 0, :], O, col(RD, m), None, ALU.mult).then_inc(dve_step, 1)
                        e.wait_ge(dve_step, c.next(dve_step))
                        e.sem_inc(ob_free[s], 1)
                    else:
                        e.tensor_scalar(col(RD, m), col(RD, m), small[:, 40:41], None, ALU.mult).then_inc(dve_step, 1)
                        e.wait_ge(dve_step, c.next(dve_step))
                        e.scalar_tensor_tensor(out=o1[:, 1, :], in0=O, scalar=col(RD, m), in1=o1[:, 0, :],
                                               op0=ALU.mult, op1=ALU.add).then_inc(dve_step, 1)
                        e.wait_ge(dve_step, c.next(dve_step))
                        e.sem_inc(ob_free[s], 1)
                        e.tensor_tensor_reduce(o1[:, 0, :], o1[:, 1, :], o1[:, 1, :], 1.0, 0.0, ALU.mult, ALU.add,
                                               small[:, 41:42]).then_inc(ss_ready, 1)
                        e.wait_ge(subn_ready, c.next(subn_ready))
                        e.scalar_tensor_tensor(out=t["dst"], in0=o1[:, 1, :], scalar=small[:, 43:44], in1=subg[:, :],
                                               op0=ALU.mult, op1=ALU.mult).then_inc(dve_step, 1)
                        e.wait_ge(dve_step, c.next(dve_step))

        def act_subnorm(e, c):
            e.wait_ge(ss_ready, c.next(ss_ready))
            e.activation(small[:, 42:43], small[:, 41:42], ACT.Ln, bias=small[:, 63:64], scale=1.0 / P)\
             .then_inc(act_step, 1)
            e.wait_ge(act_step, c.next(act_step))
            e.activation(small[:, 43:44], small[:, 42:43], ACT.Exp, scale=-0.5).then_inc(subn_ready, 1)

        def pe_features(e, c, src, nf, nt):
            take(e, c, [pt_free])
            for f in range(nf):
                if f >= (2 if nt == 4 else 1):
                    e.wait_ge(feat_ready, c.next(feat_ready))
                for r in range(nt):
                    o = pt[:, f % 2, r * P:r * P + P] if nt == 4 else pt[:, r // 3, r % 3 * P:r % 3 * P + P]
                    tr = e.transpose(o, src[:, r, f * P:f * P + P], ident[:, :])
                tr.then_inc(feat_done, 1)
            e.wait_ge(feat_ready, c.next(feat_ready, 2 if nt == 4 else 1))
            give(e, [pt_free])

        def act_features(e, c, hi, nf, nt, arrange=same):
            for f in range(nf):
                e.wait_ge(feat_done, c.next(feat_done))
                src = pt[:, f % 2, :] if nt == 4 else pt[:, :, 0:384]
                dst = hi[:, f, :] if nt == 4 else v3(hi[:, f, :], TC)
                e.activation(arrange(dst), (lambda a: a.rearrange("p (r i) -> p r i", r=4))(src) if arrange is not same else src,
                             ACT.Copy).then_inc(feat_hi, 1)

        def dve_features(e, c, hi, lo, nf, nt, arrange=same):
            for f in range(nf):
                e.wait_ge(feat_hi, c.next(feat_hi))
                src = pt[:, f % 2, :] if nt == 4 else pt[:, :, 0:384]
                if arrange is not same:
                    src = src.rearrange("p (r i) -> p r i", r=4)
                h = hi[:, f, :] if nt == 4 else v3(hi[:, f, :], TC)
                l_ = lo[:, f, :] if nt == 4 else v3(lo[:, f, :], TC)
                e.tensor_tensor(arrange(l_), src, arrange(h).bitcast(F32), ALU.subtract).then_inc(feat_ready, 1)

        def pe_ffn(e, c, T, ah, al, fresh):
            for p, (_, n) in enumerate(FF_PARTS):
                def up(e, i):
                    for _ in range(4):
                        slab(e, c, T, hh, hl, K8)
                if p == 0:
                    e.wait_ge(h_ready, c.next(h_ready, KT * fresh))
                    past(e, pe_past)
                turns(e, c, n // 2, up)
                e.wait_ge(act_ready, c.next(act_ready, n))
                past(e, pe_past)
                pe_linear_y(e, c, T, ah, al, n)

        def act_ffn(e, c, T, conv, last=False):
            for p, (_, n) in enumerate(FF_PARTS):
                def up(e, i):
                    for j in range(2):
                        for part in range(2):
                            head(e, c, KT)
                            s = c.turn("acc")
                            if part == 0:
                                e.wait_ge(slab_done, c.next(slab_done))
                                if conv:
                                    e.activation(zf[:, j, PAD:], acc[s][:, 0, :], ACT.Copy).then_inc(act_step, 1)
                                    e.wait_ge(act_step, c.next(act_step))
                                    e.sem_inc(up_ready, 1)
                                    e.sem_inc(acc_free[s], 1)
                                else:
                                    e.activation(v3(sq[:, j, 0:T], T), p3(acc[s], T), ACT.Silu).then_inc(act_step, 1)
                                    e.wait_ge(act_step, c.next(act_step))
                                    e.sem_inc(silu_ready, 1)
                                    e.sem_inc(acc_free[s], 1)
                            else:
                                c.next(slab_done)
                        if conv:
                            e.wait_ge(conv_ready, c.next(conv_ready))
                            e.activation(sq[:, j, 0:T], t2[:, j, 0:T], ACT.Silu).then_inc(silu_ready, 1)
                turns(e, c, n // 2, up)

                def down(e, i):
                    for _ in range(2):
                        head(e, c, KT)
                        passed(c)
                if last and p == len(FF_PARTS) - 1:
                    turns(e, c, KT // 2 - 1, down)
                    head(e, c, KT)
                    passed(c)
                    passed(c)
                else:
                    turns(e, c, KT // 2, down)

        def dve_ffn(e, c, T, y, ah, al, conv):
            if conv:
                e.memset(zf[:, :, 0:PAD], 0.0).then_inc(dve_step, 1)
                e.wait_ge(dve_step, c.next(dve_step))
                past(e, dve_past)
            for p, (u0, n) in enumerate(FF_PARTS):
                def up(e, i):
                    for j in range(2):
                        c.turn("slab")
                        s1 = c.turn("slab")
                        c.next(slab_done)
                        u = 2 * i + (u0 + j)
                        w = t2[:, j, 0:T]
                        if conv:
                            def wcol(k):
                                return cur[:, bass.ds(u + (70 + k * FT), 1)]
                            e.wait_ge(up_ready, c.next(up_ready))
                            e.tensor_scalar(w, zf[:, j, PAD:], wcol(2), None, ALU.mult).then_inc(dve_step, 1)
                            e.wait_ge(dve_step, c.next(dve_step))
                            e.scalar_tensor_tensor(out=w, in0=zf[:, j, PAD - 1:-1], scalar=wcol(1), in1=w,
                                                   op0=ALU.mult, op1=ALU.add).then_inc(dve_step, 1)
                            e.wait_ge(dve_step, c.next(dve_step))
                            e.scalar_tensor_tensor(out=w, in0=zf[:, j, PAD - 2:-2], scalar=wcol(0), in1=w,
                                                   op0=ALU.mult, op1=ALU.add).then_inc(conv_ready, 1)
                        e.wait_ge(slab_done, c.next(slab_done))
                        e.wait_ge(silu_ready, c.next(silu_ready))
                        e.tensor_tensor(v3(w, T), p3(acc[s1], T), v3(sq[:, j, 0:T], T), ALU.mult)\
                         .then_inc(dve_step, 1)
                        e.wait_ge(dve_step, c.next(dve_step))
                        e.sem_inc(acc_free[s1], 1)
                        a_h = ah[:, bass.ds(2 * i + j, 1), 0:T].rearrange("p o n -> p (o n)")
                        a_l = al[:, bass.ds(2 * i + j, 1), 0:T].rearrange("p o n -> p (o n)")
                        e.tensor_scalar(a_h, w, 1.0, None, ALU.mult).then_inc(dve_step, 1)
                        e.wait_ge(dve_step, c.next(dve_step))
                        e.tensor_tensor(a_l, w, a_h.bitcast(F32), ALU.subtract).then_inc(act_ready, 1)
                        e.wait_ge(act_ready, c.next(act_ready))
                turns(e, c, n // 2, up)
                dve_linear_y(e, c, T, y, first=p == 0, last=p == len(FF_PARTS) - 1)

        def sp_ffn(e, c, l, up, down):
            for p, (u0, n) in enumerate(FF_PARTS):
                def body(e, i):
                    for j in range(2):
                        u = (2 * i + j + u0) * P
                        load(e, c, [(0, P, rows_of(up, l, 0, KT, u))])
                        load(e, c, [(0, P, rows_of(up, l, 0, KT, u + FF))])
                turns(e, c, n // 2, body)
                sp_cols(e, c, down, l, n, u0 * P)

        def sp_cols(e, c, W, l, kt, k0=0):
            def body(e, i):
                for j in range(2):
                    load(e, c, [(0, P, rows_of(W, l, k0, kt, (2 * i + j) * P))])
            turns(e, c, KT // 2, body)

        block = ctx.enter_context(nc.Block())

        @block.sync
        def _(sp):
            c = Counts()
            def rows(t, r0, ap):
                sp.dma_start(prow[r0:r0 + ap.shape[0], t, 0:ap.shape[1]], ap).then_inc(loaded, 16)

            for n, name in enumerate(NORMS):
                rows(0, 16 * n, A[name].rearrange("l (k p) -> (l k) p", p=P))
            rows(1, 0, A["conv_b_w"].rearrange("l k (t p) -> (l k t) p", p=P))
            rows(1, 18, A["norm_g_2"].rearrange("l g (k p) -> (l g k) p", p=P))
            rows(1, 82, A["c_2"].rearrange("o (k p) -> (o k) p", p=P))
            rows(1, 90, A["c_ctx_2"].rearrange("(k p) -> k p", p=P))
            rows(1, 98, A["mla_q_norm_g_2"].rearrange("o (k p) -> (o k) p", p=P))
            rows(1, 101, A["mla_kv_norm_g_2"].rearrange("o (k p) -> (o k) p", p=P))
            rows(2, 0, A["ada_b_2"].rearrange("l (k p) -> (l k) p", p=P))
            for l in range(DEPTH):
                rows(3 + l, 0, A["conv_ffn_w"][l].rearrange("k (u p) -> (k u) p", p=P))
            rows(5, 0, A["pool_scale"].rearrange("l (g p) -> (l g) p", p=PG))
            for dst, name in ((ident, "ident"), (ones, "ones"), (edge, "edge"), (perm, "perm1"), (inv1, "inv1")):
                sp.dma_start(dst[:], A[name]).then_inc(loaded, 16)
            sp.dma_start(angi[:, :], A["positions"][0].partition_broadcast(P)).then_inc(loaded, 16)
            sp.dma_start(min_[:, :, :], A["mem"][0].rearrange("(r p) d -> p r d", p=P)).then_inc(loaded, 16)
            sp.dma_start(xin[:, :, :], A["x"][0].rearrange("(r p) d -> p r d", p=P)).then_inc(loaded, 16)

            def layer(e, l):
                w_in = A["w_in"]
                for g in range(4):
                    load(e, c, [(0, P, rows_of(w_in, l, 0, KT, g * PG, PG))], PG)
                    if g == 1:
                        e.wait_ge(zone_free, c.next(zone_free))
                        e.dma_start(mask1[:, :, :], A["mask1"]).then_inc(mask_in, 16)
                for i in range(CT):
                    for k in (1, 3, 2):
                        load(e, c, [(0, P, rows_of(w_in, l, 0, KT, k * CW + i * P))])
                load(e, c, [(0, PG, A["pool_w"][bass.ds(l, 1)].rearrange("o g p m -> p (o g) m"))], PG)
                for j in range(2):
                    for base in (Q1, K1, V1):
                        for g in range(3):
                            load(e, c, [(0, P, rows_of(w_in, l, 0, KT, base + g * 256 + j * P))])

                def gates(e, m):
                    for br in range(3):
                        load(e, c, [(0, P, rows_of(w_in, l, 0, KT, m * P + (G1 + br * D)))])
                    load(e, c, [(0, PG, rows_of(A["w_branch_a"], l, 0, 4, m * P, rows=PG)),
                                (4, P, rows_of(A["w_branch_b"], l, 0, 3, m * P)),
                                (7, P, rows_of(A["w_branch_c"], l, 0, 2, m * P))])
                turns(e, c, KT, gates)
                sp_cols(e, c, A["w_out"], l, KT)
                for a in range(8):
                    load(e, c, [(0, P, rows_of(A["w_mkv"], l, 0, KT, a * P))])
                for a in range(4):
                    load(e, c, [(0, P, rows_of(A["w_mq"], l, 0, KT, a * P))])
                sp_cols(e, c, A["w_mo"], l, 4)
                sp_ffn(e, c, l, A["w_up"], A["w_down"])
            turns(sp, c, DEPTH, layer)

            ab = A["ab_w_in_2"]
            for col in (1024, 1152):
                load(sp, c, [(0, P, rows_of(ab, 0, 0, KT, col))])
            sp.wait_ge(zone_free, c.next(zone_free))
            sp.dma_start(cin[:, :, :], A["ctx_2"][0].rearrange("(r p) d -> p r d", p=P)).then_inc(ctx_in, 16)
            for dst, name in ((rope_c, "cos_ab"), (rope_s, "sin_ab"), (perm, "perm_ab")):
                sp.dma_start(dst[:, :], A[name]).then_inc(ctx_in, 16)
            for l in range(DEPTH):
                def ada(e, i):
                    for j in range(2):
                        for h in range(2):
                            e.wait_ge(ada_used, c.next(ada_used))
                            w = A["ada_w_2"][l, h * 512:h * 512 + 512, bass.ds((2 * i + j) * 512, 512)]
                            e.dma_start(adaw[:, h, :, :], w.rearrange("(k p) m -> p k m", p=P)).then_inc(ada_in[h], 16)
                turns(sp, c, 6, ada)
            sp.wait_ge(zone_free, c.next(zone_free))
            sp.dma_start(mask2[:, :, :], A["mask2"]).then_inc(mask_in, 16)
            sp.dma_start(sink[:, :], A["ab_sink_2"][0].partition_broadcast(P)).then_inc(mask_in, 16)
            sp.dma_start(subg[:, :], A["diff_subln_g_2"][0].partition_broadcast(P)).then_inc(mask_in, 16)
            sp.dma_start(lamv[:, :, :], A["diff_lambda_2"][0].partition_broadcast(P)).then_inc(mask_in, 16)

            def heads_ab(e, t):
                s = c.turn("slab")
                e.wait_ge(lo_ready, c.next(lo_ready))
                for half in range(2):
                    e.dma_start(wraw[:, s, 0:KT, half * HD:half * HD + HD],
                                rows_of(ab, 0, 0, KT, t * HD + half * 256, HD)).then_inc(landed[s], 16)
                for col in (512, 1280, 1792):
                    load(e, c, [(0, P, rows_of(ab, 0, 0, KT, t * P + col))])
            turns(sp, c, 4, heads_ab)
            sp_cols(sp, c, A["ab_w_out_2"], 0, KT)
            sp_ffn(sp, c, 0, A["ffn_w13_2"], A["ffn_w2_2"])
            w = A["mla_w_in_2"]
            for j in range(2):
                load(sp, c, [(0, P, rows_of(w, 0, 0, KT, j * P))])
            sp.wait_ge(zone_free, c.next(zone_free))
            for dst, name in ((rope_c, "cos_c"), (rope_s, "sin_c"), (perm, "perm_c")):
                sp.dma_start(dst[:, :], A[name]).then_inc(ctx_in, 16)
            for j in range(2, 5):
                load(sp, c, [(0, P, rows_of(w, 0, 0, KT, j * P))])
            load(sp, c, [(0, P, rows_of(w, 0, 0, KT, 576, PG))], PG)

            def heads_c(e, i):
                for j in range(2):
                    load(e, c, [(0, P, rows_of(A["mla_wq_b_2"], 0, 0, 3, (2 * i + j) * PG, PG))], PG)
                    load(e, c, [(0, P, rows_of(A["mla_wkv_b_2"], 0, 0, 2, (2 * i + j) * P))])
            turns(sp, c, 8, heads_c)
            sp_cols(sp, c, A["mla_w_out_2"], 0, KT)
            sp_ffn(sp, c, 1, A["ffn_w13_2"], A["ffn_w2_2"])
            for r in range(4):
                sp.wait_ge(lt_out, r + 1 + 2 * KT)
                sp.dma_start(out[0, r * P:r * P + P, :], outb[:, r, :]).then_inc(stored, 16)
            sp.wait_ge(stored, 64)

        @block.gpsimd
        def _(pool):
            c = Counts()
            for s in range(2):
                pool.memset(wraw[:, s, :, :], 0.0).then_inc(lo_ready, 1)

            def cols(e, kt, n):
                def body(e, i):
                    for _ in range(2):
                        tail(e, c, kt)
                turns(e, c, n // 2, body)

            def ffn(e):
                for _, n in FF_PARTS:
                    cols(e, KT, 2 * n)
                    cols(e, n, KT)

            def layer(e, l):
                cols(e, KT, 4 + 9 - 1)
                tail(e, c, KT)
                tail(e, c, 4)
                cols(e, KT, 18)

                def gates(e, m):
                    for _ in range(3):
                        tail(e, c, KT)
                    tail(e, c, 9)
                turns(e, c, KT, gates)
                cols(e, KT, 8 + 12)
                cols(e, 4, KT)
                ffn(e)
            turns(pool, c, DEPTH, layer)
            cols(pool, KT, 2 + 16 + KT)
            ffn(pool)
            cols(pool, KT, 6)

            def heads_c(e, i):
                for _ in range(2):
                    tail(e, c, 3)
                    tail(e, c, 2)
            turns(pool, c, 8, heads_c)
            cols(pool, KT, KT)
            ffn(pool)

        def by_residue(ap):
            return ap.rearrange("p (i r) -> p r i", r=RES)

        def tiles_1(j):
            def qk(hi, lo, g):
                return dict(kind="rope", M=P, R=P, T=SEQ, hi=by_res_view(hi[:, g, :]), lo=by_res_view(lo[:, g, :]),
                            arrange=by_residue)
            tok = [slice(r, SEQ, RES) for r in range(RES)]
            return ([qk(qh, ql, g) for g in range(3)] + [qk(kh, kl, g) for g in range(3)]
                    + [dict(kind="v", M=P, T=SEQ, n=P, r0=0, tok=tok, v=vt[:, g, :, :]) for g in range(3)])

        def by_res_view(ap):
            return ap.rearrange("p (r i) -> p r i", r=RES)

        def its_1(j):
            its = []
            for h in range(2):
                rs = slice(h * HD, h * HD + HD)
                for r in range(RES):
                    cs = slice(r * P, r * P + P)
                    keys = [(qh[rs, 0, cs], ql[rs, 0, cs], kh[rs, 0, :], kl[rs, 0, :], 0)]
                    keys += [(qh[rs, g, cs], ql[rs, g, cs], kh[rs, g, cs], kl[rs, g, cs], 384 + g * P) for g in (1, 2)]
                    v = [vt[:, 0, i, rs] for i in range(RES)] + [vt[:, 1, r, rs], vt[:, 2, r, rs]]
                    its.append(dict(keys=keys, v=v, c0=0, mask=mask1[:, r, :], sink=None, scale=HD ** -0.5, dv=HD,
                                    out="plain", dst=ot1[:, r, (2 * j + h) * HD:(2 * j + h + 1) * HD]))
            return its

        def tiles_mem():
            ctx_cols = [slice(i * P, i * P + P) for i in range(2)]
            return ([dict(kind="plain", M=P, R=P, T=CTX, hi=kmh[:, a, :], lo=kml[:, a, :]) for a in range(4)]
                    + [dict(kind="v", M=P, T=CTX, n=P, r0=0, tok=ctx_cols, v=vm[:, a, :, :]) for a in range(4)]
                    + [dict(kind="plain", M=P, R=P, T=SEQ, hi=qmh[:, a, :], lo=qml[:, a, :]) for a in range(4)])

        def its_mem():
            return [dict(keys=[(qmh[:, a, r * P:r * P + P], qml[:, a, r * P:r * P + P], kmh[:, a, :], kml[:, a, :], 0)],
                         v=[vm[:, a, i, :] for i in range(2)], c0=0, mask=None, sink=None, scale=P ** -0.5, dv=P,
                         out="plain", dst=otm[:, r, a * P:a * P + P]) for a in range(4) for r in range(4)]

        all_tok = [slice(i * P, i * P + P) for i in range(6)]

        def tile_kg():
            return [dict(kind="rope", M=P, R=P, T=TC, hi=kgh[:, :], lo=kgl[:, :]),
                    dict(kind="v", M=P, T=TC, n=P, r0=0, tok=all_tok, v=vg[:, :, :])]

        def tiles_ab():
            return [dict(kind="rope", M=P, R=P, T=TC, hi=qgh[:, :], lo=qgl[:, :]),
                    dict(kind="rope", M=P, R=P, T=TC, hi=qdh[:, :], lo=qdl[:, :]),
                    dict(kind="rope", M=P, R=P, T=TC, hi=kdh[:, :], lo=kdl[:, :]),
                    dict(kind="v", M=P, T=TC, n=P, r0=0, tok=all_tok, v=vd[:, :, :])]

        def its_ab(t):
            def keys(q_hi, q_lo, k_hi, k_lo, rs, r):
                cs = slice(r * P, r * P + P)
                parts = [(0, SEQ), (SEQ, TC)] if r < 4 else [(SEQ, TC)]
                return [(q_hi[rs, cs], q_lo[rs, cs], k_hi[rs, a:b], k_lo[rs, a:b], a) for a, b in parts]
            its = []
            for h in range(2):
                rs = slice(h * HD, h * HD + HD)
                for r in range(6):
                    v = [vg[:, i, rs] for i in range(0 if r < 4 else 4, 6)]
                    its.append(dict(keys=keys(qgh, qgl, kgh, kgl, rs, r), v=v, c0=0 if r < 4 else SEQ,
                                    mask=mask2[:, r, :] if r < 4 else None, sink=h, scale=HD ** -0.5, dv=HD, out="plain",
                                    dst=ot2[:, r, bass.ds(t * HD + h * 256, HD)]))
            for r in range(6):
                for m in range(2):
                    v = [vd[:, i, :] for i in range(0 if r < 4 else 4, 6)]
                    its.append(dict(keys=keys(qdh, qdl, kdh, kdl, slice(m * HD, m * HD + HD), r), v=v,
                                    c0=0 if r < 4 else SEQ, mask=None, sink=None, scale=HD ** -0.5, dv=P,
                                    out=f"map{m}", dst=ot2[:, r, bass.ds(t * P + 512, P)]))
            return its

        def tile_kr():
            return [dict(kind="rope", M=PG, R=PG, T=TC, hi=kch[0:PG, 0, :], lo=kcl[0:PG, 0, :])]

        def tiles_c():
            out_ = []
            for j in range(2):
                out_ += [dict(kind="rope", M=PG, R=PG, T=SEQ, hi=qch[0:PG, j, :], lo=qcl[0:PG, j, :],
                              kts=[(k, k, P) for k in range(3)]),
                         dict(kind="kv", M=P, R=HD, T=TC, n=HD, r0=HD, tok=all_tok, v=vc[:, j, :, :],
                              hi=kch[0:HD, j, :], lo=kcl[0:HD, j, :], kts=[(k, 3 + k, P) for k in range(2)])]
            return out_

        def its_c(i):
            return [dict(keys=[(qch[0:PG, j, r * P:r * P + P], qcl[0:PG, j, r * P:r * P + P],
                                kch[0:PG, j, a:b], kcl[0:PG, j, a:b], a) for a, b in ((0, SEQ), (SEQ, TC))],
                         v=[vc[:, j, n, :] for n in range(6)], c0=0, mask=None, sink=None, scale=PG ** -0.5, dv=HD,
                         out="plain", dst=ot3[:, r, bass.ds((2 * i + j) * HD, HD)])
                    for j in range(2) for r in range(4)]

        K9 = [[(k, k, PG) for k in range(4)], [(k, k, P) for k in range(4, 7)], [(k, k, P) for k in range(7, 9)]]

        @block.tensor
        def _(pe):
            c = Counts()
            give(pe, acc_free + [pt_free] + ob_free)
            for s in (slab_done, sq_used, tr_done, pv_done, ada_used):
                pe.sem_inc(s, 2)
            pe.sem_inc(gates_used, 1)
            c.start(lo_ready, 2)

            def turn_tokens(e, src, n):
                take(e, c, acc_free)
                for k in range(KT):
                    if k >= 2:
                        e.wait_ge(lt_out, c.next(lt_out))
                    for r in range(n):
                        tr = e.transpose(acc[k % 2][:, 0, r * P:r * P + P], src[:, r, k * P:k * P + P], ident[:, :])
                    tr.then_inc(lt_done, 1)
                e.wait_ge(lt_out, c.next(lt_out, 2))
                give(e, acc_free)

            pe.wait_ge(loaded, 16 * N_LOADS)
            take(pe, c, acc_free)
            for t, n in enumerate(PAR_ROWS):
                w = PG if t == 5 else P
                if t >= 2:
                    pe.wait_ge(set_done, c.next(set_done))
                pe.transpose(acc[t % 2][0:w, 0, 0:n], prow[0:n, t, 0:w], ident[0:n, 0:n]).then_inc(lt_done, 1)
            pe.wait_ge(set_done, c.next(set_done, 2))
            give(pe, acc_free)
            turn_tokens(pe, min_, 2)
            take(pe, c, acc_free)
            for k in range(KT):
                if k >= 2:
                    pe.wait_ge(x_ready, k - 1)
                for r in range(4):
                    tr = pe.transpose(acc[k % 2][:, 0, r * P:r * P + P], xin[:, r, k * P:k * P + P], ident[:, :])
                tr.then_inc(lt_done, 1)
            pe.wait_ge(x_ready, KT)
            give(pe, acc_free)

            def layer(e, l):
                pe_stats(e, c, TC)
                for g in range(4):
                    slab(e, c, SEQ, hh, hl, K8, M=PG, fresh=2 if g == 0 else 0)
                for i in range(3 * CT):
                    slab(e, c, SEQ, hh, hl, K8)
                s = c.turn("slab")
                e.wait_ge(lo_ready, c.next(lo_ready))
                take(e, c, [acc_free[s], pt_free])
                e.wait_ge(pool_ready, c.next(pool_ready, 4))
                for g in range(4):
                    o = (acc[s] if g < 2 else pt)[0:PG, g % 2, :]
                    mm = mm3(e, o, whi[0:PG, s, g, 0:PG], wlo[0:PG, s, g, 0:PG], poh[0:PG, g, :], pol[0:PG, g, :],
                             True, True)
                mm.then_inc(slab_done, 1)
                for j in range(2):
                    pe_tiles(e, c, tiles_1(j), K8, hh, hl)
                    pe_attention(e, c, its_1(j))
                pe_features(e, c, ot1, 2, 4)
                e.wait_ge(bi_ready, c.next(bi_ready, 4 + CT))
                past(e, pe_past)

                def gates(e, m):
                    for _ in range(3):
                        slab(e, c, SEQ, hh, hl, K8)
                    s = c.turn("slab")
                    e.wait_ge(lo_ready, c.next(lo_ready))
                    take(e, c, [acc_free[s], pt_free])
                    for o, ks in zip((acc[s][:, 0, :], acc[s][:, 1, :], pt[:, 0, :]), K9):
                        for n, (k, _, rows) in enumerate(ks):
                            mm = mm3(e, o, whi[0:rows, s, k, :], wlo[0:rows, s, k, :], bih[0:rows, k, :],
                                     bil[0:rows, k, :], n == 0, n == len(ks) - 1)
                    mm.then_inc(slab_done, 1)
                turns(e, c, KT, gates)
                e.wait_ge(merged_ready, c.next(merged_ready, KT))
                past(e, pe_past)
                pe_linear_y(e, c, SEQ, mgh, mgl, KT)
                pe_postnorm(e, c, SEQ)
                pe_stats(e, c, SEQ)
                for _ in range(KT):
                    e.wait_ge(h_ready, c.next(h_ready))
                tiles = tiles_mem()
                for t in tiles[:8]:
                    t["c0"] = SEQ
                pe_tiles(e, c, tiles, K8, hh, hl)
                pe_attention(e, c, its_mem())
                pe_features(e, c, otm, 4, 4)
                pe_linear_y(e, c, SEQ, ofh, ofl, 4)
                pe_postnorm(e, c, SEQ)
                pe_stats(e, c, SEQ)
                pe_ffn(e, c, SEQ, act1h, act1l, 1)
                pe_postnorm(e, c, SEQ)
            turns(pe, c, DEPTH, layer)

            pe.wait_ge(ctx_in, 64)
            turn_tokens(pe, cin, 2)
            for l in range(DEPTH):
                take(pe, c, acc_free + [pt_free])
                if l == 0:
                    pe.wait_ge(cond_ready, 1)

                def chunks(e, i):
                    for j in range(2):
                        e.wait_ge(ada_out, c.next(ada_out))
                        for h in range(2):
                            e.wait_ge(ada_in[h], c.next(ada_in[h], 16))
                            for k in range(4):
                                mm = e.matmul(acc[j][0:2, 0, :], scT[:, 4 * h + k, :], adaw[:, h, k, :],
                                              start=h == 0 and k == 0, stop=h == 1 and k == 3)
                            mm.then_inc(ada_used, 1)
                turns(pe, c, 6, chunks)
                pe.wait_ge(ada_out, c.next(ada_out, 2))
                for j in range(6 * KT):
                    tr = pe.transpose(pt[:, 0, 2 * j:2 * j + 2], adar[0:2, j * P:j * P + P], ident[0:2, 0:2])
                tr.then_inc(ada_done, 1)
                pe.wait_ge(ada_out, c.next(ada_out))
                give(pe, acc_free + [pt_free])
            pe_stats(pe, c, TC)
            pe_tiles(pe, c, tile_kg(), K8, hh, hl, fresh=2)

            def heads_ab(e, t):
                pe_tiles(e, c, tiles_ab(), K8, hh, hl)
                pe_attention(e, c, its_ab(t))
            turns(pe, c, 4, heads_ab)
            pe_features(pe, c, ot2, KT, 6)
            pe_linear_y(pe, c, TC, hh, hl, KT)
            pe_postnorm(pe, c, TC)
            pe_stats(pe, c, TC)
            pe_ffn(pe, c, TC, acth, actl, 2)
            pe_postnorm(pe, c, TC)
            pe_stats(pe, c, TC)
            for j in range(5):
                slab(pe, c, SEQ if j < 3 else TC, hh, hl, K8, fresh=2 if j == 0 else 0)
                if j in (2, 4):
                    pe_postnorm(pe, c, SEQ if j < 3 else TC)
            pe.wait_ge(ctx_in, 112)
            pe.wait_ge(h_ready, c.next(h_ready, 5))
            pe_tiles(pe, c, tile_kr(), K8, hh, hl)
            pe.wait_ge(kr_ready, 2)

            def heads_c(e, i):
                pe_tiles(e, c, tiles_c(), None, lath, latl)
                pe_attention(e, c, its_c(i))
            turns(pe, c, 8, heads_c)
            pe_features(pe, c, ot3, KT, 4)
            pe_linear_y(pe, c, SEQ, o3h, o3l, KT)
            pe_postnorm(pe, c, SEQ)
            pe_stats(pe, c, SEQ)
            pe_ffn(pe, c, SEQ, act1h, act1l, 1)
            pe_postnorm(pe, c, SEQ)
            take(pe, c, acc_free)
            pe.wait_ge(x_ready, KT * (1 + 3 * DEPTH + 2 * DEPTH))
            for r in range(4):
                if r >= 2:
                    pe.wait_ge(lt_out, c.next(lt_out))
                for k in range(KT):
                    tr = pe.transpose(acc[r % 2][:, k // 4, k % 4 * P:k % 4 * P + P], xres[:, k, r * P:r * P + P], ident[:, :])
                tr.then_inc(lt_done, 1)

        @block.scalar
        def _(act):
            c = Counts()
            for s in (slab_done, sq_used):
                c.start(s, 2, "" if s is slab_done else "all")
            c.start(tr_done, 2)
            c.start(pv_done, 2)
            act.wait_ge(set_done, 1 + len(PAR_ROWS))
            act.activation(rope_s[:, :], red[:, :], ACT.Sin).then_inc(act_step, 1)
            act.wait_ge(set_done, 2 + len(PAR_ROWS))
            act.activation(rope_c[:, :], turn_n[:, :], ACT.Sin).then_inc(act_step, 1)
            act.wait_ge(act_step, c.next(act_step, 2))
            act.sem_inc(tables_ready, 1)
            head(act, c, KT)

            def layer(e, l):
                act_prenorm(e, c, TC, segs_a())
                for g in range(4):
                    head(e, c, KT)
                    s = c.turn("acc")
                    e.wait_ge(slab_done, c.next(slab_done))
                    if g >= 2:
                        e.wait_ge(pool_ready, c.next(pool_ready))
                    e.activation(ub[0:PG, g % 2, PAD:], acc[s][0:PG, 0, :], ACT.Copy).then_inc(act_step, 1)
                    e.wait_ge(act_step, c.next(act_step))
                    e.sem_inc(in_ready, 1)
                    e.sem_inc(acc_free[s], 1)
                    e.wait_ge(sum_ready, c.next(sum_ready))
                    e.activation(poh[0:PG, g, :], t2[0:PG, g % 2, 0:SEQ], ACT.Copy).then_inc(pool_hi, 1)
                c.next(pool_ready, 2)
                for i in range(CT):
                    head(e, c, KT)
                    s = c.turn("acc")
                    e.wait_ge(slab_done, c.next(slab_done))
                    if i == 2:
                        e.wait_ge(bi_ready, c.next(bi_ready))
                    e.activation(bxs[:, i % 2, :], acc[s][:, 0, :], ACT.Copy).then_inc(act_step, 1)
                    e.wait_ge(act_step, c.next(act_step))
                    e.sem_inc(in_ready, 1)
                    e.sem_inc(acc_free[s], 1)
                    head(e, c, KT)
                    passed(c)
                    head(e, c, KT if i < 2 else 4)
                    passed(c)
                    e.wait_ge(sum_ready, c.next(sum_ready))
                    e.activation(bih[:, 4 + i, :], t2[:, i % 2, 0:SEQ], ACT.Copy).then_inc(bi_hi, 1)
                c.next(bi_ready, 2)
                head(e, c, KT)
                passed(c)
                for g in range(4):
                    e.wait_ge(sum_ready, c.next(sum_ready))
                    e.activation(bih[0:PG, g, :], t2[0:PG, g % 2, 0:SEQ], ACT.Copy).then_inc(bi_hi, 1)
                c.next(bi_ready, 4)
                for j in range(2):
                    act_tiles(e, c, tiles_1(j), [(KT,)] * 9)
                    act_attention(e, c, its_1(j))
                act_features(e, c, bih[:, 7:9, :], 2, 4, by_residue)

                def gates(e, m):
                    e.wait_ge(gates_used, c.next(gates_used))
                    for b in range(3):
                        head(e, c, *((KT,) if b < 2 else (9, 3)))
                        s = c.turn("acc")
                        e.wait_ge(slab_done, c.next(slab_done))
                        e.activation(GATE[b], acc[s][:, 0, :], ACT.Sigmoid).then_inc(act_step, 1)
                        e.wait_ge(act_step, c.next(act_step))
                        e.sem_inc(gate_ready, 1)
                        e.sem_inc(acc_free[s], 1)
                    head(e, c, KT)
                    passed(c)
                turns(e, c, KT, gates)
                act_linear_y(e, c, KT)
                act_postnorm(e, c, SEQ)
                act_prenorm(e, c, SEQ, segs_m())
                act_tiles(e, c, tiles_mem(), [(KT,)] * 11 + [(4,)])
                act_attention(e, c, its_mem())
                act_features(e, c, ofh, 4, 4)
                for i in range(KT):
                    head(e, c, 4 if i < KT - 1 else KT)
                    passed(c)
                act_postnorm(e, c, SEQ)
                act_prenorm(e, c, SEQ, segs_f())
                act_ffn(e, c, SEQ, True)
                act_postnorm(e, c, SEQ)
            turns(act, c, DEPTH, layer)

            act.activation(scT[:, :, 0], par[:, 1, 82:90], ACT.Silu).then_inc(act_step, 1)
            act.activation(scT[:, :, 1], par[:, 1, 90:98], ACT.Silu).then_inc(act_step, 1)
            act.wait_ge(act_step, c.next(act_step, 2))
            act.sem_inc(cond_ready, 1)
            act.wait_ge(lam_in, 1)
            act.activation(small[:, 46:48], small[:, 44:46], ACT.Exp).then_inc(lam_out, 1)
            act_prenorm(act, c, TC, segs_2(0))
            act_tiles(act, c, tile_kg(), [(KT,), (KT, 2)])

            def turn_ab(e, t, last):
                act_tiles(e, c, tiles_ab(), [(KT,)] * 3 + [(KT,) if last else (KT, 2)])
                act_attention(e, c, its_ab(t))
            turns(act, c, 3, lambda e, t: turn_ab(e, t, False))
            turn_ab(act, 3, True)
            act_features(act, c, hh, KT, 6)
            act_linear_y(act, c, KT)
            act_postnorm(act, c, TC)
            act_prenorm(act, c, TC, segs_2(3))
            act_ffn(act, c, TC, False)
            act_postnorm(act, c, TC)
            act_prenorm(act, c, TC, segs_2(0))
            for j in range(5):
                head(act, c, KT)
                passed(c)
                if j in (2, 4):
                    T = SEQ if j < 3 else TC
                    act.wait_ge(ystat_done, c.next(ystat_done))
                    act_rstd(act, c, T, D / (C_QL if j < 3 else C_KVL))
                    act_apply(act, c, lath, range(3) if j < 3 else range(3, 5), segs_lat(T))
            act_tiles(act, c, tile_kr(), [(3,)])

            def heads_c(e, i):
                act_tiles(e, c, tiles_c(), [(2,), (3,), (2,), (KT,)])
                act_attention(e, c, its_c(i))
            turns(act, c, 8, heads_c)
            act_features(act, c, o3h, KT, 4)
            act_linear_y(act, c, KT)
            act_postnorm(act, c, SEQ)
            act_prenorm(act, c, SEQ, segs_2(3)[:1])
            act_ffn(act, c, SEQ, False, last=True)
            act_postnorm(act, c, SEQ)

        @block.vector
        def _(dve):
            c = Counts()
            for s in (slab_done, tr_done, pv_done, ada_used):
                c.start(s, 2)

            def turned(e, col0, n, signal):
                for k in range(KT):
                    e.wait_ge(lt_done, c.next(lt_done))
                    e.tensor_copy(xres[:, k, col0:col0 + n * P], acc[k % 2][:, 0, 0:n * P]).then_inc(signal, 1)

            dve.memset(small[:, 63:64], EPS).then_inc(dve_step, 1)
            dve.wait_ge(dve_step, c.next(dve_step))
            for t, n in enumerate(PAR_ROWS):
                w = PG if t == 5 else P
                dve.wait_ge(lt_done, c.next(lt_done))
                dve.tensor_copy(par[0:w, t, 0:n], acc[t % 2][0:w, 0, 0:n]).then_inc(set_done, 1)
            dve.wait_ge(loaded, 16 * N_LOADS)

            def step(ins):
                ins.then_inc(dve_step, 1)
                dve.wait_ge(dve_step, c.next(dve_step))

            step(dve.tensor_copy(ang[:, :], angi[:, :]))
            step(dve.tensor_scalar(ang[:, :], ang[:, :], inv1[:, 0:1], None, ALU.mult))
            step(dve.tensor_scalar(turn_n[:, :], ang[:, :], 1.0 / TWO_PI, ROUND, ALU.mult, ALU.add))
            step(dve.tensor_scalar(turn_n[:, :], turn_n[:, :], ROUND, None, ALU.subtract))
            for part in (CW1, CW2, CW3):
                step(dve.scalar_tensor_tensor(out=ang[:, :], in0=turn_n[:, :], scalar=-part, in1=ang[:, :],
                                              op0=ALU.mult, op1=ALU.add))
            dve.tensor_scalar(red[:, :], ang[:, :], 3.1415925, -3.1415925, ALU.min, ALU.max).then_inc(set_done, 1)
            dve.wait_ge(set_done, 1 + len(PAR_ROWS))
            step(dve.scalar_tensor_tensor(out=turn_n[:, :], in0=red[:, :], scalar=-1.0, in1=red[:, :],
                                          op0=ALU.mult, op1=ALU.max))
            dve.tensor_scalar(turn_n[:, :], turn_n[:, :], -1.0, TWO_PI / 4, ALU.mult, ALU.add).then_inc(set_done, 1)
            turned(dve, SEQ, 2, lt_out)
            turned(dve, 0, 4, x_ready)
            c.start(x_ready, KT)
            dve.wait_ge(tables_ready, 1)

            def layer(e, l):
                e.sem_inc(zone_free, 1)
                gains = par[:, 0, 0:112].rearrange("p (n l k) -> p n l k", l=DEPTH, k=KT)[:, :, bass.ds(l, 1), :]
                e.tensor_scalar(cur[:, 0:56].rearrange("p (n k) -> p n k", k=KT), gains.rearrange("p n o k -> p n (o k)"),
                                1.0, None, ALU.mult).then_inc(dve_step, 1)
                e.tensor_scalar(cur[:, 56:65], par[:, 1, bass.ds(l * 9, 9)], 1.0, None, ALU.mult).then_inc(dve_step, 1)
                e.tensor_scalar(cur[0:PG, 65:69], par[0:PG, 5, bass.ds(l * 4, 4)], 1.0, None, ALU.mult).then_inc(dve_step, 1)
                e.tensor_scalar(cur[:, 70:136], par[:, bass.ds(l + 3, 1), 0:66].rearrange("p o n -> p (o n)"), 1.0, None,
                                ALU.mult).then_inc(dve_step, 1)
                for buf in (ub, sa, zc):
                    e.memset(buf[:, :, 0:PAD], 0.0).then_inc(dve_step, 1)
                e.wait_ge(dve_step, c.next(dve_step, 7))
                dve_prenorm(e, c, segs_a())

                def st(ins):
                    ins.then_inc(dve_step, 1)
                    e.wait_ge(dve_step, c.next(dve_step))

                for g, w in enumerate(POOL_W):
                    c.turn("slab")
                    c.next(slab_done)
                    e.wait_ge(in_ready, c.next(in_ready))
                    src, shift, k = ub[0:PG, g % 2, :], 1, 0
                    u = ub[0:PG, g % 2, PAD:]
                    while shift < w:
                        dst = sa[0:PG, k % 2, :]
                        st(e.tensor_tensor(dst[:, PAD:], src[:, PAD:], src[:, PAD - shift:PAD + SEQ - shift], ALU.add))
                        src, shift, k = dst, 2 * shift, k + 1
                    pooled = t2[0:PG, g % 2, 0:SEQ]
                    e.tensor_tensor(pooled[:, 0:PAD], src[:, PAD:2 * PAD], edge[0:PG, g, :], ALU.mult).then_inc(dve_step, 1)
                    e.scalar_tensor_tensor(out=pooled[:, PAD:], in0=src[:, 2 * PAD:], scalar=1.0 / w, in1=u[:, PAD:],
                                           op0=ALU.mult, op1=ALU.subtract).then_inc(dve_step, 1)
                    e.wait_ge(dve_step, c.next(dve_step, 2))
                    e.tensor_tensor(pooled[:, 0:PAD], pooled[:, 0:PAD], u[:, 0:PAD], ALU.subtract).then_inc(sum_ready, 1)
                    e.wait_ge(pool_hi, c.next(pool_hi))
                    e.tensor_tensor(pol[0:PG, g, :], pooled, poh[0:PG, g, :].bitcast(F32), ALU.subtract)\
                     .then_inc(pool_ready, 1)
                e.wait_ge(pool_ready, c.next(pool_ready, 4))
                for i in range(CT):
                    def wcol(k):
                        return cur[:, 56 + k * CT + i:57 + k * CT + i]
                    c.turn("slab")
                    c.next(slab_done)
                    w = t2[:, i % 2, 0:SEQ]
                    e.wait_ge(in_ready, c.next(in_ready))
                    s = c.turn("slab")
                    e.wait_ge(slab_done, c.next(slab_done))
                    st(e.tensor_tensor(zc[:, i % 2, PAD:], acc[s][:, 0, :], bxs[:, i % 2, :], ALU.mult))
                    e.sem_inc(acc_free[s], 1)
                    st(e.tensor_scalar(w, zc[:, i % 2, PAD:], wcol(2), None, ALU.mult))
                    for k in (1, 0):
                        st(e.scalar_tensor_tensor(out=w, in0=zc[:, i % 2, PAD - 2 + k:PAD + SEQ - 2 + k], scalar=wcol(k),
                                                  in1=w, op0=ALU.mult, op1=ALU.add))
                    s = c.turn("slab")
                    e.wait_ge(slab_done, c.next(slab_done))
                    st(e.tensor_tensor(w, acc[s][:, 0, :], w, ALU.mult))
                    e.sem_inc(acc_free[s], 1)
                    e.sem_inc(sum_ready, 1)
                    e.wait_ge(bi_hi, c.next(bi_hi))
                    e.tensor_tensor(bil[:, 4 + i, :], w, bih[:, 4 + i, :].bitcast(F32), ALU.subtract).then_inc(bi_ready, 1)
                e.wait_ge(bi_ready, c.next(bi_ready, CT))
                s = c.turn("slab")
                e.wait_ge(slab_done, c.next(slab_done))
                for g in range(4):
                    w = t2[0:PG, g % 2, 0:SEQ]
                    st(e.tensor_scalar(w, (acc[s] if g < 2 else pt)[0:PG, g % 2, :], cur[0:PG, 65 + g:66 + g], None, ALU.mult))
                    if g == 1:
                        e.sem_inc(acc_free[s], 1)
                    if g == 3:
                        e.sem_inc(pt_free, 1)
                    e.sem_inc(sum_ready, 1)
                    e.wait_ge(bi_hi, c.next(bi_hi))
                    e.tensor_tensor(bil[0:PG, g, :], w, bih[0:PG, g, :].bitcast(F32), ALU.subtract).then_inc(bi_ready, 1)
                    e.wait_ge(bi_ready, c.next(bi_ready))
                e.wait_ge(mask_in, c.next(mask_in, 16))
                for j in range(2):
                    dve_tiles(e, c, tiles_1(j))
                    dve_attention(e, c, its_1(j))
                dve_features(e, c, bih[:, 7:9, :], bil[:, 7:9, :], 2, 4, by_residue)

                def gates(e, m):
                    c.turn("slab"), c.turn("slab"), c.turn("slab")
                    s = c.turn("slab")
                    c.next(slab_done, 3)
                    e.wait_ge(slab_done, c.next(slab_done))
                    e.wait_ge(gate_ready, c.next(gate_ready, 3))
                    for b, o in enumerate((acc[s][:, 0, :], acc[s][:, 1, :], pt[:, 0, :])):
                        e.tensor_tensor(PROD[b], o, GATE[b], ALU.mult).then_inc(dve_step, 1)
                    e.wait_ge(dve_step, c.next(dve_step, 3))
                    e.sem_inc(acc_free[s], 1)
                    e.sem_inc(pt_free, 1)
                    e.sem_inc(gates_used, 1)
                    for b in (1, 2):
                        e.tensor_tensor(PROD[0], PROD[0], PROD[b], ALU.add).then_inc(dve_step, 1)
                        e.wait_ge(dve_step, c.next(dve_step))
                    m_h = mgh[:, bass.ds(m, 1), :].rearrange("p o n -> p (o n)")
                    m_l = mgl[:, bass.ds(m, 1), :].rearrange("p o n -> p (o n)")
                    e.tensor_scalar(m_h, PROD[0], 1.0, None, ALU.mult).then_inc(dve_step, 1)
                    e.wait_ge(dve_step, c.next(dve_step))
                    e.tensor_tensor(m_l, PROD[0], m_h.bitcast(F32), ALU.subtract).then_inc(merged_ready, 1)
                    e.wait_ge(merged_ready, c.next(merged_ready))
                turns(e, c, KT, gates)
                dve_linear_y(e, c, SEQ, y1)
                dve_postnorm(e, c, SEQ, y1, [(0, SEQ, gain(8))])
                dve_prenorm(e, c, segs_m())
                dve_tiles(e, c, tiles_mem())
                dve_attention(e, c, its_mem())
                dve_features(e, c, ofh, ofl, 4, 4)
                dve_linear_y(e, c, SEQ, y1)
                dve_postnorm(e, c, SEQ, y1, [(0, SEQ, gain(24))])
                dve_prenorm(e, c, segs_f())
                dve_ffn(e, c, SEQ, y1, act1h, act1l, True)
                dve_postnorm(e, c, SEQ, y1, [(0, SEQ, gain(48))])
            turns(dve, c, DEPTH, layer)

            dve.sem_inc(zone_free, 1)
            turned(dve, SEQ, 2, lt_out)
            dve.wait_ge(ctx_in, 64)
            for l in range(DEPTH):
                dve.sem_inc(ada_out, 2)

                def chunks(e, i):
                    for j in range(2):
                        e.wait_ge(ada_used, c.next(ada_used, 2))
                        e.tensor_scalar(adar[:, bass.ds((2 * i + j) * 512, 512)], acc[j][0:2, 0, :], 1.0, None, ALU.mult)\
                         .then_inc(ada_out, 1)
                turns(dve, c, 6, chunks)
                dve.wait_ge(ada_done, l + 1)
                v = pt[:, 0, 0:96].rearrange("p (j s) -> p j s", s=2)
                for s in range(2):
                    dve.tensor_tensor(mods[:, l, :, s], v[:, :, s], par[:, 2, l * 48:l * 48 + 48], ALU.add).then_inc(dve_step, 1)
                dve.wait_ge(dve_step, c.next(dve_step, 2))
                dve.sem_inc(ada_out, 1)
            dve.sem_inc(zone_free, 1)

            def modulation(l):
                for s in range(2):
                    for a in range(2):
                        M = [mods[:, l, (3 * a + i) * KT:(3 * a + i + 1) * KT, s] for i in range(3)]
                        g = [par[:, 1, 18 + (4 * l + 2 * a + i) * KT:18 + (4 * l + 2 * a + i + 1) * KT] for i in range(2)]
                        dve.scalar_tensor_tensor(out=cur2[:, s, 3 * a, :], in0=M[1], scalar=1.0, in1=g[0], op0=ALU.add,
                                                 op1=ALU.mult).then_inc(dve_step, 1)
                        dve.tensor_copy(cur2[:, s, 3 * a + 1, :], M[0]).then_inc(dve_step, 1)
                        dve.tensor_tensor(cur2[:, s, 3 * a + 2, :], M[2], g[1], ALU.mult).then_inc(dve_step, 1)
                dve.wait_ge(dve_step, c.next(dve_step, 12))

            modulation(0)
            dve.wait_ge(mask_in, c.next(mask_in, 64))
            for k in range(2):
                dve.tensor_tensor_reduce(lamv[:, 2 * k, :], lamv[:, 2 * k, :], lamv[:, 2 * k + 1, :], 1.0, 0.0, ALU.mult,
                                         ALU.add, small[:, 44 + k:45 + k]).then_inc(dve_step, 1)
            dve.wait_ge(dve_step, c.next(dve_step, 2))
            dve.sem_inc(lam_in, 1)
            dve.wait_ge(lam_out, 1)
            step(dve.tensor_tensor(small[:, 40:41], small[:, 47:48], small[:, 46:47], ALU.subtract))
            step(dve.tensor_scalar(small[:, 40:41], small[:, 40:41], -LAM_INIT, None, ALU.add))
            step(dve.tensor_scalar(subg[:, :], subg[:, :], 1.0 - LAM_INIT, None, ALU.mult))
            dve_prenorm(dve, c, segs_2(0))
            dve_tiles(dve, c, tile_kg())

            def heads_ab(e, t):
                for h in range(2):
                    e.tensor_scalar(small[:, SK + h:SK + h + 1], sink[:, bass.ds(t + 4 * h, 1)], 1.0, None, ALU.mult)\
                     .then_inc(dve_step, 1)
                e.wait_ge(dve_step, c.next(dve_step, 2))
                dve_tiles(e, c, tiles_ab())
                dve_attention(e, c, its_ab(t))
            turns(dve, c, 4, heads_ab)
            dve_features(dve, c, hh, hl, KT, 6)
            dve_linear_y(dve, c, TC, y2)
            dve_postnorm(dve, c, TC, y2, [(0, SEQ, G2(0, 2)), (SEQ, TC, G2(1, 2))])
            dve_prenorm(dve, c, segs_2(3))
            dve_ffn(dve, c, TC, y2, acth, actl, False)
            dve_postnorm(dve, c, TC, y2, [(0, SEQ, G2(0, 5)), (SEQ, TC, G2(1, 5))])
            dve.sem_inc(zone_free, 1)
            modulation(1)
            dve_prenorm(dve, c, segs_2(0))
            for j in range(5):
                T = SEQ if j < 3 else TC
                if j in (0, 3):
                    step(dve.memset(ysum[:, 0:T], 0.0))
                s = c.turn("slab")
                dve.wait_ge(slab_done, c.next(slab_done))
                step(dve.tensor_scalar(v3(lat[:, j, 0:T], T), p3(acc[s], T), 1.0, None, ALU.mult))
                dve.sem_inc(acc_free[s], 1)
                step(dve.tensor_tensor(sq[:, 0, 0:T], lat[:, j, 0:T], lat[:, j, 0:T], ALU.mult))
                step(dve.tensor_tensor(ysum[:, 0:T], ysum[:, 0:T], sq[:, 0, 0:T], ALU.add))
                if j in (2, 4):
                    dve.sem_inc(ysum_ready, 1)
                    dve_apply(dve, c, lat, lath, latl, range(3) if j < 3 else range(3, 5), segs_lat(T))
            dve.wait_ge(ctx_in, 112)
            dve_tiles(dve, c, tile_kr())
            dve.tensor_copy(kch[HD:PG, 1, :], kch[HD:PG, 0, :].bitcast(F32)).then_inc(kr_ready, 1)
            dve.tensor_tensor(kcl[HD:PG, 1, :], t2[HD:PG, 0, :], kch[HD:PG, 0, :].bitcast(F32), ALU.subtract)\
               .then_inc(kr_ready, 1)

            def heads_c(e, i):
                dve_tiles(e, c, tiles_c())
                dve_attention(e, c, its_c(i))
            turns(dve, c, 8, heads_c)
            dve_features(dve, c, o3h, o3l, KT, 4)
            dve_linear_y(dve, c, SEQ, y3)
            dve_postnorm(dve, c, SEQ, y3, [(0, SEQ, G2(0, 2))])
            dve_prenorm(dve, c, segs_2(3)[:1])
            dve_ffn(dve, c, SEQ, y1, act1h, act1l, False)
            dve_postnorm(dve, c, SEQ, y1, [(0, SEQ, G2(0, 5))])
            for r in range(4):
                dve.wait_ge(lt_done, c.next(lt_done))
                dve.tensor_copy(outb[:, r, :], acc[r % 2][:, :, :].rearrange("p b n -> p (b n)")).then_inc(lt_out, 1)


def constants():
    def swap(lo, hi, block, half):
        m = np.zeros((P, P), np.float32)
        for p in range(lo, hi):
            q = (p - lo) % block
            if q < half:
                m[p + half, p] = -1.0
            elif q < 2 * half:
                m[p - half, p] = 1.0
        return m

    out = {"ident": np.eye(P, dtype=np.float32), "ones": np.full((P, P), 1.0 / D, np.float32)}
    inv = np.zeros((P, 1), np.float32)
    f = (np.float32(500000.0) ** (-np.arange(0, 16, 2, dtype=np.float32) / np.float32(16))).astype(np.float32)
    for p in range(P):
        if p % HD < 16:
            inv[p] = f[p % HD % 8]
    out["inv1"], out["perm1"] = inv, swap(0, P, HD, 8)
    t = np.arange(SEQ)

    def axial(rows, dim, lo):
        ax = dim // 2
        f = (np.float32(10000.0) ** (-np.arange(0, ax, 2, dtype=np.float32) / np.float32(ax))).astype(np.float32)
        cos, sin = np.ones((P, SEQ), np.float32), np.zeros((P, SEQ), np.float32)
        for p in range(lo, rows):
            q = (p - lo) % dim
            where = (t // 64 if q < ax else t % 64).astype(np.float32)
            a = (where * f[q % (ax // 2)]).astype(np.float64)
            cos[p], sin[p] = np.cos(a), np.sin(a)
        return cos, sin

    out["cos_ab"], out["sin_ab"] = axial(P, HD, 0)
    out["cos_c"], out["sin_c"] = axial(PG, C_ROPE, HD)
    out["perm_ab"], out["perm_c"] = swap(0, P, 32, 16), swap(HD, PG, 16, 8)
    edge = np.zeros((P, 4, PAD), np.float32)
    for g, w in enumerate(POOL_W):
        edge[:, g, :] = 1.0 / np.minimum(np.arange(PAD) + 1, w)
    out["edge"] = edge
    i = np.arange(P)
    m1 = np.full((P, RES, TC), MASKED, np.float32)
    m2 = np.zeros((P, 4, TC), np.float32)
    for r in range(RES):
        q = RES * i[:, None] + r
        for r2 in range(RES):
            k = RES * i[None, :] + r2
            m1[:, r, r2 * P:r2 * P + P][(q - k >= 0) & (q - k <= 128)] = 0.0
        m1[:, r, 512:640][i[:, None] >= i[None, :]] = 0.0
        m1[:, r, 640:768][(i[:, None] >= i[None, :]) & ((i[:, None] - i[None, :]) % 4 == 0)] = 0.0
        q = P * r + i[:, None]
        m2[:, r, 0:SEQ][np.abs(q - t[None, :]) > 128] = MASKED
    half = mybir.dt.np(BF16)
    out["mask1"], out["mask2"] = m1.astype(half), m2.astype(half)
    return out


def kernel(**inputs):
    import concourse.bacc as _bacc
    from concourse.bass_utils import run_bass_kernel_spmd as _run

    nc = _bacc.Bacc("TRN2", target_bir_lowering=False, num_devices=1)
    arrays, A = {}, {}
    for name, a in {**inputs, **constants()}.items():
        a = np.ascontiguousarray(a)
        arrays[f"in_{name}"] = a
        A[name] = nc.dram_tensor(f"in_{name}", a.shape, mybir.dt.from_np(a.dtype), kind="ExternalInput").ap()
    out = nc.dram_tensor("out", (1, SEQ, D), F32, kind="ExternalOutput").ap()
    two_blocks(nc, A, out)
    return _run(nc, [arrays], core_ids=[0]).results[0]["out"]
```

```python
from contextlib import ExitStack

import numpy as np

import concourse.bass as bass
from concourse import mybir

ALU = mybir.AluOpType
ACT = mybir.ActivationFunctionType
F32 = mybir.dt.float32
F32R = mybir.dt.float32r
BF16 = mybir.dt.bfloat16
I32 = mybir.dt.int32
AX_X = mybir.AxisListType.X

P = 128
D = 1024
KT = D // P
SEQ = 512
CTX = 256
TC = SEQ + CTX
DEPTH = 2
FF = 2816
FT = FF // P
FF_PARTS = ((0, 8), (8, 8), (16, 6))
POOL_W = (2, 4, 8, 16)
PG = 96
CW = 384
CT = CW // P
HD = 64
AW = 768
Q1 = 4 * CW
K1 = Q1 + AW
V1 = K1 + AW
G1 = V1 + AW
RES = 4
MW = 512
EPS = 1e-6
PAD = 16
C_HEADS, C_QL, C_KVL, C_ROPE = 16, 384, 256, 32
AC = 256
MH = 4
LAM_INIT = 0.8 - 0.6
MASKED = -1e30
TWO_PI = 6.283185307179586
NORMS = ("norm_mix_pre", "norm_mix_post", "norm_mem_pre", "norm_mem_post", "norm_memkv", "norm_ffn_pre",
         "norm_ffn_post")
PAR_ROWS = (112, 103, 96, 66, 66, 8)
N_LOADS = 25
CW1 = 6.28125
CW2 = 0.0019350051879882812
CW3 = TWO_PI - CW1 - CW2
ROUND = 12582912.0


class Counts:

    def __init__(self):
        self.here, self.outer = {}, {}

    def start(self, sem, value, view=""):
        self.here[(sem.name, view)] = value

    def next(self, sem, k=1, view=""):
        key = (sem.name, view)
        self.here[key] = self.here.get(key, 0) + k
        return self.outer.get(key, 0) + self.here[key]

    def turn(self, what):
        n = self.here.get(what, 0)
        self.here[what] = n + 1
        return n % 2


class Silent:

    def __getattr__(self, _):
        return lambda *a, **k: self


def turns(e, c, n, body):
    start = dict(c.here)
    body(Silent(), 0)
    per = {k: v - start.get(k, 0) for k, v in c.here.items()}
    if not isinstance(e, Silent):
        outer = dict(c.outer)
        c.here = dict(start)
        with e.Fori(0, n) as i:
            for k, v in per.items():
                if v and isinstance(k, tuple):
                    c.outer[k] = c.outer.get(k, 0) + i * v
            body(e, i)
        c.outer = outer
    assert all(v % 2 == 0 for k, v in per.items() if isinstance(k, str))
    c.here = {k: start.get(k, 0) + n * v for k, v in per.items()}


def two_blocks(nc, A, out):
    with ExitStack() as ctx:
        low = 16512
        high = 229368

        class Region:
            def __init__(self, at, end):
                self.at, self.end = at, end

            def __call__(self, name, shape, dt=F32):
                n = int(np.prod(shape[1:])) * (2 if dt == BF16 else 4)
                t = nc.alloc_sbuf_tensor_at(name, shape, dt, offset=self.at)
                self.at += -(-n // 32) * 32
                assert self.at <= self.end, (name, self.at, self.end)
                return t

        keep = Region(low, high)
        xres = keep("xres", [P, KT, TC])
        wraw = keep("wraw", [P, 2, 9, P])
        whi = keep("whi", [P, 2, 9, P], F32R)
        wlo = keep("wlo", [P, 2, 9, P], F32R)
        par = keep("par", [P, 6, P])
        cur = keep("cur", [P, 136])
        cur2 = keep("cur2", [P, 2, 6, KT])
        rope_c = keep("rope_c", [P, SEQ])
        rope_s = keep("rope_s", [P, SEQ])
        perm = keep("perm", [P, P])
        ones = keep("ones", [P, P])
        ident = keep("ident", [P, P])
        edge = keep("edge", [P, 5, PAD])
        small = keep("small", [P, 64])
        scT = keep("scT", [P, KT, 2])
        mods = keep("mods", [P, DEPTH * 6 * KT * 2])
        rstd = keep("rstd", [P, TC])
        t2 = keep("t2", [P, 2, TC])
        sq = keep("sq", [P, 2, TC])
        ysum = keep("ysum", [P, TC])
        hh = keep("hh", [P, KT, TC], F32R)
        hl = keep("hl", [P, KT, TC], F32R)
        zone = keep.at

        z = Region(zone, high)
        xin = z("xin", [P, 4, D])
        min_ = z("min", [P, 2, D])
        prow = z("prow", [P, 6, P])
        angi = z("angi", [P, SEQ], I32)
        ang = z("ang", [P, SEQ])
        turn_n = z("turn_n", [P, SEQ])
        red = z("red", [P, SEQ])
        inv1 = z("inv1", [P, 1])
        z = Region(zone, high)
        bih = z("bih", [P, 9, SEQ], F32R)
        bil = z("bil", [P, 9, SEQ], F32R)
        mask1 = z("mask1", [P, RES, TC], BF16)
        qkv_at = z.at
        qh = z("qh", [P, 3, SEQ], F32R)
        ql = z("ql", [P, 3, SEQ], F32R)
        kh = z("kh", [P, 3, SEQ], F32R)
        kl = z("kl", [P, 3, SEQ], F32R)
        vt = z("vt", [P, 3, RES, P])
        ot1 = z("ot1", [P, RES, 256])
        z = Region(qkv_at, high)
        mgh = z("mgh", [P, KT, SEQ], F32R)
        mgl = z("mgl", [P, KT, SEQ], F32R)
        z = Region(qkv_at, high)
        ub = z("ub", [P, 2, PAD + SEQ])
        sa = z("sa", [P, 2, PAD + SEQ])
        poh = z("poh", [P, 4, SEQ], F32R)
        pol = z("pol", [P, 4, SEQ], F32R)
        zc = z("zc", [P, 2, PAD + SEQ])
        bxs = z("bxs", [P, 2, SEQ])
        z = Region(zone, high)
        y1 = z("y1", [P, KT, SEQ])
        qmh = z("qmh", [P, 4, SEQ], F32R)
        qml = z("qml", [P, 4, SEQ], F32R)
        kmh = z("kmh", [P, 4, CTX], F32R)
        kml = z("kml", [P, 4, CTX], F32R)
        vm = z("vm", [P, 4, 2, P])
        otm = z("otm", [P, 4, MW])
        ofh = z("ofh", [P, 4, SEQ], F32R)
        ofl = z("ofl", [P, 4, SEQ], F32R)
        z = Region(zone, high)
        y2 = z("y2", [P, KT, TC])
        acth = z("acth", [P, 8, TC], F32R)
        actl = z("actl", [P, 8, TC], F32R)
        z = Region(zone + 4 * KT * SEQ, high)
        act1h = z("act1h", [P, 8, SEQ], F32R)
        act1l = z("act1l", [P, 8, SEQ], F32R)
        zf = z("zf", [P, 2, PAD + SEQ])
        adaw = z("adaw", [P, KT, AC])
        adap = z("adap", [P, 2, 2, AC])
        cin = z("cin", [P, CTX // P, D])
        z = Region(zone, high)
        kgh = z("kgh", [P, TC], F32R)
        kgl = z("kgl", [P, TC], F32R)
        vg = z("vg", [P, 6, P])
        qgh = z("qgh", [P, TC], F32R)
        qgl = z("qgl", [P, TC], F32R)
        qdh = z("qdh", [P, TC], F32R)
        qdl = z("qdl", [P, TC], F32R)
        kdh = z("kdh", [P, TC], F32R)
        kdl = z("kdl", [P, TC], F32R)
        vd = z("vd", [P, 6, P])
        mask2 = z("mask2", [P, 4, TC], BF16)
        ot2 = z("ot2", [P, 6, D])
        sink = z("sink", [P, 8])
        subg = z("subg", [P, P])
        lamv = z("lamv", [P, 4, HD])
        o1 = z("o1", [P, 2, P])
        o2 = z("o2", [P, P])
        hss = z("hss", [P, 4 * 6])
        z = Region(zone, high)
        lat = z("lat", [P, 5, TC])
        lath = z("lath", [P, 5, TC], F32R)
        latl = z("latl", [P, 5, TC], F32R)
        kch = z("kch", [P, MH, TC], F32R)
        kcl = z("kcl", [P, MH, TC], F32R)
        vc = z("vc", [P, MH, 6, HD])
        z = Region(zone - 2 * 4 * KT * TC, zone)
        ot3 = z("ot3", [P, 4, D])
        qch = z("qch", [P, MH, SEQ], F32R)
        qcl = z("qcl", [P, MH, SEQ], F32R)
        z = Region(zone, high)
        o3h = z("o3h", [P, KT, SEQ], F32R)
        o3l = z("o3l", [P, KT, SEQ], F32R)
        z = Region(zone - 2 * 4 * KT * TC, zone)
        y3 = z("y3", [P, KT, SEQ])
        z = Region(zone, high)
        outb = z("outb", [P, 4, D])

        acc = [ctx.enter_context(nc.psum_tensor(f"acc{i}", [P, 2, 512], F32)) for i in range(2)]
        pt = ctx.enter_context(nc.psum_tensor("pt", [P, 2, 512], F32))
        ob = [ctx.enter_context(nc.psum_tensor(f"ob{i}", [P, 512], F32)) for i in range(2)]

        GATE = [sq[:, 0, 0:SEQ], sq[:, 1, 0:SEQ], ysum[:, 0:SEQ]]
        PROD = [t2[:, 0, 0:SEQ], t2[:, 1, 0:SEQ], rstd[:, 0:SEQ]]

        def gain(n):
            return lambda k: cur[:, n + k:n + k + 1]

        def G2(s, i):
            return lambda k: cur2[:, s, i, k:k + 1]

        def segs_a():
            return [(0, SEQ, gain(0), None), (SEQ, TC, gain(32), None)]

        def segs_m():
            return [(0, SEQ, gain(16), None)]

        def segs_f():
            return [(0, SEQ, gain(40), None)]

        def segs_2(base):
            return [(0, SEQ, G2(0, base), G2(0, base + 1)), (SEQ, TC, G2(1, base), G2(1, base + 1))]

        def segs_lat(T):
            return [(0, T, lambda k: par[:, 1, 98 + k:99 + k], None)]

        def sem(name):
            return ctx.enter_context(nc.semaphore(name))

        loaded = sem("loaded")
        mask_in = sem("mask_in")
        ctx_in = sem("ctx_in")
        cin_in = sem("cin_in")
        zone_free = sem("zone_free")
        stored = sem("stored")
        landed = [sem(f"slab_landed{i}") for i in range(2)]
        hi_ready = sem("slab_hi_ready")
        lo_ready = sem("slab_lo_ready")
        slab_done = sem("slab_done")
        acc_free = [sem(f"acc_free{i}") for i in range(2)]
        pt_free = sem("pt_free")
        act_step, dve_step = sem("act_step"), sem("dve_step")
        set_done = sem("setup_done")
        lt_done = sem("load_transposed")
        lt_out = sem("load_copied")
        x_ready = sem("x_ready")
        sq_ready = sem("sq_ready")
        sq_used = sem("sq_used")
        rstd_ready = sem("rstd_ready")
        t_ready = sem("t_ready")
        h_hi = sem("h_hi")
        h_ready = sem("h_ready")
        ysum_ready = sem("ysum_ready")
        ystat_done = sem("ystat_done")
        raw_ready = sem("raw_ready")
        post_done = sem("post_done")
        sum_ready = sem("sum_ready")
        tile_hi = sem("tile_hi")
        tile_ready = sem("tile_ready")
        pool_hi = sem("pool_hi")
        pool_ready = sem("pool_ready")
        bi_hi = sem("bi_hi")
        bi_ready = sem("bi_ready")
        gate_ready = sem("gate_ready")
        merged_ready = sem("merged_ready")
        conv_ready = sem("conv_ready")
        silu_ready = sem("silu_ready")
        act_ready = sem("act_ready")
        scores_done = sem("scores_done")
        nb_ready = sem("nb_ready")
        sink_ready = sem("sink_ready")
        probs_ready = sem("probs_ready")
        tr_done = sem("tr_done")
        pt_copied = sem("pt_copied")
        map_ready, comb_ready, heads_normed = sem("map_ready"), sem("comb_ready"), sem("heads_normed")
        pv_done = sem("pv_done")
        ob_free = [sem(f"ob_free{i}") for i in range(2)]
        feat_done, feat_hi, feat_ready = sem("feat_done"), sem("feat_hi"), sem("feat_ready")
        ada_in = [sem(f"ada_in{i}") for i in range(2)]
        ada_used = sem("ada_used")
        ada_sums, ada_done = sem("ada_sums"), sem("ada_done")
        ss_ready, subn_ready = sem("ss_ready"), sem("subn_ready")
        tables_ready, cond_ready = sem("tables_ready"), sem("cond_ready")
        lam_in, lam_out, kr_ready = sem("lam_in"), sem("lam_out"), sem("kr_ready")
        in_ready, up_ready = sem("in_ready"), sem("up_ready")
        gates_used = sem("gates_used")

        pe_past, dve_past = sem("pe_past"), sem("dve_past")

        def past(e, s):
            e.sem_inc(s, 1)

        def nb(T):
            return (1, T) if T <= 512 else (2, T // 2)

        def v3(ap, T):
            return ap.rearrange("p (b n) -> p b n", b=nb(T)[0])

        def p3(ps, T, M=P):
            b, n = nb(T)
            return ps[0:M, 0:b, 0:n]

        def load(e, c, parts, width=P):
            s = c.turn("slab")
            e.wait_ge(lo_ready, c.next(lo_ready))
            for k0, rows, src in parts:
                n = src.shape[1]
                e.dma_start(wraw[0:rows, s, k0:k0 + n, 0:width], src).then_inc(landed[s], 16)

        def rows_of(W, l, k0, n, col, width=P, rows=P):
            w = W[bass.ds(l, 1), k0:k0 + n * rows, bass.ds(col, width)]
            return w.rearrange("o (k p) m -> p (o k) m", p=rows)

        def head(e, c, kt, dmas=1):
            s = c.turn("slab")
            e.wait_ge(landed[s], c.next(landed[s], 16 * dmas))
            e.wait_ge(slab_done, c.next(slab_done, view="slot"))
            e.activation(whi[:, s, 0:kt, :], wraw[:, s, 0:kt, :], ACT.Copy).then_inc(hi_ready, 1)

        def tail(e, c, kt):
            s = c.turn("slab")
            e.wait_ge(hi_ready, c.next(hi_ready))
            e.tensor_tensor(wlo[:, s, 0:kt, :], wraw[:, s, 0:kt, :],
                            whi[:, s, 0:kt, :].bitcast(F32), ALU.subtract).then_inc(lo_ready, 1)

        def passed(c):
            c.turn("acc")
            c.next(slab_done)

        def mm3(e, o, wh, wl, xh, xl, first, last):
            e.matmul(o, wh, xh, start=first, stop=False)
            e.matmul(o, wh, xl, start=False, stop=False)
            return e.matmul(o, wl, xh, start=False, stop=last)

        def slab(e, c, T, xh, xl, kts, M=P, fresh=0, free=True, c0=0, w0=0):
            s = c.turn("slab")
            e.wait_ge(lo_ready, c.next(lo_ready))
            if free:
                e.wait_ge(acc_free[s], c.next(acc_free[s]))
            b, n = nb(T)
            for j, (k, xk, rows) in enumerate(kts):
                if fresh:
                    e.wait_ge(h_ready, c.next(h_ready, fresh))
                for i in range(b):
                    cols = slice(c0 + i * n, c0 + i * n + n)
                    mm = mm3(e, acc[s][0:M, i, 0:n], whi[0:rows, s, k, w0:w0 + M], wlo[0:rows, s, k, w0:w0 + M],
                             xh[0:rows, xk, cols], xl[0:rows, xk, cols], j == 0, j == len(kts) - 1)
            mm.then_inc(slab_done, 1)
            return s

        K8 = [(k, k, P) for k in range(KT)]

        def take(e, c, sems):
            for s in sems:
                e.wait_ge(s, c.next(s))

        def give(e, sems):
            for s in sems:
                e.sem_inc(s, 1)

        def pe_stats(e, c, T):
            b, n = nb(T)
            e.wait_ge(pt_free, c.next(pt_free))
            for k in range(KT):
                e.wait_ge(sq_ready, c.next(sq_ready))
                for i in range(b):
                    mm = e.matmul(pt[:, i, 0:n], ones[:, :], sq[:, k % 2, i * n:i * n + n],
                                  start=k == 0, stop=k == KT - 1)
                mm.then_inc(sq_used, 1)

        def act_rstd(e, c, T, scale=1.0):
            e.activation(v3(rstd[:, 0:T], T), p3(pt, T), ACT.Ln, bias=small[:, 63:64], scale=scale)\
             .then_inc(act_step, 1)
            e.wait_ge(act_step, c.next(act_step))
            e.sem_inc(pt_free, 1)
            e.activation(rstd[:, 0:T], rstd[:, 0:T], ACT.Exp, scale=-0.5).then_inc(rstd_ready, 1)

        def act_prenorm(e, c, T, segs):
            for k in range(KT):
                e.wait_ge(x_ready, c.next(x_ready))
                e.wait_ge(sq_used, c.next(sq_used))
                e.activation(sq[:, k % 2, 0:T], xres[:, k, 0:T], ACT.Square).then_inc(sq_ready, 1)
            e.wait_ge(sq_used, c.next(sq_used, KT, view="all"))
            act_rstd(e, c, T)
            act_apply(e, c, hh, range(KT), segs)

        def act_apply(e, c, hi, tiles, segs):
            for k in tiles:
                for a, b, _, B in segs:
                    e.wait_ge(t_ready, c.next(t_ready))
                    if B is None:
                        e.activation(hi[:, k, a:b], t2[:, k % 2, a:b], ACT.Copy).then_inc(h_hi, 1)
                    else:
                        e.activation(hi[:, k, a:b], t2[:, k % 2, a:b], ACT.Identity, bias=B(k)).then_inc(h_hi, 1)

        def dve_apply(e, c, src, hi, lo, tiles, segs):
            e.wait_ge(rstd_ready, c.next(rstd_ready))
            tiles = list(tiles)

            def scaled(k):
                for a, b, Acol, _ in segs:
                    e.scalar_tensor_tensor(out=t2[:, k % 2, a:b], in0=src[:, k, a:b], scalar=Acol(k),
                                           in1=rstd[:, a:b], op0=ALU.mult, op1=ALU.mult).then_inc(t_ready, 1)

            scaled(tiles[0])
            for k in tiles:
                if k + 1 in tiles:
                    if k > tiles[0]:
                        e.wait_ge(h_ready, c.next(h_ready, len(segs)))
                    scaled(k + 1)
                for a, b, _, B in segs:
                    e.wait_ge(h_hi, c.next(h_hi))
                    if B is None:
                        e.tensor_tensor(lo[:, k, a:b], t2[:, k % 2, a:b], hi[:, k, a:b].bitcast(F32),
                                        ALU.subtract).then_inc(h_ready, 1)
                    else:
                        e.scalar_tensor_tensor(out=lo[:, k, a:b], in0=t2[:, k % 2, a:b], scalar=B(k),
                                               in1=hi[:, k, a:b].bitcast(F32), op0=ALU.add,
                                               op1=ALU.subtract).then_inc(h_ready, 1)
            e.wait_ge(h_ready, c.next(h_ready, 2 * len(segs)))

        def dve_prenorm(e, c, segs):
            dve_apply(e, c, xres, hh, hl, range(KT), segs)

        def pe_linear_y(e, c, T, xh, xl, kt, unit=False):
            kts = [(k, k, P) for k in range(kt)]

            def body(e, i):
                for _ in range(2):
                    slab(e, c, T, xh, xl, kts)
                if unit:
                    pe_unit(e, c, 0)
            turns(e, c, KT // 2, body)

        def act_linear_y(e, c, kt):
            def body(e, i):
                for _ in range(2):
                    head(e, c, kt)
                    passed(c)
            turns(e, c, KT // 2, body)

        def dve_linear_y(e, c, T, y, first=True, last=True, unit=None):
            if last:
                e.memset(ysum[:, 0:T], 0.0).then_inc(dve_step, 1)
                e.wait_ge(dve_step, c.next(dve_step))
                past(e, dve_past)

            def body(e, i):
                for j in range(2):
                    if unit:
                        dve_unit(e, c, 0, j)
                    s = c.turn("slab")
                    ym = y[:, bass.ds(2 * i + j, 1), :].rearrange("p o (b n) -> p (o b) n", b=nb(T)[0])
                    e.wait_ge(slab_done, c.next(slab_done))
                    if first:
                        e.tensor_scalar(ym, p3(acc[s], T), 1.0, None, ALU.mult).then_inc(dve_step, 1)
                    else:
                        e.tensor_tensor(ym, p3(acc[s], T), ym, ALU.add).then_inc(dve_step, 1)
                    e.wait_ge(dve_step, c.next(dve_step))
                    e.sem_inc(acc_free[s], 1)
                    if last:
                        e.tensor_tensor(v3(sq[:, j, 0:T], T), ym, ym, ALU.mult).then_inc(dve_step, 1)
                        e.wait_ge(dve_step, c.next(dve_step))
                        e.tensor_tensor(ysum[:, 0:T], ysum[:, 0:T], sq[:, j, 0:T], ALU.add).then_inc(dve_step, 1)
                        e.wait_ge(dve_step, c.next(dve_step))
                if unit:
                    dve_unit_out(e, c, 0, unit[0], i + unit[1])
            turns(e, c, KT // 2, body)
            if last:
                e.sem_inc(ysum_ready, 1)

        def pe_postnorm(e, c, T):
            b, n = nb(T)
            e.wait_ge(pt_free, c.next(pt_free))
            e.wait_ge(ysum_ready, c.next(ysum_ready))
            for i in range(b):
                mm = e.matmul(pt[:, i, 0:n], ones[:, :], ysum[:, i * n:i * n + n], start=True, stop=True)
            mm.then_inc(ystat_done, 1)

        def act_postnorm(e, c, T):
            e.wait_ge(ystat_done, c.next(ystat_done))
            act_rstd(e, c, T)

        def dve_postnorm(e, c, T, y, segs):
            e.wait_ge(rstd_ready, c.next(rstd_ready))

            def scaled(k):
                for a, b, G in segs:
                    e.scalar_tensor_tensor(out=t2[:, k % 2, a:b], in0=y[:, k, a:b], scalar=G(k),
                                           in1=rstd[:, a:b], op0=ALU.mult, op1=ALU.mult).then_inc(dve_step, 1)

            scaled(0)
            for k in range(KT):
                e.wait_ge(dve_step, c.next(dve_step, len(segs)))
                if k + 1 < KT:
                    if k:
                        e.wait_ge(x_ready, c.next(x_ready))
                    scaled(k + 1)
                e.tensor_tensor(xres[:, k, 0:T], xres[:, k, 0:T], t2[:, k % 2, 0:T], ALU.add).then_inc(x_ready, 1)
            e.wait_ge(x_ready, c.next(x_ready, 2))

        def pe_tiles(e, c, tiles, kts, xh, xl, fresh=0, tail_w=None):
            take(e, c, acc_free + [pt_free] + ob_free)

            def post(j):
                t = tiles[j]
                e.wait_ge(raw_ready, c.next(raw_ready))
                if t["kind"] == "plain":
                    return
                if t["kind"] == "rope":
                    M = t["M"]
                    e.matmul(ob[j % 2][0:M, 0:SEQ], perm[0:M, 0:M], t2raw(j)[0:M, 0:SEQ], start=True,
                             stop=True).then_inc(post_done, 1)
                else:
                    n, r0 = t["n"], t["r0"]
                    past(e, pe_past)
                    for i, cols in enumerate(t["tok"]):
                        tr = e.transpose(pt[:, i * n // 512, i * n % 512:i * n % 512 + n],
                                         t2raw(j)[r0:r0 + n, cols], ident[r0:r0 + n, r0:r0 + n])
                    tr.then_inc(post_done, 1)

            out, last_v = 0, -1
            for j in range(len(tiles) + 1):
                if j < len(tiles):
                    t = tiles[j]
                    slab(e, c, t["T"], t.get("xh", xh), t.get("xl", xl), t.get("kts", kts), M=t["M"],
                         fresh=fresh if j == 0 else 0, free=False, c0=t.get("c0", 0))
                if j:
                    if tiles[j - 1]["kind"] in ("v", "kv"):
                        need, last_v = last_v + 1, j - 1
                        if need > out:
                            e.wait_ge(tile_ready, c.next(tile_ready, need - out))
                            out = need
                    post(j - 1)
            e.wait_ge(tile_ready, c.next(tile_ready, len(tiles) - out))
            give(e, acc_free + [pt_free] + ob_free)

        def t2raw(j):
            return sq[:, j % 2, :]

        def act_tiles(e, c, tiles, heads):
            N, bank = len(tiles), []
            for j in range(N + 2):
                if j < N:
                    head(e, c, *heads[j])
                    bank.append(c.turn("acc"))
                    done = c.next(slab_done)
                if 1 <= j <= N:
                    t = tiles[j - 1]
                    T, M = t["T"], t["M"]
                    e.wait_ge(slab_done, done if j == N else done - 1)
                    if j >= 3:
                        e.wait_ge(tile_ready, c.next(tile_ready))
                    e.activation(v3(t2raw(j - 1)[0:M, 0:T], T), p3(acc[bank[j - 1]], T, M), ACT.Copy)\
                     .then_inc(raw_ready, 1)
                if j >= 2 and tiles[j - 2]["kind"] != "v":
                    t = tiles[j - 2]
                    e.wait_ge(sum_ready, c.next(sum_ready))
                    e.activation(t["hi"], t.get("arrange", same)(t2[0:t["R"], j % 2, 0:t["T"]]), ACT.Copy)\
                     .then_inc(tile_hi, 1)
            c.next(tile_ready, min(2, N))

        def dve_tiles(e, c, tiles):
            for j in range(len(tiles) + 1):
                if j < len(tiles) and tiles[j]["kind"] != "v":
                    dve_sum(e, c, tiles[j], j)
                if j and tiles[j - 1]["kind"] != "v":
                    t = tiles[j - 1]
                    w = t2[0:t["R"], (j - 1) % 2, 0:t["T"]]
                    e.wait_ge(tile_hi, c.next(tile_hi))
                    e.tensor_tensor(t["lo"], t.get("arrange", same)(w), t["hi"].bitcast(F32), ALU.subtract)\
                     .then_inc(tile_ready, 1)
                if j < len(tiles) and tiles[j]["kind"] == "v":
                    e.wait_ge(raw_ready, c.next(raw_ready))
                    dve_values(e, c, tiles[j])
                    e.sem_inc(tile_ready, 1)
                if j < len(tiles):
                    c.turn("slab")
                    c.next(slab_done)

        def dve_sum(e, c, t, j):
            T, M = t["T"], t["M"]
            raw, w = t2raw(j), t2[0:t["R"], j % 2, :]
            e.wait_ge(raw_ready, c.next(raw_ready))
            if t["kind"] == "rope":
                turned_part = (ysum, rstd)[j % 2][0:M, 0:SEQ]
                e.tensor_tensor(w[:, 0:SEQ], raw[0:M, 0:SEQ], rope_c[0:M, :], ALU.mult).then_inc(dve_step, 1)
                if T > SEQ:
                    e.tensor_copy(w[:, SEQ:T], raw[0:M, SEQ:T]).then_inc(dve_step, 1)
                e.wait_ge(post_done, c.next(post_done))
                e.tensor_tensor(turned_part, ob[j % 2][0:M, 0:SEQ], rope_s[0:M, :], ALU.mult).then_inc(dve_step, 1)
                e.wait_ge(dve_step, c.next(dve_step, 3 if T > SEQ else 2))
                e.tensor_tensor(w[:, 0:SEQ], w[:, 0:SEQ], turned_part, ALU.add).then_inc(sum_ready, 1)
            else:
                e.tensor_copy(w[:, 0:T], raw[0:t["R"], 0:T]).then_inc(sum_ready, 1)
                if t["kind"] == "kv":
                    dve_values(e, c, t)

        def dve_values(e, c, t):
            e.wait_ge(post_done, c.next(post_done))
            n, cnt = t["n"], len(t["tok"])
            fit = min(cnt, 512 // n)
            e.tensor_copy(t["v"][:, 0:fit, :], pt[:, 0, 0:fit * n].rearrange("p (t d) -> p t d", d=n)).then_inc(dve_step, 1)
            if cnt > fit:
                e.tensor_copy(t["v"][:, fit:cnt, :], pt[:, 1, 0:(cnt - fit) * n].rearrange("p (t d) -> p t d", d=n))\
                 .then_inc(dve_step, 1)
            e.wait_ge(dve_step, c.next(dve_step, 1 + (cnt > fit)))

        def same(ap):
            return ap

        def pe_attention(e, c, its):
            N = len(its)
            take(e, c, acc_free + [pt_free])
            for n in range(N + 2):
                if n < N:
                    t = its[n]
                    S = acc[n % 2][:, :, :].rearrange("p b n -> p (b n)")
                    for q_hi, q_lo, k_hi, k_lo, c0 in t["keys"]:
                        mm = mm3(e, S[:, c0:c0 + k_hi.shape[-1]], q_hi, q_lo, k_hi, k_lo, True, True)
                    mm.then_inc(scores_done, 1)
                if n >= 2:
                    e.wait_ge(pt_copied, c.next(pt_copied))
                if 1 <= n <= N:
                    t, s = its[n - 1], (n - 1) % 2
                    e.wait_ge(probs_ready, c.next(probs_ready))
                    for j in range(len(t["v"])):
                        tr = e.transpose(pt[:, j // 3, j % 3 * P:j % 3 * P + P], t2[:, s, j * P:j * P + P], ident[:, :])
                    tr.then_inc(tr_done, 1)
                if n >= 2:
                    t, s = its[n - 2], n % 2
                    e.wait_ge(ob_free[s], c.next(ob_free[s]))
                    for j, vj in enumerate(t["v"]):
                        mm = e.matmul(ob[s][:, 0:t["dv"]], sq[:, s, j * P:j * P + P], vj,
                                      start=j == 0, stop=j == len(t["v"]) - 1)
                    mm.then_inc(pv_done, 1)
            take(e, c, ob_free)
            give(e, acc_free + [pt_free] + ob_free)

        MX, NB, DEN, RD, ES, SK, CF, SS = 0, 4, 8, 12, 16, 20, 24, 28

        def pt_copy(s, nv):
            if nv <= 3:
                return sq[:, s, 0:nv * P], pt[:, 0, 0:nv * P]
            return sq[:, s, 0:nv * P].rearrange("p (b n) -> p b n", b=2), pt[:, :, 0:nv * P // 2]

        def act_attention(e, c, its):
            N = len(its)
            for n in range(N + 2):
                if n < N:
                    t, s = its[n], n % 2
                    w, c0 = len(t["v"]) * P, t["c0"]
                    e.wait_ge(nb_ready, c.next(nb_ready))
                    e.wait_ge(tr_done, c.next(tr_done, view="slot"))
                    S = acc[s][:, :, :].rearrange("p b n -> p (b n)")[:, c0:c0 + w]
                    src = t2[:, s, 0:w] if t["mask"] is not None else S
                    if t["sink"] is not None:
                        e.activation(small[:, ES + n % 4:ES + n % 4 + 1], small[:, SK + t["sink"]:SK + t["sink"] + 1],
                                     ACT.Exp, bias=small[:, NB + n % 4:NB + n % 4 + 1]).then_inc(sink_ready, 1)
                    e.activation(t2[:, s, 0:w], src, ACT.Exp, bias=small[:, NB + n % 4:NB + n % 4 + 1],
                                 scale=t["scale"], accum_out=small[:, DEN + n % 4:DEN + n % 4 + 1])\
                     .then_inc(probs_ready, 1)
                if 1 <= n <= N:
                    t, s = its[n - 1], (n - 1) % 2
                    e.wait_ge(tr_done, c.next(tr_done))
                    e.wait_ge(pv_done, c.next(pv_done, view="slot"))
                    e.activation(*pt_copy(s, len(t["v"])), ACT.Copy).then_inc(pt_copied, 1)

        def dve_attention(e, c, its):
            N = len(its)

            def col(k, n):
                return small[:, k + n % 4:k + n % 4 + 1]

            for n in range(N + 2):
                if n < N:
                    t, s = its[n], n % 2
                    w, c0 = len(t["v"]) * P, t["c0"]
                    S = acc[s][:, :, :].rearrange("p b n -> p (b n)")[:, c0:c0 + w]
                    e.wait_ge(scores_done, c.next(scores_done))
                    e.wait_ge(tr_done, c.next(tr_done, view="slot"))
                    if t["mask"] is not None:
                        past(e, dve_past)
                        e.tensor_tensor_reduce(t2[:, s, 0:w], S, t["mask"], 1.0, -3e38, ALU.add, ALU.max,
                                               col(MX, n)).then_inc(dve_step, 1)
                    else:
                        e.tensor_reduce(col(MX, n), S, AX_X, ALU.max).then_inc(dve_step, 1)
                    e.wait_ge(dve_step, c.next(dve_step))
                    if t["sink"] is not None:
                        k = SK + t["sink"]
                        e.scalar_tensor_tensor(out=col(MX, n), in0=small[:, k:k + 1], scalar=1.0 / t["scale"],
                                               in1=col(MX, n), op0=ALU.mult, op1=ALU.max).then_inc(dve_step, 1)
                        e.wait_ge(dve_step, c.next(dve_step))
                    e.tensor_scalar(col(NB, n), col(MX, n), -t["scale"], None, ALU.mult).then_inc(nb_ready, 1)
                if n >= 2:
                    t, s, m = its[n - 2], n % 2, n - 2
                    if t["sink"] is not None:
                        e.wait_ge(sink_ready, c.next(sink_ready))
                    e.wait_ge(pv_done, c.next(pv_done))
                    if t["sink"] is not None:
                        e.tensor_tensor(col(DEN, m), col(DEN, m), col(ES, m), ALU.add).then_inc(dve_step, 1)
                        e.wait_ge(dve_step, c.next(dve_step))
                    e.reciprocal(col(RD, m), col(DEN, m)).then_inc(dve_step, 1)
                    e.wait_ge(dve_step, c.next(dve_step))
                    O = ob[s][:, 0:t["dv"]]
                    e.tensor_scalar(t["dst"], O, col(RD, m), None, ALU.mult).then_inc(ob_free[s], 1)

        comb = [ysum, rstd]

        def pe_diff(e, c, its):
            N = len(its)
            take(e, c, acc_free + [pt_free])
            for n in range(N + 2):
                def scores(m):
                    if n:
                        e.wait_ge(map_ready, c.next(map_ready))
                    for q_hi, q_lo, k_hi, k_lo, c0 in its[n]["maps"][m]:
                        S = acc[m][:, :, :].rearrange("p b n -> p (b n)")
                        mm = mm3(e, S[:, c0:c0 + k_hi.shape[-1]], q_hi, q_lo, k_hi, k_lo, True, True)
                    mm.then_inc(scores_done, 1)
                if n < N:
                    scores(0)
                if n >= 2:
                    t, s = its[n - 2], n % 2
                    e.wait_ge(pt_copied, c.next(pt_copied))
                    e.wait_ge(ob_free[s], c.next(ob_free[s]))
                    for j, vj in enumerate(t["v"]):
                        mm = e.matmul(ob[s][:, 0:P], sq[:, s, j * P:j * P + P], vj, start=j == 0, stop=j == len(t["v"]) - 1)
                    mm.then_inc(pv_done, 1)
                if n < N:
                    scores(1)
                if 1 <= n <= N:
                    t = its[n - 1]
                    e.wait_ge(comb_ready, c.next(comb_ready))
                    for j in range(len(t["v"])):
                        tr = e.transpose(pt[:, j // 3, j % 3 * P:j % 3 * P + P], comb[(n - 1) % 2][:, j * P:j * P + P],
                                         ident[:, :])
                    tr.then_inc(tr_done, 1)
            c.next(map_ready, 2)
            take(e, c, ob_free)
            give(e, acc_free + [pt_free] + ob_free)

        def act_diff(e, c, its):
            N = len(its)
            for n in range(N + 1):
                def exps(m):
                    t, k = its[n], 2 * (n % 2) + m
                    w, c0 = len(t["v"]) * P, t["c0"]
                    e.wait_ge(nb_ready, c.next(nb_ready))
                    if n and m == 0:
                        e.wait_ge(comb_ready, c.next(comb_ready))
                    S = acc[m][:, :, :].rearrange("p b n -> p (b n)")[:, c0:c0 + w]
                    e.activation(t2[:, m, 0:w], S, ACT.Exp, bias=small[:, NB + k:NB + k + 1], scale=t["scale"],
                                 accum_out=small[:, DEN + k:DEN + k + 1]).then_inc(map_ready, 1)
                if n < N:
                    exps(0)
                if n:
                    e.wait_ge(tr_done, c.next(tr_done))
                    c.next(tr_done, view="slot")
                    e.wait_ge(pv_done, c.next(pv_done, view="slot"))
                    e.activation(*pt_copy((n - 1) % 2, len(its[n - 1]["v"])), ACT.Copy).then_inc(pt_copied, 1)
                if n < N:
                    exps(1)
            c.next(comb_ready)

        def dve_diff(e, c, its):
            N = len(its)

            def col(k, n):
                return small[:, k + n:k + n + 1]

            for n in range(N + 2):
                def maxima(m):
                    t, k = its[n], 2 * (n % 2) + m
                    S = acc[m][:, :, :].rearrange("p b n -> p (b n)")[:, t["c0"]:t["c0"] + len(t["v"]) * P]
                    e.wait_ge(scores_done, c.next(scores_done))
                    e.tensor_reduce(col(MX, k), S, AX_X, ALU.max).then_inc(dve_step, 1)
                    e.wait_ge(dve_step, c.next(dve_step))
                    e.tensor_scalar(col(NB, k), col(MX, k), -t["scale"], None, ALU.mult).then_inc(nb_ready, 1)
                if n < N:
                    maxima(0)
                if 1 <= n <= N:
                    s, k = (n - 1) % 2, 2 * ((n - 1) % 2)
                    w = len(its[n - 1]["v"]) * P
                    e.wait_ge(map_ready, c.next(map_ready, 2))
                    e.reciprocal(col(RD, k), col(DEN, k)).then_inc(dve_step, 1)
                    e.reciprocal(col(RD, k + 1), col(DEN, k + 1)).then_inc(dve_step, 1)
                    e.wait_ge(dve_step, c.next(dve_step, 2))
                    e.tensor_scalar(col(CF, k), col(RD, k + 1), col(DEN, k), small[:, 40:41], ALU.mult, ALU.mult)\
                     .then_inc(dve_step, 1)
                    e.wait_ge(dve_step, c.next(dve_step))
                    e.wait_ge(tr_done, c.next(tr_done, view="slot"))
                    past(e, dve_past)
                    e.scalar_tensor_tensor(out=comb[s][:, 0:w], in0=t2[:, 1, 0:w], scalar=col(CF, k), in1=t2[:, 0, 0:w],
                                           op0=ALU.mult, op1=ALU.add).then_inc(comb_ready, 1)
                if n >= 2:
                    m, s = n - 2, n % 2
                    e.wait_ge(pv_done, c.next(pv_done))
                    e.tensor_scalar(o1[:, s, :], ob[s][:, 0:P], col(RD, 2 * s), None, ALU.mult).then_inc(dve_step, 1)
                    e.wait_ge(dve_step, c.next(dve_step))
                    e.sem_inc(ob_free[s], 1)
                    e.tensor_tensor_reduce(o2[:, :], o1[:, s, :], o1[:, s, :], 1.0, 0.0, ALU.mult, ALU.add,
                                           col(SS, m)).then_inc(dve_step, 1)
                    e.tensor_scalar(its[m]["dst"], o1[:, s, :], 1.0, None, ALU.mult).then_inc(dve_step, 1)
                    e.wait_ge(dve_step, c.next(dve_step, 2))
                if n < N:
                    maxima(1)
            e.wait_ge(comb_ready, c.next(comb_ready, N))

        def pe_features(e, c, src, nf, nt, normed=KT):
            take(e, c, [pt_free])
            for f in range(nf):
                if f >= normed:
                    e.wait_ge(heads_normed, c.next(heads_normed, nt))
                if f >= (2 if nt == 4 else 1):
                    e.wait_ge(feat_ready, c.next(feat_ready))
                for r in range(nt):
                    o = pt[:, f % 2, r * P:r * P + P] if nt == 4 else pt[:, r // 3, r % 3 * P:r % 3 * P + P]
                    tr = e.transpose(o, src[:, r, f * P:f * P + P], ident[:, :])
                tr.then_inc(feat_done, 1)
            e.wait_ge(feat_ready, c.next(feat_ready, 2 if nt == 4 else 1))
            give(e, [pt_free])

        def act_features(e, c, hi, nf, nt, arrange=same):
            for f in range(nf):
                e.wait_ge(feat_done, c.next(feat_done))
                src = pt[:, f % 2, :] if nt == 4 else pt[:, :, 0:384]
                dst = hi[:, f, :] if nt == 4 else v3(hi[:, f, :], TC)
                e.activation(arrange(dst), (lambda a: a.rearrange("p (r i) -> p r i", r=4))(src) if arrange is not same else src,
                             ACT.Copy).then_inc(feat_hi, 1)

        def dve_features(e, c, hi, lo, nf, nt, arrange=same, normed=KT):
            for f in range(nf):
                if f + normed < nf:
                    for r in range(nt):
                        o = ot2[:, r, (normed + f) * P:(normed + f + 1) * P]
                        e.scalar_tensor_tensor(out=o, in0=o, scalar=hss[:, f * 6 + r:f * 6 + r + 1], in1=subg[:, :],
                                               op0=ALU.mult, op1=ALU.mult).then_inc(heads_normed, 1)
                e.wait_ge(feat_hi, c.next(feat_hi))
                src = pt[:, f % 2, :] if nt == 4 else pt[:, :, 0:384]
                if arrange is not same:
                    src = src.rearrange("p (r i) -> p r i", r=4)
                h = hi[:, f, :] if nt == 4 else v3(hi[:, f, :], TC)
                l_ = lo[:, f, :] if nt == 4 else v3(lo[:, f, :], TC)
                e.tensor_tensor(arrange(l_), src, arrange(h).bitcast(F32), ALU.subtract).then_inc(feat_ready, 1)

        def act_unit(e, c, l, u):
            for h in range(2):
                e.wait_ge(ada_used, c.next(ada_used))
                w = A["ada_w_2"][bass.ds(l, 1), h * 512:h * 512 + 512, bass.ds(u * AC, AC)]
                e.dma_start(adaw[:, 4 * h:4 * h + 4, :], w.rearrange("o (k p) m -> p (o k) m", p=P)).then_inc(ada_in[h], 16)

        def dve_unit(e, c, b, half=None):
            for k in range(KT) if half is None else range(4 * half, 4 * half + 4):
                if k % 4 == 0:
                    e.wait_ge(ada_in[k // 4], c.next(ada_in[k // 4], 16))
                for s in range(2):
                    o, w, x = adap[:, b, s, :], adaw[:, k, :], scT[:, k, s:s + 1]
                    if k == 0:
                        i = e.tensor_scalar(o, w, x, None, ALU.mult)
                    else:
                        i = e.scalar_tensor_tensor(out=o, in0=w, scalar=x, in1=o, op0=ALU.mult, op1=ALU.add)
                    i.then_inc(dve_step, 1)
                e.wait_ge(dve_step, c.next(dve_step, 2))
                if k % 4 == 3:
                    e.sem_inc(ada_used, 1)
            if half != 0:
                e.sem_inc(ada_sums, 1)

        def pe_unit(e, c, b):
            e.wait_ge(ada_sums, c.next(ada_sums))
            past(e, pe_past)
            for j in range(AC // P):
                for s in range(2):
                    mm = e.matmul(ob[b][:, 2 * j + s:2 * j + s + 1], adap[:, b, s, j * P:j * P + P], edge[:, 4, 0:1],
                                  start=True, stop=True)
            mm.then_inc(ada_done, 1)

        def dve_unit_out(e, c, b, l, u):
            n = 2 * AC // P
            e.wait_ge(ada_done, c.next(ada_done))
            e.tensor_scalar(mods[:, bass.ds(l * (6 * KT * 2) + u * n, n)], ob[b][:, 0:n], 1.0, None, ALU.mult)\
             .then_inc(dve_step, 1)
            e.wait_ge(dve_step, c.next(dve_step))
            past(e, dve_past)

        def unit_of(part, down):
            before = sum(n // 2 for _, n in FF_PARTS[:part + down]) + KT // 2 * part
            return 1 + before

        def pe_ffn(e, c, T, ah, al, fresh, units=False):
            for p, (_, n) in enumerate(FF_PARTS):
                def up(e, i):
                    for _ in range(4):
                        slab(e, c, T, hh, hl, K8)
                    if units:
                        pe_unit(e, c, 0)
                if p == 0:
                    e.wait_ge(h_ready, c.next(h_ready, KT * fresh))
                    past(e, pe_past)
                if units and p == 0:
                    c.next(ada_sums)
                turns(e, c, n // 2, up)
                if units and p == 0:
                    c.next(ada_sums, -1)
                    pe_unit(e, c, 1)
                e.wait_ge(act_ready, c.next(act_ready, n))
                past(e, pe_past)
                pe_linear_y(e, c, T, ah, al, n, units)

        def act_ffn(e, c, T, conv, last=False, l=None):
            if conv:
                act_unit(e, c, l, 0)
                e.dma_start(cin[:, :, :], A["ctx_2"][0].rearrange("(r p) d -> p r d", p=P)).then_inc(cin_in, 16)
            for p, (_, n) in enumerate(FF_PARTS):
                def up(e, i):
                    if conv:
                        act_unit(e, c, l, i + unit_of(p, False))
                    for j in range(2):
                        for part in range(2):
                            head(e, c, KT)
                            s = c.turn("acc")
                            if part == 0:
                                e.wait_ge(slab_done, c.next(slab_done))
                                if conv:
                                    e.activation(zf[:, j, PAD:], acc[s][:, 0, :], ACT.Copy).then_inc(act_step, 1)
                                    e.wait_ge(act_step, c.next(act_step))
                                    e.sem_inc(up_ready, 1)
                                    e.sem_inc(acc_free[s], 1)
                                else:
                                    e.activation(v3(sq[:, j, 0:T], T), p3(acc[s], T), ACT.Silu).then_inc(act_step, 1)
                                    e.wait_ge(act_step, c.next(act_step))
                                    e.sem_inc(silu_ready, 1)
                                    e.sem_inc(acc_free[s], 1)
                            else:
                                c.next(slab_done)
                        if conv:
                            e.wait_ge(conv_ready, c.next(conv_ready))
                            e.activation(sq[:, j, 0:T], t2[:, j, 0:T], ACT.Silu).then_inc(silu_ready, 1)
                turns(e, c, n // 2, up)

                def down(e, i):
                    if conv:
                        act_unit(e, c, l, i + unit_of(p, True))
                    for _ in range(2):
                        head(e, c, KT)
                        passed(c)
                if last and p == len(FF_PARTS) - 1:
                    turns(e, c, KT // 2 - 1, down)
                    head(e, c, KT)
                    passed(c)
                    passed(c)
                else:
                    turns(e, c, KT // 2, down)

        def dve_ffn(e, c, T, y, ah, al, conv, l=None):
            if conv:
                dve_unit(e, c, 1)
                e.memset(zf[:, :, 0:PAD], 0.0).then_inc(dve_step, 1)
                e.wait_ge(dve_step, c.next(dve_step))
                past(e, dve_past)
            for p, (u0, n) in enumerate(FF_PARTS):
                def up(e, i):
                    for j in range(2):
                        if conv:
                            dve_unit(e, c, 0, j)
                        c.turn("slab")
                        s1 = c.turn("slab")
                        c.next(slab_done)
                        u = 2 * i + (u0 + j)
                        w = t2[:, j, 0:T]
                        if conv:
                            def wcol(k):
                                return cur[:, bass.ds(u + (70 + k * FT), 1)]
                            e.wait_ge(up_ready, c.next(up_ready))
                            e.tensor_scalar(w, zf[:, j, PAD:], wcol(2), None, ALU.mult).then_inc(dve_step, 1)
                            e.wait_ge(dve_step, c.next(dve_step))
                            e.scalar_tensor_tensor(out=w, in0=zf[:, j, PAD - 1:-1], scalar=wcol(1), in1=w,
                                                   op0=ALU.mult, op1=ALU.add).then_inc(dve_step, 1)
                            e.wait_ge(dve_step, c.next(dve_step))
                            e.scalar_tensor_tensor(out=w, in0=zf[:, j, PAD - 2:-2], scalar=wcol(0), in1=w,
                                                   op0=ALU.mult, op1=ALU.add).then_inc(conv_ready, 1)
                        e.wait_ge(slab_done, c.next(slab_done))
                        e.wait_ge(silu_ready, c.next(silu_ready))
                        e.tensor_tensor(v3(w, T), p3(acc[s1], T), v3(sq[:, j, 0:T], T), ALU.mult)\
                         .then_inc(dve_step, 1)
                        e.wait_ge(dve_step, c.next(dve_step))
                        e.sem_inc(acc_free[s1], 1)
                        a_h = ah[:, bass.ds(2 * i + j, 1), 0:T].rearrange("p o n -> p (o n)")
                        a_l = al[:, bass.ds(2 * i + j, 1), 0:T].rearrange("p o n -> p (o n)")
                        e.tensor_scalar(a_h, w, 1.0, None, ALU.mult).then_inc(dve_step, 1)
                        e.wait_ge(dve_step, c.next(dve_step))
                        e.tensor_tensor(a_l, w, a_h.bitcast(F32), ALU.subtract).then_inc(act_ready, 1)
                        e.wait_ge(act_ready, c.next(act_ready))
                    if conv:
                        dve_unit_out(e, c, 0, l, i + unit_of(p, False))
                turns(e, c, n // 2, up)
                if conv and p == 0:
                    dve_unit_out(e, c, 1, l, 0)
                dve_linear_y(e, c, T, y, first=p == 0, last=p == len(FF_PARTS) - 1,
                             unit=(l, unit_of(p, True)) if conv else None)

        def sp_ffn(e, c, l, up, down):
            for p, (u0, n) in enumerate(FF_PARTS):
                def body(e, i):
                    for j in range(2):
                        u = (2 * i + j + u0) * P
                        load(e, c, [(0, P, rows_of(up, l, 0, KT, u))])
                        load(e, c, [(0, P, rows_of(up, l, 0, KT, u + FF))])
                turns(e, c, n // 2, body)
                sp_cols(e, c, down, l, n, u0 * P)

        def sp_cols(e, c, W, l, kt, k0=0):
            def body(e, i):
                for j in range(2):
                    load(e, c, [(0, P, rows_of(W, l, k0, kt, (2 * i + j) * P))])
            turns(e, c, KT // 2, body)

        block = ctx.enter_context(nc.Block())

        @block.sync
        def _(sp):
            c = Counts()
            def rows(t, r0, ap):
                sp.dma_start(prow[r0:r0 + ap.shape[0], t, 0:ap.shape[1]], ap).then_inc(loaded, 16)

            for n, name in enumerate(NORMS):
                rows(0, 16 * n, A[name].rearrange("l (k p) -> (l k) p", p=P))
            rows(1, 0, A["conv_b_w"].rearrange("l k (t p) -> (l k t) p", p=P))
            rows(1, 18, A["norm_g_2"].rearrange("l g (k p) -> (l g k) p", p=P))
            rows(1, 82, A["c_2"].rearrange("o (k p) -> (o k) p", p=P))
            rows(1, 90, A["c_ctx_2"].rearrange("(k p) -> k p", p=P))
            rows(1, 98, A["mla_q_norm_g_2"].rearrange("o (k p) -> (o k) p", p=P))
            rows(1, 101, A["mla_kv_norm_g_2"].rearrange("o (k p) -> (o k) p", p=P))
            rows(2, 0, A["ada_b_2"].rearrange("l (k p) -> (l k) p", p=P))
            for l in range(DEPTH):
                rows(3 + l, 0, A["conv_ffn_w"][l].rearrange("k (u p) -> (k u) p", p=P))
            rows(5, 0, A["pool_scale"].rearrange("l (g p) -> (l g) p", p=PG))
            for dst, name in ((ident, "ident"), (ones, "ones"), (edge, "edge"), (perm, "perm1"), (inv1, "inv1")):
                sp.dma_start(dst[:], A[name]).then_inc(loaded, 16)
            sp.dma_start(angi[:, :], A["positions"][0].partition_broadcast(P)).then_inc(loaded, 16)
            sp.dma_start(min_[:, :, :], A["mem"][0].rearrange("(r p) d -> p r d", p=P)).then_inc(loaded, 16)
            sp.dma_start(xin[:, :, :], A["x"][0].rearrange("(r p) d -> p r d", p=P)).then_inc(loaded, 16)

            def layer(e, l):
                w_in = A["w_in"]
                for g in range(4):
                    load(e, c, [(0, P, rows_of(w_in, l, 0, KT, g * PG, PG))], PG)
                    if g == 1:
                        e.wait_ge(zone_free, c.next(zone_free))
                        e.dma_start(mask1[:, :, :], A["mask1"]).then_inc(mask_in, 16)
                for i in range(CT):
                    for k in (1, 3, 2):
                        load(e, c, [(0, P, rows_of(w_in, l, 0, KT, k * CW + i * P))])
                load(e, c, [(0, PG, A["pool_w"][bass.ds(l, 1)].rearrange("o g p m -> p (o g) m"))], PG)
                for j in range(2):
                    for base in (Q1, K1, V1):
                        for g in range(3):
                            load(e, c, [(0, P, rows_of(w_in, l, 0, KT, base + g * 256 + j * P))])

                def gates(e, m):
                    for br in range(3):
                        load(e, c, [(0, P, rows_of(w_in, l, 0, KT, m * P + (G1 + br * D)))])
                    load(e, c, [(0, PG, rows_of(A["w_branch_a"], l, 0, 4, m * P, rows=PG)),
                                (4, P, rows_of(A["w_branch_b"], l, 0, 3, m * P)),
                                (7, P, rows_of(A["w_branch_c"], l, 0, 2, m * P))])
                turns(e, c, KT, gates)
                sp_cols(e, c, A["w_out"], l, KT)
                for a in range(8):
                    load(e, c, [(0, P, rows_of(A["w_mkv"], l, 0, KT, a * P))])
                for a in range(4):
                    load(e, c, [(0, P, rows_of(A["w_mq"], l, 0, KT, a * P))])
                sp_cols(e, c, A["w_mo"], l, 4)
                sp_ffn(e, c, l, A["w_up"], A["w_down"])
            turns(sp, c, DEPTH, layer)

            ab = A["ab_w_in_2"]
            for col in (1024, 1152):
                load(sp, c, [(0, P, rows_of(ab, 0, 0, KT, col))])
            sp.wait_ge(zone_free, c.next(zone_free))
            for dst, name in ((rope_c, "cos_ab"), (rope_s, "sin_ab"), (perm, "perm_ab")):
                sp.dma_start(dst[:, :], A[name]).then_inc(ctx_in, 16)
            sp.wait_ge(zone_free, c.next(zone_free))
            sp.dma_start(mask2[:, :, :], A["mask2"]).then_inc(mask_in, 16)
            sp.dma_start(sink[:, :], A["ab_sink_2"][0].partition_broadcast(P)).then_inc(mask_in, 16)
            sp.dma_start(subg[:, :], A["diff_subln_g_2"][0].partition_broadcast(P)).then_inc(mask_in, 16)
            sp.dma_start(lamv[:, :, :], A["diff_lambda_2"][0].partition_broadcast(P)).then_inc(mask_in, 16)

            def heads_ab(e, t):
                s = c.turn("slab")
                e.wait_ge(lo_ready, c.next(lo_ready))
                for half in range(2):
                    e.dma_start(wraw[:, s, 0:KT, half * HD:half * HD + HD],
                                rows_of(ab, 0, 0, KT, t * HD + half * 256, HD)).then_inc(landed[s], 16)
                for col in (512, 1280, 1792):
                    load(e, c, [(0, P, rows_of(ab, 0, 0, KT, t * P + col))])
            turns(sp, c, 4, heads_ab)
            sp_cols(sp, c, A["ab_w_out_2"], 0, KT)
            sp_ffn(sp, c, 0, A["ffn_w13_2"], A["ffn_w2_2"])
            w = A["mla_w_in_2"]
            for j in range(2):
                load(sp, c, [(0, P, rows_of(w, 0, 0, KT, j * P))])
            sp.wait_ge(zone_free, c.next(zone_free))
            for dst, name in ((rope_c, "cos_c"), (rope_s, "sin_c"), (perm, "perm_c")):
                sp.dma_start(dst[:, :], A[name]).then_inc(ctx_in, 16)
            for j in range(2, 5):
                load(sp, c, [(0, P, rows_of(w, 0, 0, KT, j * P))])
            load(sp, c, [(0, P, rows_of(w, 0, 0, KT, 576, PG))], PG)

            def heads_c(e, i):
                for j in range(MH):
                    load(e, c, [(0, P, rows_of(A["mla_wq_b_2"], 0, 0, 3, (MH * i + j) * PG, PG))], PG)
                    load(e, c, [(0, P, rows_of(A["mla_wkv_b_2"], 0, 0, 2, (MH * i + j) * P))])
            turns(sp, c, C_HEADS // MH, heads_c)
            sp_cols(sp, c, A["mla_w_out_2"], 0, KT)
            sp_ffn(sp, c, 1, A["ffn_w13_2"], A["ffn_w2_2"])
            for r in range(4):
                sp.wait_ge(lt_out, r + 1 + 2 * KT)
                sp.dma_start(out[0, r * P:r * P + P, :], outb[:, r, :]).then_inc(stored, 16)
            sp.wait_ge(stored, 64)

        @block.gpsimd
        def _(pool):
            c = Counts()
            for s in range(2):
                pool.memset(wraw[:, s, :, :], 0.0).then_inc(lo_ready, 1)

            def cols(e, kt, n):
                def body(e, i):
                    for _ in range(2):
                        tail(e, c, kt)
                turns(e, c, n // 2, body)

            def ffn(e):
                for _, n in FF_PARTS:
                    cols(e, KT, 2 * n)
                    cols(e, n, KT)

            def layer(e, l):
                cols(e, KT, 4 + 9 - 1)
                tail(e, c, KT)
                tail(e, c, 4)
                cols(e, KT, 18)

                def gates(e, m):
                    for _ in range(3):
                        tail(e, c, KT)
                    tail(e, c, 9)
                turns(e, c, KT, gates)
                cols(e, KT, 8 + 12)
                cols(e, 4, KT)
                ffn(e)
            turns(pool, c, DEPTH, layer)
            cols(pool, KT, 2 + 16 + KT)
            ffn(pool)
            cols(pool, KT, 6)

            def heads_c(e, i):
                for _ in range(MH):
                    tail(e, c, 3)
                    tail(e, c, 2)
            turns(pool, c, C_HEADS // MH, heads_c)
            cols(pool, KT, KT)
            ffn(pool)

        def by_residue(ap):
            return ap.rearrange("p (i r) -> p r i", r=RES)

        def tiles_1(j):
            def qk(hi, lo, g):
                return dict(kind="rope", M=P, R=P, T=SEQ, hi=by_res_view(hi[:, g, :]), lo=by_res_view(lo[:, g, :]),
                            arrange=by_residue)
            tok = [slice(r, SEQ, RES) for r in range(RES)]
            return ([qk(qh, ql, g) for g in range(3)] + [qk(kh, kl, g) for g in range(3)]
                    + [dict(kind="v", M=P, T=SEQ, n=P, r0=0, tok=tok, v=vt[:, g, :, :]) for g in range(3)])

        def by_res_view(ap):
            return ap.rearrange("p (r i) -> p r i", r=RES)

        def its_1(j):
            its = []
            for h in range(2):
                rs = slice(h * HD, h * HD + HD)
                for r in range(RES):
                    cs = slice(r * P, r * P + P)
                    keys = [(qh[rs, 0, cs], ql[rs, 0, cs], kh[rs, 0, :], kl[rs, 0, :], 0)]
                    keys += [(qh[rs, g, cs], ql[rs, g, cs], kh[rs, g, cs], kl[rs, g, cs], 384 + g * P) for g in (1, 2)]
                    v = [vt[:, 0, i, rs] for i in range(RES)] + [vt[:, 1, r, rs], vt[:, 2, r, rs]]
                    its.append(dict(keys=keys, v=v, c0=0, mask=mask1[:, r, :], sink=None, scale=HD ** -0.5, dv=HD,
                                    dst=ot1[:, r, (2 * j + h) * HD:(2 * j + h + 1) * HD]))
            return its

        def tiles_mem():
            ctx_cols = [slice(i * P, i * P + P) for i in range(2)]
            return ([dict(kind="plain", M=P, R=P, T=CTX, hi=kmh[:, a, :], lo=kml[:, a, :]) for a in range(4)]
                    + [dict(kind="v", M=P, T=CTX, n=P, r0=0, tok=ctx_cols, v=vm[:, a, :, :]) for a in range(4)]
                    + [dict(kind="plain", M=P, R=P, T=SEQ, hi=qmh[:, a, :], lo=qml[:, a, :]) for a in range(4)])

        def its_mem():
            return [dict(keys=[(qmh[:, a, r * P:r * P + P], qml[:, a, r * P:r * P + P], kmh[:, a, :], kml[:, a, :], 0)],
                         v=[vm[:, a, i, :] for i in range(2)], c0=0, mask=None, sink=None, scale=P ** -0.5, dv=P,
                         dst=otm[:, r, a * P:a * P + P]) for a in range(4) for r in range(4)]

        all_tok = [slice(i * P, i * P + P) for i in range(6)]

        def tile_kg():
            return [dict(kind="rope", M=P, R=P, T=TC, hi=kgh[:, :], lo=kgl[:, :]),
                    dict(kind="v", M=P, T=TC, n=P, r0=0, tok=all_tok, v=vg[:, :, :])]

        def tiles_ab():
            return [dict(kind="rope", M=P, R=P, T=TC, hi=qgh[:, :], lo=qgl[:, :]),
                    dict(kind="rope", M=P, R=P, T=TC, hi=qdh[:, :], lo=qdl[:, :]),
                    dict(kind="rope", M=P, R=P, T=TC, hi=kdh[:, :], lo=kdl[:, :]),
                    dict(kind="v", M=P, T=TC, n=P, r0=0, tok=all_tok, v=vd[:, :, :])]

        def its_ab(t):
            def keys(q_hi, q_lo, k_hi, k_lo, rs, r):
                cs = slice(r * P, r * P + P)
                parts = [(0, SEQ), (SEQ, TC)] if r < 4 else [(SEQ, TC)]
                return [(q_hi[rs, cs], q_lo[rs, cs], k_hi[rs, a:b], k_lo[rs, a:b], a) for a, b in parts]
            its = []
            for h in range(2):
                rs = slice(h * HD, h * HD + HD)
                for r in range(6):
                    v = [vg[:, i, rs] for i in range(0 if r < 4 else 4, 6)]
                    its.append(dict(keys=keys(qgh, qgl, kgh, kgl, rs, r), v=v, c0=0 if r < 4 else SEQ,
                                    mask=mask2[:, r, :] if r < 4 else None, sink=h, scale=HD ** -0.5, dv=HD,
                                    dst=ot2[:, r, bass.ds(t * HD + h * 256, HD)]))
            return its

        def its_diff(t):
            def keys(m, r):
                rs, cs = slice(m * HD, m * HD + HD), slice(r * P, r * P + P)
                parts = [(0, SEQ), (SEQ, TC)] if r < 4 else [(SEQ, TC)]
                return [(qdh[rs, cs], qdl[rs, cs], kdh[rs, a:b], kdl[rs, a:b], a) for a, b in parts]
            return [dict(maps=[keys(m, r) for m in range(2)], v=[vd[:, i, :] for i in range(0 if r < 4 else 4, 6)],
                         c0=0 if r < 4 else SEQ, scale=HD ** -0.5, dst=ot2[:, r, bass.ds(t * P + 512, P)])
                    for r in range(6)]

        def tile_kr():
            return [dict(kind="rope", M=PG, R=PG, T=TC, hi=kch[0:PG, 0, :], lo=kcl[0:PG, 0, :])]

        def tiles_c():
            out_ = []
            for j in range(MH):
                out_ += [dict(kind="rope", M=PG, R=PG, T=SEQ, hi=qch[0:PG, j, :], lo=qcl[0:PG, j, :],
                              kts=[(k, k, P) for k in range(3)]),
                         dict(kind="kv", M=P, R=HD, T=TC, n=HD, r0=HD, tok=all_tok, v=vc[:, j, :, :],
                              hi=kch[0:HD, j, :], lo=kcl[0:HD, j, :], kts=[(k, 3 + k, P) for k in range(2)])]
            return out_

        def its_c(i):
            return [dict(keys=[(qch[0:PG, j, r * P:r * P + P], qcl[0:PG, j, r * P:r * P + P],
                                kch[0:PG, j, a:b], kcl[0:PG, j, a:b], a) for a, b in ((0, SEQ), (SEQ, TC))],
                         v=[vc[:, j, n, :] for n in range(6)], c0=0, mask=None, sink=None, scale=PG ** -0.5, dv=HD,
                         dst=ot3[:, r, bass.ds((MH * i + j) * HD, HD)])
                    for j in range(MH) for r in range(4)]

        K9 = [[(k, k, PG) for k in range(4)], [(k, k, P) for k in range(4, 7)], [(k, k, P) for k in range(7, 9)]]

        @block.tensor
        def _(pe):
            c = Counts()
            give(pe, acc_free + [pt_free] + ob_free)
            for s in (slab_done, sq_used, tr_done, pv_done, ada_used):
                pe.sem_inc(s, 2)
            pe.sem_inc(gates_used, 1)
            c.start(lo_ready, 2)

            def turn_tokens(e, src, n):
                take(e, c, acc_free)
                for k in range(KT):
                    if k >= 2:
                        e.wait_ge(lt_out, c.next(lt_out))
                    for r in range(n):
                        tr = e.transpose(acc[k % 2][:, 0, r * P:r * P + P], src[:, r, k * P:k * P + P], ident[:, :])
                    tr.then_inc(lt_done, 1)
                e.wait_ge(lt_out, c.next(lt_out, 2))
                give(e, acc_free)

            pe.wait_ge(loaded, 16 * N_LOADS)
            take(pe, c, acc_free)
            for t, n in enumerate(PAR_ROWS):
                w = PG if t == 5 else P
                if t >= 2:
                    pe.wait_ge(set_done, c.next(set_done))
                pe.transpose(acc[t % 2][0:w, 0, 0:n], prow[0:n, t, 0:w], ident[0:n, 0:n]).then_inc(lt_done, 1)
            pe.wait_ge(set_done, c.next(set_done, 2))
            give(pe, acc_free)
            turn_tokens(pe, min_, 2)
            take(pe, c, acc_free)
            for k in range(KT):
                if k >= 2:
                    pe.wait_ge(x_ready, k - 1)
                for r in range(4):
                    tr = pe.transpose(acc[k % 2][:, 0, r * P:r * P + P], xin[:, r, k * P:k * P + P], ident[:, :])
                tr.then_inc(lt_done, 1)
            pe.wait_ge(x_ready, KT)
            give(pe, acc_free)

            def layer(e, l):
                pe_stats(e, c, TC)
                for g in range(4):
                    slab(e, c, SEQ, hh, hl, K8, M=PG, fresh=2 if g == 0 else 0)
                for i in range(3 * CT):
                    slab(e, c, SEQ, hh, hl, K8)
                s = c.turn("slab")
                e.wait_ge(lo_ready, c.next(lo_ready))
                take(e, c, [acc_free[s], pt_free])
                e.wait_ge(pool_ready, c.next(pool_ready, 4))
                for g in range(4):
                    o = (acc[s] if g < 2 else pt)[0:PG, g % 2, :]
                    mm = mm3(e, o, whi[0:PG, s, g, 0:PG], wlo[0:PG, s, g, 0:PG], poh[0:PG, g, :], pol[0:PG, g, :],
                             True, True)
                mm.then_inc(slab_done, 1)
                for j in range(2):
                    pe_tiles(e, c, tiles_1(j), K8, hh, hl)
                    pe_attention(e, c, its_1(j))
                pe_features(e, c, ot1, 2, 4)
                e.wait_ge(bi_ready, c.next(bi_ready, 4 + CT))
                past(e, pe_past)

                def gates(e, m):
                    for _ in range(3):
                        slab(e, c, SEQ, hh, hl, K8)
                    s = c.turn("slab")
                    e.wait_ge(lo_ready, c.next(lo_ready))
                    take(e, c, [acc_free[s], pt_free])
                    for o, ks in zip((acc[s][:, 0, :], acc[s][:, 1, :], pt[:, 0, :]), K9):
                        for n, (k, _, rows) in enumerate(ks):
                            mm = mm3(e, o, whi[0:rows, s, k, :], wlo[0:rows, s, k, :], bih[0:rows, k, :],
                                     bil[0:rows, k, :], n == 0, n == len(ks) - 1)
                    mm.then_inc(slab_done, 1)
                turns(e, c, KT, gates)
                e.wait_ge(merged_ready, c.next(merged_ready, KT))
                past(e, pe_past)
                pe_linear_y(e, c, SEQ, mgh, mgl, KT)
                pe_postnorm(e, c, SEQ)
                pe_stats(e, c, SEQ)
                for _ in range(KT):
                    e.wait_ge(h_ready, c.next(h_ready))
                tiles = tiles_mem()
                for t in tiles[:8]:
                    t["c0"] = SEQ
                pe_tiles(e, c, tiles, K8, hh, hl)
                pe_attention(e, c, its_mem())
                pe_features(e, c, otm, 4, 4)
                pe_linear_y(e, c, SEQ, ofh, ofl, 4)
                pe_postnorm(e, c, SEQ)
                pe_stats(e, c, SEQ)
                pe_ffn(e, c, SEQ, act1h, act1l, 1, units=True)
                pe_postnorm(e, c, SEQ)
            turns(pe, c, DEPTH, layer)

            pe.wait_ge(cin_in, 16 * DEPTH)
            turn_tokens(pe, cin, 2)
            pe_stats(pe, c, TC)
            pe.wait_ge(ctx_in, 48)
            pe_tiles(pe, c, tile_kg(), K8, hh, hl, fresh=2)

            def heads_ab(e, t):
                pe_tiles(e, c, tiles_ab(), K8, hh, hl)
                pe_attention(e, c, its_ab(t))
                pe_diff(e, c, its_diff(t))
            turns(pe, c, 4, heads_ab)
            pe_features(pe, c, ot2, KT, 6, normed=4)
            pe_linear_y(pe, c, TC, hh, hl, KT)
            pe_postnorm(pe, c, TC)
            pe_stats(pe, c, TC)
            pe_ffn(pe, c, TC, acth, actl, 2)
            pe_postnorm(pe, c, TC)
            pe_stats(pe, c, TC)
            for j in range(5):
                slab(pe, c, SEQ if j < 3 else TC, hh, hl, K8, fresh=2 if j == 0 else 0)
                if j in (2, 4):
                    pe_postnorm(pe, c, SEQ if j < 3 else TC)
            pe.wait_ge(ctx_in, 96)
            pe.wait_ge(h_ready, c.next(h_ready, 5))
            pe_tiles(pe, c, tile_kr(), K8, hh, hl)
            pe.wait_ge(kr_ready, 2 * (MH - 1))

            def heads_c(e, i):
                pe_tiles(e, c, tiles_c(), None, lath, latl)
                pe_attention(e, c, its_c(i))
            turns(pe, c, C_HEADS // MH, heads_c)
            pe_features(pe, c, ot3, KT, 4)
            pe_linear_y(pe, c, SEQ, o3h, o3l, KT)
            pe_postnorm(pe, c, SEQ)
            pe_stats(pe, c, SEQ)
            pe_ffn(pe, c, SEQ, act1h, act1l, 1)
            pe_postnorm(pe, c, SEQ)
            take(pe, c, acc_free)
            pe.wait_ge(x_ready, KT * (1 + 3 * DEPTH + 2 * DEPTH))
            for r in range(4):
                if r >= 2:
                    pe.wait_ge(lt_out, c.next(lt_out))
                for k in range(KT):
                    tr = pe.transpose(acc[r % 2][:, k // 4, k % 4 * P:k % 4 * P + P], xres[:, k, r * P:r * P + P], ident[:, :])
                tr.then_inc(lt_done, 1)

        @block.scalar
        def _(act):
            c = Counts()
            for s in (slab_done, sq_used):
                c.start(s, 2, "" if s is slab_done else "all")
            c.start(tr_done, 2)
            c.start(pv_done, 2)
            act.wait_ge(set_done, 1 + len(PAR_ROWS))
            act.activation(scT[:, :, 0], par[:, 1, 82:90], ACT.Silu).then_inc(act_step, 1)
            act.activation(scT[:, :, 1], par[:, 1, 90:98], ACT.Silu).then_inc(act_step, 1)
            act.wait_ge(act_step, c.next(act_step, 2))
            act.sem_inc(cond_ready, 1)
            act.activation(rope_s[:, :], red[:, :], ACT.Sin).then_inc(act_step, 1)
            act.wait_ge(set_done, 2 + len(PAR_ROWS))
            act.activation(rope_c[:, :], turn_n[:, :], ACT.Sin).then_inc(act_step, 1)
            act.wait_ge(act_step, c.next(act_step, 2))
            act.sem_inc(tables_ready, 1)
            head(act, c, KT)

            def layer(e, l):
                act_prenorm(e, c, TC, segs_a())
                for g in range(4):
                    head(e, c, KT)
                    s = c.turn("acc")
                    e.wait_ge(slab_done, c.next(slab_done))
                    if g >= 2:
                        e.wait_ge(pool_ready, c.next(pool_ready))
                    e.activation(ub[0:PG, g % 2, PAD:], acc[s][0:PG, 0, :], ACT.Copy).then_inc(act_step, 1)
                    e.wait_ge(act_step, c.next(act_step))
                    e.sem_inc(in_ready, 1)
                    e.sem_inc(acc_free[s], 1)
                    e.wait_ge(sum_ready, c.next(sum_ready))
                    e.activation(poh[0:PG, g, :], t2[0:PG, g % 2, 0:SEQ], ACT.Copy).then_inc(pool_hi, 1)
                c.next(pool_ready, 2)
                for i in range(CT):
                    head(e, c, KT)
                    s = c.turn("acc")
                    e.wait_ge(slab_done, c.next(slab_done))
                    if i == 2:
                        e.wait_ge(bi_ready, c.next(bi_ready))
                    e.activation(bxs[:, i % 2, :], acc[s][:, 0, :], ACT.Copy).then_inc(act_step, 1)
                    e.wait_ge(act_step, c.next(act_step))
                    e.sem_inc(in_ready, 1)
                    e.sem_inc(acc_free[s], 1)
                    head(e, c, KT)
                    passed(c)
                    head(e, c, KT if i < 2 else 4)
                    passed(c)
                    e.wait_ge(sum_ready, c.next(sum_ready))
                    e.activation(bih[:, 4 + i, :], t2[:, i % 2, 0:SEQ], ACT.Copy).then_inc(bi_hi, 1)
                c.next(bi_ready, 2)
                head(e, c, KT)
                passed(c)
                for g in range(4):
                    e.wait_ge(sum_ready, c.next(sum_ready))
                    e.activation(bih[0:PG, g, :], t2[0:PG, g % 2, 0:SEQ], ACT.Copy).then_inc(bi_hi, 1)
                c.next(bi_ready, 4)
                for j in range(2):
                    act_tiles(e, c, tiles_1(j), [(KT,)] * 9)
                    act_attention(e, c, its_1(j))
                act_features(e, c, bih[:, 7:9, :], 2, 4, by_residue)

                def gates(e, m):
                    e.wait_ge(gates_used, c.next(gates_used))
                    for b in range(3):
                        head(e, c, *((KT,) if b < 2 else (9, 3)))
                        s = c.turn("acc")
                        e.wait_ge(slab_done, c.next(slab_done))
                        e.activation(GATE[b], acc[s][:, 0, :], ACT.Sigmoid).then_inc(act_step, 1)
                        e.wait_ge(act_step, c.next(act_step))
                        e.sem_inc(gate_ready, 1)
                        e.sem_inc(acc_free[s], 1)
                    head(e, c, KT)
                    passed(c)
                turns(e, c, KT, gates)
                act_linear_y(e, c, KT)
                act_postnorm(e, c, SEQ)
                act_prenorm(e, c, SEQ, segs_m())
                act_tiles(e, c, tiles_mem(), [(KT,)] * 11 + [(4,)])
                act_attention(e, c, its_mem())
                act_features(e, c, ofh, 4, 4)
                for i in range(KT):
                    head(e, c, 4 if i < KT - 1 else KT)
                    passed(c)
                act_postnorm(e, c, SEQ)
                act_prenorm(e, c, SEQ, segs_f())
                act_ffn(e, c, SEQ, True, l=l)
                act_postnorm(e, c, SEQ)
            turns(act, c, DEPTH, layer)

            act.wait_ge(lam_in, 1)
            act.activation(small[:, 46:48], small[:, 44:46], ACT.Exp).then_inc(lam_out, 1)
            act_prenorm(act, c, TC, segs_2(0))
            act_tiles(act, c, tile_kg(), [(KT,), (KT, 2)])

            def turn_ab(e, t, last):
                act_tiles(e, c, tiles_ab(), [(KT,)] * 3 + [(KT,) if last else (KT, 2)])
                act_attention(e, c, its_ab(t))
                act_diff(e, c, its_diff(t))
            turns(act, c, 3, lambda e, t: turn_ab(e, t, False))
            turn_ab(act, 3, True)
            act.wait_ge(ss_ready, 1)
            act.activation(hss[:, :], hss[:, :], ACT.Ln, bias=small[:, 63:64], scale=1.0 / P).then_inc(act_step, 1)
            act.wait_ge(act_step, c.next(act_step))
            act.activation(hss[:, :], hss[:, :], ACT.Exp, scale=-0.5).then_inc(subn_ready, 1)
            act_features(act, c, hh, KT, 6)
            act_linear_y(act, c, KT)
            act_postnorm(act, c, TC)
            act_prenorm(act, c, TC, segs_2(3))
            act_ffn(act, c, TC, False)
            act_postnorm(act, c, TC)
            act_prenorm(act, c, TC, segs_2(0))
            for j in range(5):
                head(act, c, KT)
                passed(c)
                if j in (2, 4):
                    T = SEQ if j < 3 else TC
                    act.wait_ge(ystat_done, c.next(ystat_done))
                    act_rstd(act, c, T, D / (C_QL if j < 3 else C_KVL))
                    act_apply(act, c, lath, range(3) if j < 3 else range(3, 5), segs_lat(T))
            act_tiles(act, c, tile_kr(), [(3,)])

            def heads_c(e, i):
                act_tiles(e, c, tiles_c(), [(2,), (3,)] * (MH - 1) + [(2,), (KT,)])
                act_attention(e, c, its_c(i))
            turns(act, c, C_HEADS // MH, heads_c)
            act_features(act, c, o3h, KT, 4)
            act_linear_y(act, c, KT)
            act_postnorm(act, c, SEQ)
            act_prenorm(act, c, SEQ, segs_2(3)[:1])
            act_ffn(act, c, SEQ, False, last=True)
            act_postnorm(act, c, SEQ)

        @block.vector
        def _(dve):
            c = Counts()
            for s in (slab_done, tr_done, pv_done):
                c.start(s, 2)

            def turned(e, col0, n, signal):
                for k in range(KT):
                    e.wait_ge(lt_done, c.next(lt_done))
                    e.tensor_copy(xres[:, k, col0:col0 + n * P], acc[k % 2][:, 0, 0:n * P]).then_inc(signal, 1)

            dve.memset(small[:, 63:64], EPS).then_inc(dve_step, 1)
            dve.wait_ge(dve_step, c.next(dve_step))
            for t, n in enumerate(PAR_ROWS):
                w = PG if t == 5 else P
                dve.wait_ge(lt_done, c.next(lt_done))
                dve.tensor_copy(par[0:w, t, 0:n], acc[t % 2][0:w, 0, 0:n]).then_inc(set_done, 1)
            dve.wait_ge(loaded, 16 * N_LOADS)

            def step(ins):
                ins.then_inc(dve_step, 1)
                dve.wait_ge(dve_step, c.next(dve_step))

            step(dve.tensor_copy(ang[:, :], angi[:, :]))
            step(dve.tensor_scalar(ang[:, :], ang[:, :], inv1[:, 0:1], None, ALU.mult))
            step(dve.tensor_scalar(turn_n[:, :], ang[:, :], 1.0 / TWO_PI, ROUND, ALU.mult, ALU.add))
            step(dve.tensor_scalar(turn_n[:, :], turn_n[:, :], ROUND, None, ALU.subtract))
            for part in (CW1, CW2, CW3):
                step(dve.scalar_tensor_tensor(out=ang[:, :], in0=turn_n[:, :], scalar=-part, in1=ang[:, :],
                                              op0=ALU.mult, op1=ALU.add))
            dve.tensor_scalar(red[:, :], ang[:, :], 3.1415925, -3.1415925, ALU.min, ALU.max).then_inc(set_done, 1)
            dve.wait_ge(set_done, 1 + len(PAR_ROWS))
            step(dve.scalar_tensor_tensor(out=turn_n[:, :], in0=red[:, :], scalar=-1.0, in1=red[:, :],
                                          op0=ALU.mult, op1=ALU.max))
            dve.tensor_scalar(turn_n[:, :], turn_n[:, :], -1.0, TWO_PI / 4, ALU.mult, ALU.add).then_inc(set_done, 1)
            turned(dve, SEQ, 2, lt_out)
            turned(dve, 0, 4, x_ready)
            c.start(x_ready, KT)
            dve.wait_ge(cond_ready, 1)
            dve.wait_ge(tables_ready, 1)

            def layer(e, l):
                e.sem_inc(zone_free, 1)
                gains = par[:, 0, 0:112].rearrange("p (n l k) -> p n l k", l=DEPTH, k=KT)[:, :, bass.ds(l, 1), :]
                e.tensor_scalar(cur[:, 0:56].rearrange("p (n k) -> p n k", k=KT), gains.rearrange("p n o k -> p n (o k)"),
                                1.0, None, ALU.mult).then_inc(dve_step, 1)
                e.tensor_scalar(cur[:, 56:65], par[:, 1, bass.ds(l * 9, 9)], 1.0, None, ALU.mult).then_inc(dve_step, 1)
                e.tensor_scalar(cur[0:PG, 65:69], par[0:PG, 5, bass.ds(l * 4, 4)], 1.0, None, ALU.mult).then_inc(dve_step, 1)
                e.tensor_scalar(cur[:, 70:136], par[:, bass.ds(l + 3, 1), 0:66].rearrange("p o n -> p (o n)"), 1.0, None,
                                ALU.mult).then_inc(dve_step, 1)
                for buf in (ub, sa, zc):
                    e.memset(buf[:, :, 0:PAD], 0.0).then_inc(dve_step, 1)
                e.wait_ge(dve_step, c.next(dve_step, 7))
                dve_prenorm(e, c, segs_a())

                def st(ins):
                    ins.then_inc(dve_step, 1)
                    e.wait_ge(dve_step, c.next(dve_step))

                for g, w in enumerate(POOL_W):
                    c.turn("slab")
                    c.next(slab_done)
                    e.wait_ge(in_ready, c.next(in_ready))
                    src, shift, k = ub[0:PG, g % 2, :], 1, 0
                    u = ub[0:PG, g % 2, PAD:]
                    while shift < w:
                        dst = sa[0:PG, k % 2, :]
                        st(e.tensor_tensor(dst[:, PAD:], src[:, PAD:], src[:, PAD - shift:PAD + SEQ - shift], ALU.add))
                        src, shift, k = dst, 2 * shift, k + 1
                    pooled = t2[0:PG, g % 2, 0:SEQ]
                    e.tensor_tensor(pooled[:, 0:PAD], src[:, PAD:2 * PAD], edge[0:PG, g, :], ALU.mult).then_inc(dve_step, 1)
                    e.scalar_tensor_tensor(out=pooled[:, PAD:], in0=src[:, 2 * PAD:], scalar=1.0 / w, in1=u[:, PAD:],
                                           op0=ALU.mult, op1=ALU.subtract).then_inc(dve_step, 1)
                    e.wait_ge(dve_step, c.next(dve_step, 2))
                    e.tensor_tensor(pooled[:, 0:PAD], pooled[:, 0:PAD], u[:, 0:PAD], ALU.subtract).then_inc(sum_ready, 1)
                    e.wait_ge(pool_hi, c.next(pool_hi))
                    e.tensor_tensor(pol[0:PG, g, :], pooled, poh[0:PG, g, :].bitcast(F32), ALU.subtract)\
                     .then_inc(pool_ready, 1)
                e.wait_ge(pool_ready, c.next(pool_ready, 4))
                for i in range(CT):
                    def wcol(k):
                        return cur[:, 56 + k * CT + i:57 + k * CT + i]
                    c.turn("slab")
                    c.next(slab_done)
                    w = t2[:, i % 2, 0:SEQ]
                    e.wait_ge(in_ready, c.next(in_ready))
                    s = c.turn("slab")
                    e.wait_ge(slab_done, c.next(slab_done))
                    st(e.tensor_tensor(zc[:, i % 2, PAD:], acc[s][:, 0, :], bxs[:, i % 2, :], ALU.mult))
                    e.sem_inc(acc_free[s], 1)
                    st(e.tensor_scalar(w, zc[:, i % 2, PAD:], wcol(2), None, ALU.mult))
                    for k in (1, 0):
                        st(e.scalar_tensor_tensor(out=w, in0=zc[:, i % 2, PAD - 2 + k:PAD + SEQ - 2 + k], scalar=wcol(k),
                                                  in1=w, op0=ALU.mult, op1=ALU.add))
                    s = c.turn("slab")
                    e.wait_ge(slab_done, c.next(slab_done))
                    st(e.tensor_tensor(w, acc[s][:, 0, :], w, ALU.mult))
                    e.sem_inc(acc_free[s], 1)
                    e.sem_inc(sum_ready, 1)
                    e.wait_ge(bi_hi, c.next(bi_hi))
                    e.tensor_tensor(bil[:, 4 + i, :], w, bih[:, 4 + i, :].bitcast(F32), ALU.subtract).then_inc(bi_ready, 1)
                e.wait_ge(bi_ready, c.next(bi_ready, CT))
                s = c.turn("slab")
                e.wait_ge(slab_done, c.next(slab_done))
                for g in range(4):
                    w = t2[0:PG, g % 2, 0:SEQ]
                    st(e.tensor_scalar(w, (acc[s] if g < 2 else pt)[0:PG, g % 2, :], cur[0:PG, 65 + g:66 + g], None, ALU.mult))
                    if g == 1:
                        e.sem_inc(acc_free[s], 1)
                    if g == 3:
                        e.sem_inc(pt_free, 1)
                    e.sem_inc(sum_ready, 1)
                    e.wait_ge(bi_hi, c.next(bi_hi))
                    e.tensor_tensor(bil[0:PG, g, :], w, bih[0:PG, g, :].bitcast(F32), ALU.subtract).then_inc(bi_ready, 1)
                    e.wait_ge(bi_ready, c.next(bi_ready))
                e.wait_ge(mask_in, c.next(mask_in, 16))
                for j in range(2):
                    dve_tiles(e, c, tiles_1(j))
                    dve_attention(e, c, its_1(j))
                dve_features(e, c, bih[:, 7:9, :], bil[:, 7:9, :], 2, 4, by_residue)

                def gates(e, m):
                    c.turn("slab"), c.turn("slab"), c.turn("slab")
                    s = c.turn("slab")
                    c.next(slab_done, 3)
                    e.wait_ge(slab_done, c.next(slab_done))
                    e.wait_ge(gate_ready, c.next(gate_ready, 3))
                    for b, o in enumerate((acc[s][:, 0, :], acc[s][:, 1, :], pt[:, 0, :])):
                        e.tensor_tensor(PROD[b], o, GATE[b], ALU.mult).then_inc(dve_step, 1)
                    e.wait_ge(dve_step, c.next(dve_step, 3))
                    e.sem_inc(acc_free[s], 1)
                    e.sem_inc(pt_free, 1)
                    e.sem_inc(gates_used, 1)
                    for b in (1, 2):
                        e.tensor_tensor(PROD[0], PROD[0], PROD[b], ALU.add).then_inc(dve_step, 1)
                        e.wait_ge(dve_step, c.next(dve_step))
                    m_h = mgh[:, bass.ds(m, 1), :].rearrange("p o n -> p (o n)")
                    m_l = mgl[:, bass.ds(m, 1), :].rearrange("p o n -> p (o n)")
                    e.tensor_scalar(m_h, PROD[0], 1.0, None, ALU.mult).then_inc(dve_step, 1)
                    e.wait_ge(dve_step, c.next(dve_step))
                    e.tensor_tensor(m_l, PROD[0], m_h.bitcast(F32), ALU.subtract).then_inc(merged_ready, 1)
                    e.wait_ge(merged_ready, c.next(merged_ready))
                turns(e, c, KT, gates)
                dve_linear_y(e, c, SEQ, y1)
                dve_postnorm(e, c, SEQ, y1, [(0, SEQ, gain(8))])
                dve_prenorm(e, c, segs_m())
                dve_tiles(e, c, tiles_mem())
                dve_attention(e, c, its_mem())
                dve_features(e, c, ofh, ofl, 4, 4)
                dve_linear_y(e, c, SEQ, y1)
                dve_postnorm(e, c, SEQ, y1, [(0, SEQ, gain(24))])
                dve_prenorm(e, c, segs_f())
                dve_ffn(e, c, SEQ, y1, act1h, act1l, True, l=l)
                dve_postnorm(e, c, SEQ, y1, [(0, SEQ, gain(48))])
            turns(dve, c, DEPTH, layer)

            dve.sem_inc(zone_free, 1)
            turned(dve, SEQ, 2, lt_out)
            dve.sem_inc(zone_free, 1)
            mod = mods[:, :].rearrange("p (j s) -> p j s", s=2)
            for s in range(2):
                dve.tensor_tensor(mod[:, :, s], mod[:, :, s], par[:, 2, 0:DEPTH * 6 * KT], ALU.add).then_inc(dve_step, 1)
            dve.wait_ge(dve_step, c.next(dve_step, 2))

            def modulation(l):
                for s in range(2):
                    for a in range(2):
                        M = [mod[:, (6 * l + 3 * a + i) * KT:(6 * l + 3 * a + i + 1) * KT, s] for i in range(3)]
                        g = [par[:, 1, 18 + (4 * l + 2 * a + i) * KT:18 + (4 * l + 2 * a + i + 1) * KT] for i in range(2)]
                        dve.scalar_tensor_tensor(out=cur2[:, s, 3 * a, :], in0=M[1], scalar=1.0, in1=g[0], op0=ALU.add,
                                                 op1=ALU.mult).then_inc(dve_step, 1)
                        dve.tensor_copy(cur2[:, s, 3 * a + 1, :], M[0]).then_inc(dve_step, 1)
                        dve.tensor_tensor(cur2[:, s, 3 * a + 2, :], M[2], g[1], ALU.mult).then_inc(dve_step, 1)
                dve.wait_ge(dve_step, c.next(dve_step, 12))

            modulation(0)
            dve.wait_ge(mask_in, c.next(mask_in, 64))
            for k in range(2):
                dve.tensor_tensor_reduce(lamv[:, 2 * k, :], lamv[:, 2 * k, :], lamv[:, 2 * k + 1, :], 1.0, 0.0, ALU.mult,
                                         ALU.add, small[:, 44 + k:45 + k]).then_inc(dve_step, 1)
            dve.wait_ge(dve_step, c.next(dve_step, 2))
            dve.sem_inc(lam_in, 1)
            dve.wait_ge(lam_out, 1)
            step(dve.tensor_tensor(small[:, 40:41], small[:, 47:48], small[:, 46:47], ALU.subtract))
            step(dve.tensor_scalar(small[:, 40:41], small[:, 40:41], -LAM_INIT, None, ALU.add))
            step(dve.tensor_scalar(subg[:, :], subg[:, :], 1.0 - LAM_INIT, None, ALU.mult))
            dve_prenorm(dve, c, segs_2(0))
            dve.wait_ge(ctx_in, 48)
            dve_tiles(dve, c, tile_kg())

            def heads_ab(e, t):
                for h in range(2):
                    e.tensor_scalar(small[:, SK + h:SK + h + 1], sink[:, bass.ds(t + 4 * h, 1)], 1.0, None, ALU.mult)\
                     .then_inc(dve_step, 1)
                e.wait_ge(dve_step, c.next(dve_step, 2))
                dve_tiles(e, c, tiles_ab())
                dve_attention(e, c, its_ab(t))
                dve_diff(e, c, its_diff(t))
                e.tensor_scalar(hss[:, bass.ds(t * 6, 6)], small[:, SS:SS + 6], 1.0, None, ALU.mult).then_inc(dve_step, 1)
                e.wait_ge(dve_step, c.next(dve_step))
            turns(dve, c, 4, heads_ab)
            dve.sem_inc(ss_ready, 1)
            dve.wait_ge(subn_ready, 1)
            dve_features(dve, c, hh, hl, KT, 6, normed=4)
            dve_linear_y(dve, c, TC, y2)
            dve_postnorm(dve, c, TC, y2, [(0, SEQ, G2(0, 2)), (SEQ, TC, G2(1, 2))])
            dve_prenorm(dve, c, segs_2(3))
            dve_ffn(dve, c, TC, y2, acth, actl, False)
            dve_postnorm(dve, c, TC, y2, [(0, SEQ, G2(0, 5)), (SEQ, TC, G2(1, 5))])
            dve.sem_inc(zone_free, 1)
            modulation(1)
            dve_prenorm(dve, c, segs_2(0))
            for j in range(5):
                T = SEQ if j < 3 else TC
                if j in (0, 3):
                    step(dve.memset(ysum[:, 0:T], 0.0))
                s = c.turn("slab")
                dve.wait_ge(slab_done, c.next(slab_done))
                step(dve.tensor_scalar(v3(lat[:, j, 0:T], T), p3(acc[s], T), 1.0, None, ALU.mult))
                dve.sem_inc(acc_free[s], 1)
                step(dve.tensor_tensor(sq[:, 0, 0:T], lat[:, j, 0:T], lat[:, j, 0:T], ALU.mult))
                step(dve.tensor_tensor(ysum[:, 0:T], ysum[:, 0:T], sq[:, 0, 0:T], ALU.add))
                if j in (2, 4):
                    dve.sem_inc(ysum_ready, 1)
                    dve_apply(dve, c, lat, lath, latl, range(3) if j < 3 else range(3, 5), segs_lat(T))
            dve.wait_ge(ctx_in, 96)
            dve_tiles(dve, c, tile_kr())
            for j in range(1, MH):
                dve.tensor_copy(kch[HD:PG, j, :], kch[HD:PG, 0, :].bitcast(F32)).then_inc(kr_ready, 1)
                dve.tensor_tensor(kcl[HD:PG, j, :], t2[HD:PG, 0, :], kch[HD:PG, 0, :].bitcast(F32), ALU.subtract)\
                   .then_inc(kr_ready, 1)

            def heads_c(e, i):
                dve_tiles(e, c, tiles_c())
                dve_attention(e, c, its_c(i))
            turns(dve, c, C_HEADS // MH, heads_c)
            dve_features(dve, c, o3h, o3l, KT, 4)
            dve_linear_y(dve, c, SEQ, y3)
            dve_postnorm(dve, c, SEQ, y3, [(0, SEQ, G2(0, 2))])
            dve_prenorm(dve, c, segs_2(3)[:1])
            dve_ffn(dve, c, SEQ, y1, act1h, act1l, False)
            dve_postnorm(dve, c, SEQ, y1, [(0, SEQ, G2(0, 5))])
            for r in range(4):
                dve.wait_ge(lt_done, c.next(lt_done))
                dve.tensor_copy(outb[:, r, :], acc[r % 2][:, :, :].rearrange("p b n -> p (b n)")).then_inc(lt_out, 1)


def constants():
    def swap(lo, hi, block, half):
        m = np.zeros((P, P), np.float32)
        for p in range(lo, hi):
            q = (p - lo) % block
            if q < half:
                m[p + half, p] = -1.0
            elif q < 2 * half:
                m[p - half, p] = 1.0
        return m

    out = {"ident": np.eye(P, dtype=np.float32), "ones": np.full((P, P), 1.0 / D, np.float32)}
    inv = np.zeros((P, 1), np.float32)
    f = (np.float32(500000.0) ** (-np.arange(0, 16, 2, dtype=np.float32) / np.float32(16))).astype(np.float32)
    for p in range(P):
        if p % HD < 16:
            inv[p] = f[p % HD % 8]
    out["inv1"], out["perm1"] = inv, swap(0, P, HD, 8)
    t = np.arange(SEQ)

    def axial(rows, dim, lo):
        ax = dim // 2
        f = (np.float32(10000.0) ** (-np.arange(0, ax, 2, dtype=np.float32) / np.float32(ax))).astype(np.float32)
        cos, sin = np.ones((P, SEQ), np.float32), np.zeros((P, SEQ), np.float32)
        for p in range(lo, rows):
            q = (p - lo) % dim
            where = (t // 64 if q < ax else t % 64).astype(np.float32)
            a = (where * f[q % (ax // 2)]).astype(np.float64)
            cos[p], sin[p] = np.cos(a), np.sin(a)
        return cos, sin

    out["cos_ab"], out["sin_ab"] = axial(P, HD, 0)
    out["cos_c"], out["sin_c"] = axial(PG, C_ROPE, HD)
    out["perm_ab"], out["perm_c"] = swap(0, P, 32, 16), swap(HD, PG, 16, 8)
    edge = np.ones((P, 5, PAD), np.float32)
    for g, w in enumerate(POOL_W):
        edge[:, g, :] = 1.0 / np.minimum(np.arange(PAD) + 1, w)
    out["edge"] = edge
    i = np.arange(P)
    m1 = np.full((P, RES, TC), MASKED, np.float32)
    m2 = np.zeros((P, 4, TC), np.float32)
    for r in range(RES):
        q = RES * i[:, None] + r
        for r2 in range(RES):
            k = RES * i[None, :] + r2
            m1[:, r, r2 * P:r2 * P + P][(q - k >= 0) & (q - k <= 128)] = 0.0
        m1[:, r, 512:640][i[:, None] >= i[None, :]] = 0.0
        m1[:, r, 640:768][(i[:, None] >= i[None, :]) & ((i[:, None] - i[None, :]) % 4 == 0)] = 0.0
        q = P * r + i[:, None]
        m2[:, r, 0:SEQ][np.abs(q - t[None, :]) > 128] = MASKED
    half = mybir.dt.np(BF16)
    out["mask1"], out["mask2"] = m1.astype(half), m2.astype(half)
    return out


def kernel(**inputs):
    import concourse.bacc as _bacc
    from concourse.bass_utils import run_bass_kernel_spmd as _run

    nc = _bacc.Bacc("TRN2", target_bir_lowering=False, num_devices=1)
    arrays, A = {}, {}
    for name, a in {**inputs, **constants()}.items():
        a = np.ascontiguousarray(a)
        arrays[f"in_{name}"] = a
        A[name] = nc.dram_tensor(f"in_{name}", a.shape, mybir.dt.from_np(a.dtype), kind="ExternalInput").ap()
    out = nc.dram_tensor("out", (1, SEQ, D), F32, kind="ExternalOutput").ap()
    two_blocks(nc, A, out)
    return _run(nc, [arrays], core_ids=[0]).results[0]["out"]
```
